# Optimizing a Trainium2 kernel written in Bass

```python
import jax, jax.numpy as jnp
from jax import lax
import numpy as np
import math

D_MODEL = 1024
BATCH = 1
SEQ = 1024
DEPTH = 1

N_ATTN_HEADS = 8
HEAD_DIM = 64
ATTN_WIDTH = N_ATTN_HEADS * HEAD_DIM
CONV_GROUPS = 8
CONV_WIDTH = 512
CONV_K = 3
D_FF = 4 * D_MODEL
PLE_DIM = 256
Q_BLOCK = 128
EPS = 1e-6
SPLIT_SIZES = (ATTN_WIDTH, ATTN_WIDTH, ATTN_WIDTH, CONV_WIDTH, CONV_WIDTH, CONV_WIDTH, D_MODEL, D_MODEL)
SPLIT_POINTS = tuple(int(v) for v in np.cumsum(SPLIT_SIZES)[:-1])
D_IN = sum(SPLIT_SIZES)


def rms_norm(x, g):
    xf = x.astype(jnp.float32)
    var = jnp.mean(xf * xf, axis=-1, keepdims=True)
    return (xf * lax.rsqrt(var + EPS) * g.astype(jnp.float32)).astype(x.dtype)

def stick_breaking_attention(q, k, v):
    b, h, s, dh = q.shape
    nblk = s // Q_BLOCK
    scale = dh ** -0.5
    kf = k.astype(jnp.float32)
    vf = v.astype(jnp.float32)
    q_blocks = q.reshape(b, h, nblk, Q_BLOCK, dh).transpose(2, 0, 1, 3, 4)
    key_pos = jnp.arange(s, dtype=jnp.int32)
    starts = jnp.arange(nblk, dtype=jnp.int32) * Q_BLOCK

    def block(args):
        qb, start = args
        z = jnp.einsum('bhqd,bhkd->bhqk', qb.astype(jnp.float32), kf) * scale
        q_pos = start + jnp.arange(Q_BLOCK, dtype=jnp.int32)
        causal = key_pos[None, :] < q_pos[:, None]
        log_beta = jax.nn.log_sigmoid(z)
        log_keep = jnp.where(causal, log_beta - z, 0.0)
        between = lax.cumsum(log_keep, axis=3, reverse=True) - log_keep
        w = jnp.where(causal, jnp.exp(log_beta + between), 0.0)
        return jnp.einsum('bhqk,bhkd->bhqd', w, vf)

    out = lax.map(block, (q_blocks, starts))
    return out.transpose(1, 2, 0, 3, 4).reshape(b, h, s, dh).astype(q.dtype)

def causal_depthwise_conv(u, w):
    c = u.shape[-1]
    return lax.conv_general_dilated(
        u, w[:, None, :].astype(u.dtype), window_strides=(1,),
        padding=((CONV_K - 1, 0),), dimension_numbers=('NWC', 'WIO', 'NWC'),
        feature_group_count=c)

def first_inputs(seed: int = 0) -> dict:
    key = jax.random.key(seed)
    ks = jax.random.split(key, 20)
    f32 = jnp.float32

    def nrm(k, shape, fan_in):
        return jax.random.normal(k, shape, f32) * (fan_in ** -0.5)

    def gain(k, shape):
        return jnp.ones(shape, f32) + 0.05 * jax.random.normal(k, shape, f32)

    return {
        'x': jax.random.normal(ks[0], (BATCH, SEQ, D_MODEL), f32),
        'p': jax.random.normal(ks[1], (DEPTH, BATCH, SEQ, PLE_DIM), f32),
        'g_pre_mix': gain(ks[2], (DEPTH, D_MODEL)),
        'w_in': nrm(ks[3], (DEPTH, D_MODEL, D_IN), D_MODEL),
        'b_gate': 0.1 * jax.random.normal(ks[4], (DEPTH, 2 * D_MODEL), f32),
        'w_conv': nrm(ks[5], (DEPTH, CONV_K, CONV_WIDTH), CONV_K),
        'w_attn_out': nrm(ks[6], (DEPTH, ATTN_WIDTH, D_MODEL), ATTN_WIDTH),
        'w_conv_out': nrm(ks[7], (DEPTH, CONV_WIDTH, D_MODEL), CONV_WIDTH),
        'w_o': nrm(ks[8], (DEPTH, D_MODEL, D_MODEL), D_MODEL),
        'g_post_mix': gain(ks[9], (DEPTH, D_MODEL)),
        'g_pre_mlp': gain(ks[10], (DEPTH, D_MODEL)),
        'w_up': nrm(ks[11], (DEPTH, D_MODEL, D_FF), D_MODEL),
        'w_down': nrm(ks[12], (DEPTH, D_FF, D_MODEL), D_FF),
        'g_post_mlp': gain(ks[13], (DEPTH, D_MODEL)),
        'g_ple': gain(ks[14], (DEPTH, D_MODEL)),
        'w_ple_gate': nrm(ks[15], (DEPTH, D_MODEL, D_MODEL), D_MODEL),
        'w_ple_proj': nrm(ks[16], (DEPTH, PLE_DIM, D_MODEL), PLE_DIM),
    }

def first_block(x, p, g_pre_mix, w_in, b_gate, w_conv, w_attn_out, w_conv_out, w_o,
              g_post_mix, g_pre_mlp, w_up, w_down, g_post_mlp, g_ple, w_ple_gate, w_ple_proj):
    bsz, seq, _ = x.shape
    for i in range(DEPTH):
        h = rms_norm(x, g_pre_mix[i])
        proj = h @ w_in[i]
        q, k, v, cb, cc, cu, ga, gc = jnp.split(proj, SPLIT_POINTS, axis=-1)

        def heads(t):
            return t.reshape(bsz, seq, N_ATTN_HEADS, HEAD_DIM).transpose(0, 2, 1, 3)

        o = stick_breaking_attention(heads(q), heads(k), heads(v))
        o = o.transpose(0, 2, 1, 3).reshape(bsz, seq, ATTN_WIDTH)
        y_attn = o @ w_attn_out[i]

        y_conv = (cb * causal_depthwise_conv(cc * cu, w_conv[i])) @ w_conv_out[i]

        gates = jax.nn.sigmoid(jnp.concatenate([ga, gc], axis=-1) + b_gate[i])
        gate_attn, gate_conv = jnp.split(gates, 2, axis=-1)
        mixed = (gate_attn * y_attn + gate_conv * y_conv) @ w_o[i]
        x = x + rms_norm(mixed, g_post_mix[i])

        h = rms_norm(x, g_pre_mlp[i])
        f = jnp.square(jax.nn.relu(h @ w_up[i])) @ w_down[i]
        x = x + rms_norm(f, g_post_mlp[i])

        ple_gate = jax.nn.sigmoid(rms_norm(x, g_ple[i]) @ w_ple_gate[i])
        x = x + ple_gate * (p[i] @ w_ple_proj[i])
    return x


DEPTH_2 = 2

N_MEM = 256
BLOCK_Q = 128
MIX_WIDTH = D_MODEL
MEM_WIDTH = D_MODEL // 4
MAIN_WIDTH = MIX_WIDTH - MEM_WIDTH
MEM_HEADS = 4
MEM_DIM = MEM_WIDTH // MEM_HEADS
MLA_V = 64
MLA_HEADS = MAIN_WIDTH // MLA_V
MLA_NOPE = 64
MLA_ROPE = 32
MLA_QK = MLA_NOPE + MLA_ROPE
Q_LORA = 384
KV_LORA = 256
ROPE_THETA = 10000.0
MAX_POS_OFFSET = 4096
FOX_DIM = 64
FOX_HEADS = MAIN_WIDTH // FOX_DIM
N_A = (DEPTH_2 + 1) // 2
N_B = DEPTH_2 // 2
A_IN = Q_LORA + KV_LORA + MLA_ROPE + MEM_WIDTH + MIX_WIDTH
B_IN = 3 * MAIN_WIDTH + FOX_HEADS + MEM_WIDTH + MIX_WIDTH


def rms_norm_2(x, g):
    xf = x.astype(jnp.float32)
    y = xf * lax.rsqrt(jnp.mean(xf * xf, axis=-1, keepdims=True) + EPS)
    return (y * g.astype(jnp.float32)).astype(x.dtype)

def split_cols(a, sizes):
    idx = np.cumsum(sizes)[:-1].tolist()
    return jnp.split(a, idx, axis=-1)

def rope(x, pos):
    half = x.shape[-1] // 2
    inv = ROPE_THETA ** (-jnp.arange(half, dtype=jnp.float32) / half)
    ang = pos.astype(jnp.float32)[..., None] * inv
    if x.ndim == 4:
        ang = ang[:, :, None, :]
    cos, sin = jnp.cos(ang), jnp.sin(ang)
    x1 = x[..., :half].astype(jnp.float32)
    x2 = x[..., half:].astype(jnp.float32)
    return jnp.concatenate([x1 * cos - x2 * sin, x2 * cos + x1 * sin], axis=-1).astype(x.dtype)

def causal_block_attention(q, k, v, scale, log_f_cum=None):
    B, S, H, Dk = q.shape
    nb = S // BLOCK_Q
    qb = q.reshape(B, nb, BLOCK_Q, H, Dk).swapaxes(0, 1)
    blk = jnp.arange(nb)
    key_pos = jnp.arange(S)
    if log_f_cum is not None:
        f_t = log_f_cum.transpose(0, 2, 1)
        fb = jnp.moveaxis(f_t.reshape(B, H, nb, BLOCK_Q), 2, 0)
        xs = (blk, qb, fb)
    else:
        xs = (blk, qb)

    def one_block(args):
        i, q_i = args[0], args[1]
        s = jnp.einsum('bqhd,bkhd->bhqk', q_i, k,
                       preferred_element_type=jnp.float32) * scale
        if log_f_cum is not None:
            s = s + (args[2][..., None].astype(jnp.float32) - f_t[:, :, None, :].astype(jnp.float32))
        q_pos = i * BLOCK_Q + jnp.arange(BLOCK_Q)
        mask = key_pos[None, :] <= q_pos[:, None]
        s = jnp.where(mask, s, -jnp.inf)
        p = jax.nn.softmax(s, axis=-1)
        return jnp.einsum('bhqk,bkhd->bqhd', p.astype(v.dtype), v)

    out = lax.map(one_block, xs)
    return out.swapaxes(0, 1).reshape(B, S, H, v.shape[-1])

def memory_attention(q, k, v):
    s = jnp.einsum('bshd,bmhd->bhsm', q, k,
                   preferred_element_type=jnp.float32) * (MEM_DIM ** -0.5)
    p = jax.nn.softmax(s, axis=-1)
    return jnp.einsum('bhsm,bmhd->bshd', p.astype(v.dtype), v)

def mla_mixer(c_q, c_kv, k_r, pos, q_norm, kv_norm, w_q_up, w_kv_up):
    B, S, _ = c_q.shape
    q = (rms_norm_2(c_q, q_norm) @ w_q_up).reshape(B, S, MLA_HEADS, MLA_QK)
    q_nope, q_rope = q[..., :MLA_NOPE], rope(q[..., MLA_NOPE:], pos)
    kv = (rms_norm_2(c_kv, kv_norm) @ w_kv_up).reshape(B, S, MLA_HEADS, MLA_NOPE + MLA_V)
    k_nope, v = kv[..., :MLA_NOPE], kv[..., MLA_NOPE:]
    k_rope = jnp.broadcast_to(rope(k_r, pos)[:, :, None, :], (B, S, MLA_HEADS, MLA_ROPE))
    qf = jnp.concatenate([q_nope, q_rope], axis=-1)
    kf = jnp.concatenate([k_nope, k_rope], axis=-1)
    out = causal_block_attention(qf, kf, v, MLA_QK ** -0.5)
    return out.reshape(B, S, MAIN_WIDTH)

def fox_mixer(q, k, v, f_logit, b_f):
    B, S, _ = q.shape
    log_f = jax.nn.log_sigmoid(f_logit.astype(jnp.float32) + b_f.astype(jnp.float32))
    log_f_cum = jnp.cumsum(log_f, axis=1)
    qh = q.reshape(B, S, FOX_HEADS, FOX_DIM)
    kh = k.reshape(B, S, FOX_HEADS, FOX_DIM)
    vh = v.reshape(B, S, FOX_HEADS, FOX_DIM)
    out = causal_block_attention(qh, kh, vh, FOX_DIM ** -0.5, log_f_cum)
    return out.reshape(B, S, MAIN_WIDTH)

def second_inputs(seed: int = 0) -> dict:
    key = jax.random.key(seed)
    ks = jax.random.split(key, 16)
    f32 = jnp.float32

    def nrm(k, shape, fan_in):
        return jax.random.normal(k, shape, f32) * (fan_in ** -0.5)

    def gain(k, shape):
        return 1.0 + 0.01 * jax.random.normal(k, shape, f32)

    x = jax.random.normal(ks[0], (BATCH, SEQ, D_MODEL), f32)
    mem = jax.random.normal(ks[1], (BATCH, N_MEM, D_MODEL), f32)
    positions = (jax.random.randint(ks[2], (BATCH, 1), 0, MAX_POS_OFFSET, dtype=jnp.int32)
                 + jnp.arange(SEQ, dtype=jnp.int32)[None, :])
    return {
        "x": x,
        "mem": mem,
        "positions": positions,
        "norm_pre": gain(ks[3], (DEPTH_2, D_MODEL)),
        "norm_post": gain(ks[4], (DEPTH_2, D_MODEL)),
        "mem_norm": gain(ks[5], (D_MODEL,)),
        "w_mem_kv": nrm(ks[6], (DEPTH_2, D_MODEL, 2 * MEM_WIDTH), D_MODEL),
        "w_out": nrm(ks[7], (DEPTH_2, MIX_WIDTH, D_MODEL), MIX_WIDTH),
        "w_in_a": nrm(ks[8], (N_A, D_MODEL, A_IN), D_MODEL),
        "q_norm_a": gain(ks[9], (N_A, Q_LORA)),
        "kv_norm_a": gain(ks[10], (N_A, KV_LORA)),
        "w_q_up_a": nrm(ks[11], (N_A, Q_LORA, MLA_HEADS * MLA_QK), Q_LORA),
        "w_kv_up_a": nrm(ks[12], (N_A, KV_LORA, MLA_HEADS * (MLA_NOPE + MLA_V)), KV_LORA),
        "w_in_b": nrm(ks[13], (N_B, D_MODEL, B_IN), D_MODEL),
        "b_f": jax.random.uniform(ks[14], (N_B, FOX_HEADS), f32, 1.0, 4.0),
    }

def second_block(x, mem, positions, norm_pre, norm_post, mem_norm, w_mem_kv, w_out,
              w_in_a, q_norm_a, kv_norm_a, w_q_up_a, w_kv_up_a, w_in_b, b_f):
    B, S, _ = x.shape
    M = mem.shape[1]
    mem_n = rms_norm_2(mem, mem_norm)
    h = x
    for i in range(DEPTH_2):
        j = i // 2
        hn = rms_norm_2(h, norm_pre[i])
        mkv = (mem_n @ w_mem_kv[i]).reshape(M, 2, MEM_HEADS, MEM_DIM) if False else \
            (mem_n @ w_mem_kv[i]).reshape(B, M, 2, MEM_HEADS, MEM_DIM)
        k_m, v_m = mkv[:, :, 0], mkv[:, :, 1]
        if i % 2 == 0:
            proj = hn @ w_in_a[j]
            c_q, c_kv, k_r, q_m, gate = split_cols(
                proj, [Q_LORA, KV_LORA, MLA_ROPE, MEM_WIDTH, MIX_WIDTH])
            main = mla_mixer(c_q, c_kv, k_r, positions, q_norm_a[j], kv_norm_a[j],
                             w_q_up_a[j], w_kv_up_a[j])
        else:
            proj = hn @ w_in_b[j]
            q, k, v, f_logit, q_m, gate = split_cols(
                proj, [MAIN_WIDTH, MAIN_WIDTH, MAIN_WIDTH, FOX_HEADS, MEM_WIDTH, MIX_WIDTH])
            main = fox_mixer(q, k, v, f_logit, b_f[j])
        mem_out = memory_attention(q_m.reshape(B, S, MEM_HEADS, MEM_DIM), k_m, v_m)
        y = jnp.concatenate([main, mem_out.reshape(B, S, MEM_WIDTH)], axis=-1) * jax.nn.silu(gate)
        h = h + rms_norm_2(y @ w_out[i], norm_post[i])
    return h


def setup_inputs(seed=0):
    out = dict(first_inputs(seed))
    for name, value in second_inputs(seed + 1).items():
        if name != "x":
            out[name + "_2"] = value
    return out


def reference(
    x, p, g_pre_mix, w_in, b_gate, w_conv, w_attn_out, w_conv_out, w_o, g_post_mix, g_pre_mlp,
    w_up, w_down, g_post_mlp, g_ple, w_ple_gate, w_ple_proj, mem_2, positions_2, norm_pre_2,
    norm_post_2, mem_norm_2, w_mem_kv_2, w_out_2, w_in_a_2, q_norm_a_2, kv_norm_a_2, w_q_up_a_2,
    w_kv_up_a_2, w_in_b_2, b_f_2,
):
    x = first_block(
        x, p, g_pre_mix, w_in, b_gate, w_conv, w_attn_out, w_conv_out, w_o, g_post_mix,
        g_pre_mlp, w_up, w_down, g_post_mlp, g_ple, w_ple_gate, w_ple_proj,
    )
    return second_block(
        x, mem_2, positions_2, norm_pre_2, norm_post_2, mem_norm_2, w_mem_kv_2, w_out_2,
        w_in_a_2, q_norm_a_2, kv_norm_a_2, w_q_up_a_2, w_kv_up_a_2, w_in_b_2, b_f_2,
    )


_drawn_inputs = setup_inputs


def setup_inputs(seed=0):
    import zlib

    import numpy as np

    out = dict(_drawn_inputs(seed))
    spreads = {}
    factors = {'g_ple': 8.0,
     'norm_pre_2': 5.145,
     'norm_post_2': 7.744,
     'mem_norm_2': 8.0,
     'q_norm_a_2': 8.0,
     'kv_norm_a_2': 8.0}
    for name, (base, spread) in spreads.items():
        noise = np.random.default_rng([zlib.crc32(name.encode()), seed]).standard_normal(out[name].shape)
        drawn = base * np.exp(spread * noise) if base else spread * noise
        out[name] = __import__('jax').numpy.asarray(drawn.astype(out[name].dtype))
    for name, factor in factors.items():
        out[name] = (out[name] * factor).astype(out[name].dtype)
    return out
```

```python
from contextlib import ExitStack

import numpy as np

import concourse.bass as bass
from concourse import mybir

F32 = mybir.dt.float32
F32R = mybir.dt.float32r
I32 = mybir.dt.int32
ALU = mybir.AluOpType
ACT = mybir.ActivationFunctionType
AX = mybir.AxisListType

P = 128
S = 1024
D = 1024
KT = D // P
HALF = 512
N_MEM = 256
EPS = 1e-6
SB_PAIRS = 4
CONV_TILES = 4
FF = 4 * D
FF_CHUNK = 256
MLA_HEADS = 12
FOX_PAIRS = 6
MAIN_TILES = 6
SCALE_64 = 64.0 ** -0.5
SCALE_MLA = 96.0 ** -0.5
NEG = -float(2.0 ** 100)
UNIT = 4096
UNITS = 27

C_ID, C_ONE, C_TRI, C_REST = 0, 128, 256, 384
C_MASK01, C_CAP, C_NEG = 512, 768, 1024
C_HEAD = 1536
C_INV, C_OFF, C_SIGN, C_SHIFT = 1548, 1549, 1550, 1551
C_EPS = 1552
N_CONST = 1554

V_PRE, V_POST, V_MLP, V_POSTMLP, V_PLE = 0, 8, 16, 24, 32
V_PRE2, V_POST2, V_MEM = 40, 56, 72
V_QN, V_KVN = 80, 83
V_BGA, V_BGC = 85, 93
V_CONV = 101
V_BF = 113
N_VEC = 114

N_SLABS = {"sb": 3 * SB_PAIRS, "conv": 3 * CONV_TILES, "mix": 3 * KT, "wo": KT,
           "mlp": 4 * (FF // FF_CHUNK), "ple": 2 + KT, "mem": 8,
           "a_in": 2 + 3 + 2 + 1, "mla": MLA_HEADS, "a_gate": KT, "a_out": KT,
           "b_in": 3, "fox": 3 * FOX_PAIRS, "b_gate": KT, "b_out": KT}
TOTAL_SLABS = sum(N_SLABS.values())


class Tally:

    def __init__(self):
        self.counts = {}

    def now(self, what):
        return self.counts.get(what if isinstance(what, str) else id(what), 0)

    def take(self, what, k=1):
        before = self.now(what)
        self.counts[what if isinstance(what, str) else id(what)] = before + k
        return before

    def next(self, what, k=1):
        return self.take(what, k) + k


def program(nc, wall, vecs, consts, xt, pt, memt, pos, spill_x, spill_out, out):
    ctx = ExitStack()

    def sb(name, shape, dt):
        return ctx.enter_context(nc.sbuf_tensor(name, shape, dt))

    def sem(name):
        return ctx.enter_context(nc.semaphore(name))

    con = sb("con", [P, N_CONST], F32)
    vec = sb("vec", [P, N_VEC], F32)
    tri_r = sb("tri_r", [P, P], F32R)
    rest_r = sb("rest_r", [P, P], F32R)
    id_r = sb("id_r", [P, P], F32R)
    neg_r = sb("neg_r", [P, 2, 256], F32R)
    zero_r = sb("zero_r", [P, P], F32R)
    neg_flat = neg_r[:, :, :].rearrange("p a b -> p (a b)")
    raw = sb("raw", [P, 2, KT, P], F32)
    wh = sb("wh", [P, 2, KT, P], F32R)
    wl = sb("wl", [P, 2, KT, P], F32R)
    with nc.sbuf_tensor("xold_t", [P, KT, S], F32) as xold_t, nc.sbuf_tensor("z_t", [P, KT, S], F32) as z_t:
        pass
    hh = sb("hh", [P, KT, S], F32R)
    hl = sb("hl", [P, KT, S], F32R)
    small = sb("small", [P, 64], F32)
    rt, rs = small[:, 0:8], small[:, 8:16]
    mx, nm, rsum, rinv = (small[:, a:a + 4] for a in (16, 20, 24, 28))
    region = nc.sbuf_base

    def at(unit, name, shape, dt, extra=0):
        with ExitStack() as s:
            if unit or extra:
                s.enter_context(nc.sbuf_tensor(name + "_below", [P, unit * UNIT // 4 + extra // 4], F32))
            t = s.enter_context(nc.sbuf_tensor(name, shape, dt))
        return t

    assert region + UNITS * UNIT <= nc.sbuf_usable_end, (region, nc.sbuf_usable_end)
    ident, ones = con[:, C_ID:C_ID + P], con[:, C_ONE:C_ONE + P]

    x_t = at(0, "x_t", [P, KT, S], F32)
    y_t = at(8, "y_t", [P, KT, S], F32)
    sq = [at(22 + i, f"sq{i}", [P, S], F32) for i in range(2)]
    nt = [at(24 + i, f"nt{i}", [P, S], F32) for i in range(2)]
    acc = at(26, "acc", [P, S], F32)
    o_h, o_l = at(0, "o_h", [P, 4, S], F32R), at(4, "o_l", [P, 4, S], F32R)
    qp_h, qp_l = at(8, "qp_h", [P, 2, S], F32R), at(10, "qp_l", [P, 2, S], F32R)
    k_h, k_l = at(12, "k_h", [P, S], F32R), at(13, "k_l", [P, S], F32R)
    vp_h, vp_l = at(14, "vp_h", [P, 2, 8, P], F32R), at(16, "vp_l", [P, 2, 8, P], F32R)
    zb = [at(18 + i, f"zb{i}", [P, 2, HALF], F32) for i in range(2)]
    eb = at(20, "eb", [P, 2, HALF], F32)
    vt = at(20, "vt", [P, S], F32)
    sp_h = [at(21 + i, f"sp_h{i}", [P, 2, HALF], F32R) for i in range(2)]
    sp_l = [at(23 + i, f"sp_l{i}", [P, 2, HALF], F32R) for i in range(2)]
    pw_h, pw_l = at(25, "pw_h", [P, 2, HALF], F32R), at(26, "pw_l", [P, 2, HALF], F32R)
    c_h, c_l = at(8, "c_h", [P, 4, S], F32R), at(12, "c_l", [P, 4, S], F32R)
    cc = at(16, "cc", [P, S], F32)
    cu = at(17, "cu", [P, 2 + S], F32)
    cv = at(19, "cv", [P, S], F32)
    mix_t = at(16, "mix_t", [P, KT, S], F32)
    ga, gc = at(24, "ga", [P, S], F32), at(25, "gc", [P, S], F32)
    f_h = [at(16 + 2 * i, f"f_h{i}", [P, 2, S], F32R) for i in range(2)]
    f_l = [at(20 + 2 * i, f"f_l{i}", [P, 2, S], F32R) for i in range(2)]
    fr, ff = at(24, "fr", [P, S], F32), at(25, "ff", [P, S], F32)
    p_t = at(16, "p_t", [P, 2, S], F32)
    p_h, p_l = at(18, "p_h", [P, 2, S], F32R), at(20, "p_l", [P, 2, S], F32R)
    pg = at(22, "pg", [P, S], F32)
    m_t = at(8, "m_t", [P, KT, N_MEM], F32)
    m_h, m_l = at(10, "m_h", [P, KT, N_MEM], F32R), at(12, "m_l", [P, KT, N_MEM], F32R)
    mv = at(14, "mv", [P, N_MEM], F32)
    km_h = [at(18 + 2 * i, f"km_h{i}", [P, 2, N_MEM], F32R) for i in range(2)]
    km_l = [at(18 + 2 * i, f"km_l{i}", [P, 2, N_MEM], F32R, 2048) for i in range(2)]
    vm_h = [at(19 + 2 * i, f"vm_h{i}", [P, 2, 2 * P], F32R) for i in range(2)]
    vm_l = [at(19 + 2 * i, f"vm_l{i}", [P, 2, 2 * P], F32R, 2048) for i in range(2)]
    prob = [[at(16, "prob00", [P, S], F32), at(17, "prob01", [P, S], F32)],
            [at(22, "prob10", [P, S], F32), at(23, "prob11", [P, S], F32)]]
    pt_h = [at(24 + i, f"pt_h{i}", [P, HALF], F32R) for i in range(2)]
    pt_l = [at(24 + i, f"pt_l{i}", [P, HALF], F32R, 2048) for i in range(2)]
    ot = at(26, "ot", [P, S], F32)
    cq_h, cq_l = at(0, "cq_h", [P, 3, S], F32R), at(3, "cq_l", [P, 3, S], F32R)
    ckv_h, ckv_l = at(6, "ckv_h", [P, 2, S], F32R), at(13, "ckv_l", [P, 2, S], F32R)
    cq_t, ckv_t = at(8, "cq_t", [P, 3, S], F32), at(11, "ckv_t", [P, 2, S], F32)
    qa_h, qa_l = at(8, "qa_h", [P, S], F32R), at(9, "qa_l", [P, S], F32R)
    ka_h, ka_l = at(10, "ka_h", [P, S], F32R), at(11, "ka_l", [P, S], F32R)
    kvf = at(12, "kvf", [P, S], F32)
    va_h, va_l = at(15, "va_h", [P, 8, 64], F32R), at(15, "va_l", [P, 8, 64], F32R, 2048)
    trig = at(18, "trig", [P, S], F32)
    qf = at(19, "qf", [P, S], F32)
    ang = [at(22 + i, f"ang{i}", [P, S], F32) for i in range(3)]
    posi = at(25, "posi", [P, S], I32)
    vf_h, vf_l = at(14, "vf_h", [P, 8, P], F32R), at(15, "vf_l", [P, 8, P], F32R)
    fvt = at(0, "fvt", [P, S], F32)
    a_base, a_head, b_all = at(1, "a_base", [P, S], F32), at(2, "a_head", [P, S], F32R), at(3, "b_all", [P, S], F32R)
    fx, fe, fone = at(4, "fx", [P, S], F32), at(5, "fe", [P, S], F32), at(6, "fone", [P, S], F32)
    y_h, y_l = at(0, "y_h", [P, KT, S], F32R), at(8, "y_l", [P, KT, S], F32R)
    gt = [at(16 + i, f"gt{i}", [P, S], F32) for i in range(2)]
    go = [at(22 + i, f"go{i}", [P, S], F32) for i in range(4)]
    ps = ctx.enter_context(nc.psum_tensor("ps", [P, 2, S], F32))
    aux = ctx.enter_context(nc.psum_tensor("aux", [P, 2, HALF], F32))
    ob = ctx.enter_context(nc.psum_tensor("ob", [P, 2, HALF], F32))

    init_in, x_in, p_in, m_in, pos_in, xold_in = map(sem, ("init_in", "x_in", "p_in", "m_in", "pos_in", "xold_in"))
    raw_in, out_in = [sem(f"raw_in{i}") for i in range(2)], [sem(f"out_in{i}") for i in range(4)]
    ot_out, spill_done, end_out = map(sem, ("ot_out", "spill_done", "end_out"))
    w_high, w_split, slab_begun, work_done = map(sem, ("w_high", "w_split", "slab_begun", "work_done"))
    work_free = [sem(f"work_free{i}") for i in range(2)]
    act_end, dve_end, act_chain, dve_chain = map(sem, ("act_end", "dve_end", "act_chain", "dve_chain"))
    const_ready = sem("const_ready")
    high_ready, tile_ready, tile_split = map(sem, ("high_ready", "tile_ready", "tile_split"))
    sq_ready, sq_used, rt_ready, diag_ready = map(sem, ("sq_ready", "sq_used", "rt_ready", "diag_ready"))
    nt_ready, nh_ready, norm_ready = map(sem, ("nt_ready", "nh_ready", "norm_ready"))
    upd_ready, final_ready = map(sem, ("upd_ready", "final_ready"))
    ln_ready, sp_ready, sph_ready, spl_ready = map(sem, ("ln_ready", "sp_ready", "sph_ready", "spl_ready"))
    tri_done, d_ready, pwh_ready, pwl_ready = map(sem, ("tri_done", "d_ready", "pwh_ready", "pwl_ready"))
    av_done, oh_ready, o_ready = map(sem, ("av_done", "oh_ready", "o_ready"))
    nm_ready, p_ready, pn_ready, pt_done = map(sem, ("nm_ready", "p_ready", "pn_ready", "pt_done"))
    pth_ready, ptl_ready, oa_done, oa_taken = map(sem, ("pth_ready", "ptl_ready", "oa_done", "oa_taken"))
    table_ready, sin_ready, qn_ready, rope_ready = map(sem, ("table_ready", "sin_ready", "qn_ready", "rope_ready"))
    ahead_ready = sem("ahead_ready")
    block = ctx.enter_context(nc.Block())

    def barrier(eng, t, me):
        eng.drain().then_inc(me, 1)
        n = t.next("end")
        eng.wait_ge(act_end, n)
        eng.wait_ge(dve_end, n)

    SB_UNITS = []
    for chunk in range(2):
        for kb in range(4 * chunk + 3, -1, -1):
            first = min(max(kb * P - chunk * HALF, 0), HALF - 256)
            SB_UNITS.append((chunk, kb, first, HALF - first))
    NU = len(SB_UNITS)
    def widths(keys):
        return [(0, min(keys, HALF))] + ([(HALF, keys)] if keys > HALF else [])

    @block.sync
    def _(sp):
        sp.dma_start(con[:], consts).then_inc(init_in, 16)
        sp.dma_start(vec[:], vecs).then_inc(init_in, 16)
        for k in range(KT):
            sp.dma_start(x_t[:, k, :], xt[k * P:(k + 1) * P, :]).then_inc(x_in, 16)
        for s in range(2):
            sp.dma_start(raw[:, s, :, :], wall[s]).then_inc(raw_in[s], 16)

        with sp.Fori(1, TOTAL_SLABS // 2) as i:
            for s in range(2):
                sp.wait_ge(w_split, 2 * i + s - 1)
                sp.dma_start(raw[:, s, :, :], wall[bass.ds(2 * i + s, 1)].rearrange("a p k m -> (a p) k m")).then_inc(raw_in[s], 16)

        if TOTAL_SLABS % 2:
            sp.wait_ge(w_split, TOTAL_SLABS - 2)
            sp.dma_start(raw[:, 0, :, :], wall[TOTAL_SLABS - 1]).then_inc(raw_in[0], 16)
        for k in range(KT):
            sp.wait_ge(final_ready, k + 1)
            sp.dma_start(out[k * P:(k + 1) * P, :], x_t[:, k, :]).then_inc(end_out, 16)
        sp.wait_ge(end_out, 16 * KT)

    @block.gpsimd
    def _(pool):
        def split(s, slab_words):
            loaded, begun, high = slab_words
            pool.wait_ge(raw_in[s], loaded)
            if begun is not None:
                pool.wait_ge(slab_begun, begun)
            pool.tensor_tensor(wh[:, s, :, :], raw[:, s, :, :], ones.unsqueeze(1).broadcast_to([P, KT, P]), ALU.mult).then_inc(w_high, 1)
            pool.wait_ge(w_high, high)
            pool.tensor_tensor(wl[:, s, :, :], raw[:, s, :, :], wh[:, s, :, :].bitcast(F32), ALU.subtract).then_inc(w_split, 1)

        for s in range(2):
            split(s, (16, None, s + 1))
        with pool.Fori(1, TOTAL_SLABS // 2) as i:
            for s in range(2):
                split(s, (16 * i + 16, 2 * i + s, 2 * i + s + 1))
        if TOTAL_SLABS % 2:
            last = TOTAL_SLABS - 1
            split(0, (8 * last + 16, last, last + 1))

    @block.tensor
    def _(pe):
        t = Tally()

        def work():
            w = t.take("work")
            if w >= 2:
                pe.wait_ge(work_free[w % 2], w // 2)
            return w, w % 2

        def evacuated(w):
            pe.wait_ge(work_free[w % 2], w // 2 + 1)

        def slab():
            s = t.take("slab")
            pe.wait_ge(w_split, s + 1)
            t.fresh = True
            return s % 2

        def proj(w, sl, ks, rh, rl, n=S, ready=None):
            halves = [(a, min(a + HALF, n)) for a in range(0, n, HALF)]
            for i, k in enumerate(ks):
                if ready:
                    ready(i)
                for j, (lw, r) in enumerate(((wh, rh), (wh, rl), (wl, rh))):
                    for a, b in halves:
                        m = pe.matmul(ps[:, w, a:b], lw[:, sl, k, :], r[:, i, a:b],
                                      start=(i == 0 and j == 0), stop=(i == len(ks) - 1 and j == 2))
                        if t.fresh:
                            m.then_inc(slab_begun, 1)
                            t.fresh = False
            m.then_inc(work_done, 1)

        def product(ks, rh, rl, n=S, ready=None, sl=None):
            sl = slab() if sl is None else sl
            w, slot = work()
            proj(slot, sl, ks, rh, rl, n, ready)
            return w

        def transposes(src, n):
            w, slot = work()
            for j in range(n):
                m = pe.transpose(ps[:, slot, j * P:(j + 1) * P], src[:, j * P:(j + 1) * P], ident)
            m.then_inc(work_done, 1)
            return w

        def norm_stats(ktiles, n):
            pe.wait_ge(sq_used, t.next(sq_used, ktiles))
            w, slot = work()
            for j in range(n // P):
                m = pe.matmul(ps[:, slot, j:j + 1], acc[:, j * P:(j + 1) * P], ones[:, 0:1], start=True, stop=True)
            m.then_inc(work_done, 1)
            pe.wait_ge(diag_ready, t.next(diag_ready))
            w, slot = work()
            for a in range(0, n, HALF):
                b = min(a + HALF, n)
                m = pe.matmul(ps[:, slot, a:b], ones, sq[0][:, a:b], start=True, stop=True)
            m.then_inc(work_done, 1)

        def norm_tiles(ktiles):
            base = t.take(norm_ready, ktiles)
            return lambda i: pe.wait_ge(norm_ready, base + i + 1)

        pe.wait_ge(init_in, 32)
        norm_stats(KT, S)
        ready = norm_tiles(KT)

        pe.wait_ge(const_ready, 1)
        for pair in range(SB_PAIRS):
            for _ in range(2):
                product(range(KT), hh, hl, ready=ready)
                ready = None
            w = product(range(KT), hh, hl)
            evacuated(w)
            w = transposes(vt, 8)
            evacuated(w)

            def z_unit(u):
                chunk, kb, first, n = SB_UNITS[u]
                w, slot = work()
                for h in range(2):
                    for j, (l, r) in enumerate(((k_h, qp_h), (k_l, qp_h), (k_h, qp_l))):
                        q0 = chunk * HALF + first
                        m = pe.matmul(ps[:, slot, h * HALF:h * HALF + n], l[:, kb * P:(kb + 1) * P],
                                      r[:, h, q0:q0 + n], start=(j == 0), stop=(j == 2))
                m.then_inc(work_done, 1)

            def suffix(u, tri):
                chunk, kb, first, n = SB_UNITS[u]
                for h in range(2):
                    for r in (sp_h[u % 2], sp_l[u % 2]):
                        m = pe.matmul(aux[:, h, first:first + n], tri[:, :], r[:, h, 0:n],
                                      start=False, stop=True, skip_group_check=True)
                return m

            def clear_sums():
                for h in range(2):
                    pe.matmul(aux[:, h, :], zero_r[:, :], neg_flat, start=True, stop=True, skip_group_check=True)

            def av(u):
                chunk, kb, first, n = SB_UNITS[u]
                pe.wait_ge(pwl_ready, t.next(pwl_ready))
                o = t.o_chunk % 2
                if kb == 4 * chunk + 3:
                    if t.o_chunk >= 2:
                        pe.wait_ge(o_ready, t.o_chunk - 1)
                    pe.matmul(ob[:, o, :], zero_r[:, :], neg_flat, start=True, stop=True, skip_group_check=True)
                for h in range(2):
                    for l, r in ((vp_h, pw_h), (vp_l, pw_h), (vp_h, pw_l)):
                        m = pe.matmul(ob[:, o, first:first + n], l[:, h, kb, :], r[:, h, 0:n],
                                      start=False, stop=True, skip_group_check=True)
                m.then_inc(av_done, 1)
                if kb == 0:
                    t.o_chunk += 1

            if pair == 0:
                t.o_chunk = 0
            z_unit(0)
            for u in range(NU + 1):
                if u + 1 < NU:
                    z_unit(u + 1)
                if u > 0:
                    pe.wait_ge(d_ready, t.next(d_ready))
                if u < NU:
                    if SB_UNITS[u][1] == 4 * SB_UNITS[u][0] + 3:
                        clear_sums()
                    else:
                        suffix(u - 1, rest_r)
                    pe.wait_ge(spl_ready, t.next(spl_ready))
                    suffix(u, tri_r).then_inc(tri_done, 1)
                if u > 0:
                    av(u - 1)

        for j in range(CONV_TILES):
            for _ in range(3):
                product(range(KT), hh, hl)

        for m in range(KT):
            product(range(KT), hh, hl)
            product(range(KT), hh, hl)
            sl = slab()
            product(range(4), o_h, o_l, sl=sl, ready=(lambda i: pe.wait_ge(o_ready, 2 * SB_PAIRS)) if m == 0 else None)
            product(range(4, 8), c_h, c_l, sl=sl,
                    ready=(lambda i: pe.wait_ge(tile_split, CONV_TILES)) if m == 0 else None)
        t.take(tile_split, CONV_TILES)

        def from_split(ktiles):
            base = t.take(tile_split, ktiles)
            return lambda i: pe.wait_ge(tile_split, base + i + 1)

        ready = from_split(KT)
        for m in range(KT):
            product(range(KT), hh, hl, ready=ready if m == 0 else None)

        norm_stats(KT, S)
        norm_stats(KT, S)
        ready = norm_tiles(KT)
        nch = FF // FF_CHUNK
        for c in range(nch + 1):
            if c < nch:
                for j in range(2):
                    product(range(KT), hh, hl, ready=ready)
                    ready = None
            if c > 0:
                b = t.take(tile_split, 2)
                for q in range(2):
                    sl = slab()
                    for m in range(4):
                        product([2 * m, 2 * m + 1], f_h[(c - 1) % 2], f_l[(c - 1) % 2], sl=sl,
                                ready=(lambda i: pe.wait_ge(tile_split, b + i + 1)) if q == m == 0 else None)

        norm_stats(KT, S)
        norm_stats(KT, S)
        nready = norm_tiles(KT)
        ready = from_split(2)
        for q in range(2):
            sl = slab()
            for m in range(4):
                product([2 * m, 2 * m + 1], p_h, p_l, sl=sl, ready=ready)
                ready = None
        for m in range(KT):
            product(range(KT), hh, hl, ready=nready)
            nready = None

        norm_stats(KT, N_MEM)
        ready = norm_tiles(KT)
        for layer in range(2):
            for j in range(2):
                product(range(KT), m_h, m_l, n=N_MEM, ready=ready)
                ready = None
            for j in range(2):
                w = product(range(KT), m_h, m_l, n=N_MEM)
                evacuated(w)
                transposes(mv, 2)

        norm_stats(KT, S)
        ready = norm_tiles(KT)

        def attend(heads, q_of, k_of, v_of, rows, keys_of, causal, bias=None):
            units = [(h, c) for h in range(heads) for c in range(4)]

            def scores(n):
                h, c = units[n]
                keys = keys_of(c)
                for qi in range(2):
                    w, slot = work()
                    q0 = c * 256 + qi * P
                    parts = [(q_of(h)[0][0:rows, q0:q0 + P], k_of(h)[0], rows), (q_of(h)[0][0:rows, q0:q0 + P], k_of(h)[1], rows),
                             (q_of(h)[1][0:rows, q0:q0 + P], k_of(h)[0], rows)]
                    if bias:
                        if c == 0 and qi == 0:
                            pe.wait_ge(ahead_ready, t.next(ahead_ready))
                        parts.append((bias[0][:, q0:q0 + P], bias[1], P))
                    for a, b in widths(keys):
                        masked = causal and b == keys
                        for j, (l, r, n_rows) in enumerate(parts):
                            m = pe.matmul(ps[:, slot, a:b], l, r[0:n_rows, a:b], start=(j == 0),
                                          stop=(j == len(parts) - 1 and not masked), skip_group_check=True)
                        if masked:
                            m = pe.matmul(ps[:, slot, b - 256:b], id_r[:, :], neg_r[:, qi, :], start=False, stop=True,
                                          skip_group_check=True)
                    m.then_inc(work_done, 1)

            def values(n):
                h, c = units[n]
                keys = keys_of(c)
                for j in range(keys // 256):
                    if j == 0:
                        pe.wait_ge(pn_ready, t.next(pn_ready, 2))
                    g = t.take("pt")
                    if g >= 2:
                        pe.wait_ge(ptl_ready, g - 1)
                    for kbl in range(2):
                        for qi in range(2):
                            kb = 2 * j + kbl
                            m = pe.transpose(aux[:, g % 2, kbl * 256 + qi * P:kbl * 256 + (qi + 1) * P],
                                             prob[n % 2][qi][:, kb * P:(kb + 1) * P], ident)
                    m.then_inc(pt_done, 1)
                    if j > 0:
                        value_part(h, c, g - 1, j - 1, keys)
                value_part(h, c, g, keys // 256 - 1, keys)

            def value_part(h, c, g, j, keys):
                o = t.now("oa")
                if j == 0:
                    if o >= 2:
                        pe.wait_ge(oa_taken, o - 1)
                pe.wait_ge(ptl_ready, g + 1)
                last = j == keys // 256 - 1
                for kbl in range(2):
                    kb = 2 * j + kbl
                    for i, (l, r) in enumerate(((0, pt_h), (1, pt_h), (0, pt_l))):
                        m = pe.matmul(ob[0:64, o % 2, 0:256], v_of(h, kb)[l], r[g % 2][:, kbl * 256:(kbl + 1) * 256],
                                      start=(kb == 0 and i == 0), stop=(last and kbl == 1 and i == 2), skip_group_check=True)
                if last:
                    t.take("oa")
                    m.then_inc(oa_done, 1)

            for n in range(len(units) + 1):
                if n < len(units):
                    scores(n)
                if n > 0:
                    values(n - 1)

        def memory_pair(layer, pair, ready):
            w = product(range(KT), hh, hl, ready=ready)
            evacuated(w)
            attend(2, lambda h: (qp_h[:, h, :], qp_l[:, h, :]), lambda h: (km_h[layer][:, pair, :], km_l[layer][:, pair, :]),
                   lambda h, kb: (vm_h[layer][:, kb, pair * P + h * 64:pair * P + h * 64 + 64],
                                  vm_l[layer][:, kb, pair * P + h * 64:pair * P + h * 64 + 64]),
                   P, lambda c: N_MEM, False)

        def gates_and_output():
            for m in range(KT):
                product(range(KT), hh, hl)
            ready = from_split(KT)
            for m in range(KT):
                product(range(KT), y_h, y_l, ready=ready if m == 0 else None)
            norm_stats(KT, S)

        for pair in range(2):
            memory_pair(0, pair, ready)
            ready = None
        for _ in range(6):
            product(range(KT), hh, hl)
        norm_stats(3, S)
        readyq = norm_tiles(3)
        norm_stats(2, S)
        readykv = norm_tiles(2)
        for h in range(MLA_HEADS):
            sl = slab()
            product(range(3), cq_h, cq_l, sl=sl, ready=readyq)
            w = product(range(3, 5), ckv_h, ckv_l, sl=sl, ready=readykv)
            readyq = readykv = None
            evacuated(w)
            w = transposes(kvf, 8)
            evacuated(w)
            attend(1, lambda h: (qa_h, qa_l), lambda h: (ka_h, ka_l),
                   lambda h, kb: (va_h[:, kb, :], va_l[:, kb, :]), 96, lambda c: (c + 1) * 256, True)
        gates_and_output()

        norm_stats(KT, S)
        ready = norm_tiles(KT)
        for pair in range(2):
            memory_pair(1, pair, ready)
            ready = None
        product(range(KT), hh, hl)
        for pair in range(FOX_PAIRS):
            for _ in range(2):
                product(range(KT), hh, hl)
            w = product(range(KT), hh, hl)
            evacuated(w)
            w = transposes(fvt, 8)
            evacuated(w)
            attend(2, lambda h: (qp_h[:, h, :], qp_l[:, h, :]), lambda h: (k_h, k_l),
                   lambda h, kb: (vf_h[:, kb, h * 64:(h + 1) * 64], vf_l[:, kb, h * 64:(h + 1) * 64]),
                   P, lambda c: (c + 1) * 256, True, (a_head, b_all))
        gates_and_output()
        assert t.now("slab") == TOTAL_SLABS, (t.now("slab"), TOTAL_SLABS)

    vcol = lambda c, rows=slice(0, P): vec[rows, c:c + 1]
    ccol = lambda c, rows=slice(0, P): con[rows, c:c + 1]
    LO, HI = slice(0, 64), slice(64, P)

    @block.scalar
    def _(act):
        t = Tally()

        def work():
            w = t.take("work")
            act.wait_ge(work_done, w + 1)
            return w, w % 2

        def skip(n=1):
            t.take("work", n)

        def evacuated(w):
            act.wait_ge(work_free[w % 2], w // 2 + 1)

        def chain(ins):
            ins.then_inc(act_chain, 1)
            act.wait_ge(act_chain, t.next(act_chain))

        def copy(out_, in_, scale=1.0):
            return act.activation(out_, in_, ACT.Copy, scale=scale)

        def take_out(dst, func=ACT.Copy, n=S, **kw):
            w, slot = work()
            act.activation(dst, ps[:, slot, 0:n], func, **kw).then_inc(work_free[slot], 1)
            return w

        def norm_stats(src, ktiles, n, d, ready=None):
            base = t.take(sq_used, ktiles)
            for k in range(ktiles):
                if ready:
                    ready(k)
                if k >= 2:
                    act.wait_ge(sq_used, base + k - 1)
                act.activation(sq[k % 2][:, 0:n], src[:, k, :], ACT.Square).then_inc(sq_ready, 1)
            w, slot = work()
            act.activation(rt[:, 0:n // P], ps[:, slot, 0:n // P], ACT.Sqrt, bias=ccol(C_EPS), scale=1.0 / d).then_inc(rt_ready, 1)
            skip()

        def norm_tiles(ktiles, n, dst):
            for k in range(ktiles):
                act.wait_ge(nt_ready, t.next(nt_ready))
                copy(dst[:, k, :], nt[k % 2][:, 0:n]).then_inc(nh_ready, 1)

        def updated():
            base = t.take(upd_ready, KT)
            return lambda i: act.wait_ge(upd_ready, base + i + 1)

        def q_pair(scale):
            w, slot = work()
            copy(qp_h[LO, 0, :], ps[LO, slot, :], scale)
            copy(qp_h[HI, 1, :], ps[HI, slot, :], scale).then_inc(high_ready, 1)

        act.wait_ge(init_in, 32)
        act.wait_ge(x_in, 16 * KT)
        norm_stats(x_t, KT, S, D)
        norm_tiles(KT, S, hh)

        for pair in range(SB_PAIRS):
            q_pair(SCALE_64)
            w, slot = work()
            copy(k_h[:, :], ps[:, slot, :]).then_inc(high_ready, 1)
            take_out(vt[:, :])
            w, slot = work()
            tiles = ps[:, slot, :].rearrange("p (k f) -> p k f", k=8)
            copy(vp_h[:, 0, :, 0:64], tiles[:, :, 0:64])
            copy(vp_h[:, 1, :, 64:P], tiles[:, :, 64:P]).then_inc(high_ready, 1)
            d_base, spl_base, av_base = t.take(d_ready, NU), t.take(spl_ready, NU), t.take(av_done, NU)
            for u in range(NU + 2):
                if u < NU:
                    n = SB_UNITS[u][3]
                    w = t.take("work")
                    evacuated(w)
                    if spl_base + u > 0:
                        act.wait_ge(spl_ready, spl_base + u)
                    z, e = zb[u % 2][:, :, 0:n], eb[:, :, 0:n]
                    chain(act.activation(e, z, ACT.Abs))
                    chain(act.activation(e, e, ACT.Exp, scale=-1.0))
                if 0 < u <= NU:
                    nb = SB_UNITS[u - 1][3]
                    zp = zb[(u - 1) % 2][:, :, 0:nb]
                    act.wait_ge(d_ready, d_base + u)
                    act.activation(zp, zp, ACT.Exp).then_inc(act_chain, 1)
                    exp_done = t.next(act_chain)
                if u < NU:
                    act.activation(e, e, ACT.Ln, bias=ccol(C_ONE), scale=1.0).then_inc(ln_ready, 1)
                if 0 < u <= NU:
                    act.wait_ge(act_chain, exp_done)
                    if av_base + u > 1:
                        act.wait_ge(av_done, av_base + u - 1)
                    copy(pw_h[:, :, 0:nb], zp).then_inc(pwh_ready, 1)
                if u < NU:
                    act.wait_ge(sp_ready, t.next(sp_ready))
                    copy(sp_h[u % 2][:, :, 0:n], e).then_inc(sph_ready, 1)
                if u >= 2 and SB_UNITS[u - 2][1] == 0:
                    o = t.take("o_chunk")
                    if av_base + u > 1:
                        act.wait_ge(av_done, av_base + u - 1)
                    c = SB_UNITS[u - 2][0]
                    copy(o_h[:, pair, c * HALF:(c + 1) * HALF], ob[:, o % 2, :]).then_inc(oh_ready, 1)

        for j in range(CONV_TILES):
            take_out(cc[:, :])
            skip()
            w = t.take("work")
            evacuated(w)
            copy(c_h[:, j, :], cv[:, :]).then_inc(high_ready, 1)

        base = t.take(tile_ready, KT)
        for m in range(KT):
            if base + m > 0:
                act.wait_ge(tile_ready, base + m)
            take_out(ga[:, :], ACT.Sigmoid, bias=vcol(V_BGA + m))
            take_out(gc[:, :], ACT.Sigmoid, bias=vcol(V_BGC + m))
            skip(2)
        act.wait_ge(work_done, t.now("work"))
        act.wait_ge(tile_ready, base + KT)
        act.dma_start(x_t[:, :, :], xt.rearrange("(k p) s -> p k s", p=P)).then_inc(xold_in, 16)
        for k in range(KT):
            copy(hh[:, k, :], mix_t[:, k, :]).then_inc(high_ready, 1)

        for m in range(KT):
            take_out(y_t[:, m, :])
        barrier(act, t, act_end)
        norm_stats(y_t, KT, S, D)
        norm_stats(x_t, KT, S, D, updated())
        norm_tiles(KT, S, hh)

        nch = FF // FF_CHUNK
        for c in range(nch + 1):
            if c < nch:
                for j in range(2):
                    take_out(fr[:, :], ACT.Relu)
                    act.wait_ge(tile_ready, t.next(tile_ready))
                    copy(f_h[c % 2][:, j, :], ff[:, :]).then_inc(high_ready, 1)
            if c == 1:
                for m in range(KT):
                    take_out(y_t[:, m, :])
            elif c > 1:
                skip(KT)
        barrier(act, t, act_end)
        act.dma_start(p_t[:, :, :], pt.rearrange("(k p) s -> p k s", p=P)).then_inc(p_in, 16)
        norm_stats(y_t, KT, S, D)
        norm_stats(x_t, KT, S, D, updated())
        norm_tiles(KT, S, hh)

        barrier(act, t, act_end)
        act.wait_ge(p_in, 16)
        for k in range(2):
            copy(p_h[:, k, :], p_t[:, k, :]).then_inc(high_ready, 1)
        for m in range(KT):
            take_out(y_t[:, m, :])
        base = t.take(tile_ready, KT)
        for m in range(KT):
            if base + m > 0:
                act.wait_ge(tile_ready, base + m)
            take_out(pg[:, :], ACT.Sigmoid)
        act.wait_ge(tile_ready, base + KT)
        spilled = [0]

        def spill():
            act.dma_start(spill_x, x_t[:, :, :]).then_inc(spill_done, 16)
            spilled[0] += 16

        spill()
        act.dma_start(m_t[:, :, :], memt.rearrange("(k p) s -> p k s", p=P)).then_inc(m_in, 16)
        barrier(act, t, act_end)
        act.wait_ge(m_in, 16)
        norm_stats(m_t, KT, N_MEM, D)
        norm_tiles(KT, N_MEM, m_h)
        for layer in range(2):
            for j in range(2):
                w, slot = work()
                copy(km_h[layer][:, j, :], ps[:, slot, 0:N_MEM]).then_inc(high_ready, 1)
            for j in range(2):
                take_out(mv[:, :], n=N_MEM)
                w, slot = work()
                copy(vm_h[layer][:, :, j * P:(j + 1) * P], ps[:, slot, 0:N_MEM].rearrange("p (k f) -> p k f", k=2)).then_inc(high_ready, 1)
        barrier(act, t, act_end)
        norm_stats(x_t, KT, S, D)
        norm_tiles(KT, S, hh)

        def attend(heads, scale, keys_of, rows_of, tile):
            units = [(h, c) for h in range(heads) for c in range(4)]
            for n in range(len(units) + 1):
                if n < len(units):
                    keys = keys_of(units[n][1])
                    for qi in range(2):
                        w = t.take("work")
                        i = (2 * n + qi) % 4
                        act.wait_ge(nm_ready, t.next(nm_ready))
                        act.activation(prob[n % 2][qi][:, 0:keys], ps[:, w % 2, 0:keys], ACT.Exp, bias=nm[:, i:i + 1],
                                           scale=scale, accum_out=rsum[:, i:i + 1]).then_inc(p_ready, 1)
                if n > 0:
                    h, c = units[n - 1]
                    for j in range(keys_of(c) // 256):
                        g = t.take("pt")
                        act.wait_ge(pt_done, g + 1)
                        copy(pt_h[g % 2][:, :], aux[:, g % 2, :]).then_inc(pth_ready, 1)
                    o = t.take("oa")
                    act.wait_ge(oa_done, o + 1)
                    if c == 0 and rows_of(h) == LO:
                        if t.now(ot_out) > 0:
                            act.wait_ge(ot_out, t.now(ot_out))
                    copy(ot[rows_of(h), c * 256:(c + 1) * 256], ob[0:64, o % 2, 0:256]).then_inc(oa_taken, 1)
            if tile is not None:
                act.wait_ge(oa_taken, t.now("oa"))
                act.dma_start(spill_out[tile], ot[:, :]).then_inc(ot_out, 16)
                t.take(ot_out, 16)

        halves = lambda h: (LO, HI)[h]

        def memory_pair(pair):
            q_pair(1.0)
            attend(2, SCALE_64, lambda c: N_MEM, halves, MAIN_TILES + pair)

        def gates_and_output():
            barrier(act, t, act_end)
            if t.now(ot_out) > 0:
                act.wait_ge(ot_out, t.now(ot_out))
            base, n_out = t.take(tile_ready, KT), t.take(out_in, KT) // 4

            def fetch(m):
                act.dma_start(go[m % 4][:, :], spill_out[m]).then_inc(out_in[m % 4], 16)

            for m in range(4):
                fetch(m)
            for m in range(KT):
                if m > 0:
                    act.wait_ge(tile_ready, base + m)
                last = take_out(gt[m % 2][:, :], ACT.Silu)
                if m > 0:
                    if base + m > 0:
                        act.wait_ge(tile_ready, base + m)
                    copy(y_h[:, m - 1, :], gt[(m - 1) % 2][:, :]).then_inc(high_ready, 1)
                    if m + 3 < KT:
                        fetch(m + 3)
            act.wait_ge(tile_ready, base + KT)
            copy(y_h[:, KT - 1, :], gt[(KT - 1) % 2][:, :]).then_inc(high_ready, 1)
            act.wait_ge(work_done, last + 1)
            act.wait_ge(spill_done, spilled[0])
            act.dma_start(xold_t[:, :, :], spill_x).then_inc(xold_in, 16)
            for m in range(KT):
                take_out(z_t[:, m, :])
            barrier(act, t, act_end)
            norm_stats(z_t, KT, S, D)

        barrier(act, t, act_end)
        for pair in range(2):
            memory_pair(pair)
        barrier(act, t, act_end)
        act.dma_start(posi[HI, :], pos.partition_broadcast(64)).then_inc(pos_in, 16)
        for j in range(3):
            take_out(cq_t[:, j, :])
        for j in range(2):
            take_out(ckv_t[:, j, :])
        skip()
        act.wait_ge(table_ready, 1)
        act.activation(trig[HI, :], ang[1][HI, :], ACT.Sin).then_inc(sin_ready, 1)
        if t.now(ot_out) > 0:
            act.wait_ge(ot_out, t.now(ot_out))
        act.wait_ge(spill_done, spilled[0])
        barrier(act, t, act_end)
        norm_stats(cq_t, 3, S, 384)
        norm_tiles(3, S, cq_h)
        norm_stats(ckv_t, 2, S, 256)
        norm_tiles(2, S, ckv_h)
        barrier(act, t, act_end)
        copy(ka_h[64:96, :], qf[64:96, :]).then_inc(high_ready, 1)
        for h in range(MLA_HEADS):
            w, slot = work()
            copy(qf[LO, :], ps[LO, slot, :]).then_inc(qn_ready, 1)
            act.wait_ge(rope_ready, t.next(rope_ready))
            copy(qa_h[0:96, :], qf[0:96, :]).then_inc(high_ready, 1)
            w, slot = work()
            chain(copy(kvf[:, :], ps[:, slot, :]))
            copy(ka_h[LO, :], kvf[LO, :]).then_inc(high_ready, 1)
            w, slot = work()
            copy(va_h[:, :, :], ps[:, slot, :].rearrange("p (k f) -> p k f", k=8)[:, :, 64:P]).then_inc(high_ready, 1)
            attend(1, SCALE_MLA, lambda c: (c + 1) * 256, lambda _: halves(h % 2), h // 2 if h % 2 else None)
        gates_and_output()
        ready = updated()
        norm_stats(x_t, KT, S, D, ready)
        spill()
        norm_tiles(KT, S, hh)

        barrier(act, t, act_end)
        act.wait_ge(spill_done, spilled[0])
        for pair in range(2):
            memory_pair(pair)
        w, slot = work()
        act.activation(fx[:, :], ps[:, slot, :], ACT.Identity, bias=vcol(V_BF)).then_inc(work_free[slot], 1)
        evacuated(w)
        chain(act.activation(fe[:, :], fx[:, :], ACT.Abs))
        chain(act.activation(fe[:, :], fe[:, :], ACT.Exp, scale=-1.0))
        act.activation(fe[:, :], fe[:, :], ACT.Ln, bias=ccol(C_ONE), scale=1.0).then_inc(ln_ready, 1)
        for pair in range(FOX_PAIRS):
            q_pair(1.0)
            w, slot = work()
            copy(k_h[:, :], ps[:, slot, :]).then_inc(high_ready, 1)
            take_out(fvt[:, :])
            w, slot = work()
            copy(vf_h[:, :, :], ps[:, slot, :].rearrange("p (k f) -> p k f", k=8)).then_inc(high_ready, 1)
            attend(2, SCALE_64, lambda c: (c + 1) * 256, halves, pair)
        gates_and_output()

    @block.vector
    def _(dve):
        t = Tally()

        def work():
            w = t.take("work")
            dve.wait_ge(work_done, w + 1)
            return w, w % 2

        def skip(n=1):
            t.take("work", n)

        def evacuated(w):
            dve.wait_ge(work_free[w % 2], w // 2 + 1)

        def link(ins):
            ins.then_inc(dve_chain, 1)
            return t.next(dve_chain)

        def chain(ins):
            dve.wait_ge(dve_chain, link(ins))

        def low(dst, src, hi):
            return dve.tensor_tensor(dst, src, hi.bitcast(F32), ALU.subtract)

        def low_out(dst, hi, slot_src, slot):
            dve.wait_ge(high_ready, t.next(high_ready))
            low(dst, slot_src, hi).then_inc(work_free[slot], 1)

        def norm_stats(ktiles, n):
            base, used = t.take(sq_ready, ktiles), t.take(sq_used, ktiles)
            for k in range(ktiles):
                dve.wait_ge(sq_ready, base + k + 1)
                if k == 0:
                    dve.tensor_copy(acc[:, 0:n], sq[0][:, 0:n]).then_inc(sq_used, 1)
                else:
                    dve.wait_ge(sq_used, used + k)
                    dve.tensor_tensor(acc[:, 0:n], acc[:, 0:n], sq[k % 2][:, 0:n], ALU.add).then_inc(sq_used, 1)
            w = t.take("work")
            dve.wait_ge(rt_ready, t.next(rt_ready))
            dve.reciprocal(rs[:, 0:n // P], rt[:, 0:n // P]).then_inc(work_free[w % 2], 1)
            evacuated(w)
            for j in range(n // P):
                i = dve.tensor_scalar(sq[0][:, j * P:(j + 1) * P], ident, rs[:, j:j + 1], None, ALU.mult)
            i.then_inc(diag_ready, 1)
            return work()

        def norm_tiles(src, ktiles, n, gain, hi, lo, slot):
            base = t.take(norm_ready, ktiles)
            for k in range(ktiles + 1):
                if k < ktiles:
                    if k >= 2:
                        dve.wait_ge(norm_ready, base + k - 1)
                    dve.scalar_tensor_tensor(out=nt[k % 2][:, 0:n], in0=src[:, k, :], scalar=vcol(gain + k),
                                                 in1=ps[:, slot, 0:n], op0=ALU.mult, op1=ALU.mult).then_inc(nt_ready, 1)
                if k > 0:
                    dve.wait_ge(nh_ready, t.next(nh_ready))
                    low(lo[:, k - 1, :], nt[(k - 1) % 2][:, 0:n], hi[:, k - 1, :]).then_inc(norm_ready, 1)
            dve.drain().then_inc(work_free[slot], 1)

        def norm(src, ktiles, n, gain, hi, lo):
            w, slot = norm_stats(ktiles, n)
            norm_tiles(src, ktiles, n, gain, hi, lo, slot)

        def update(ysrc, xsrc, dst, gain, ready=upd_ready):
            w, slot = norm_stats(KT, S)
            before = None
            for k in range(KT + 1):
                if k < KT:
                    now = link(dve.scalar_tensor_tensor(out=ysrc[:, k, :], in0=ysrc[:, k, :], scalar=vcol(gain + k),
                                                        in1=ps[:, slot, :], op0=ALU.mult, op1=ALU.mult))
                if k > 0:
                    dve.wait_ge(dve_chain, before)
                    dve.tensor_tensor(dst[:, k - 1, :], xsrc[:, k - 1, :], ysrc[:, k - 1, :], ALU.add).then_inc(ready, 1)
                before = now
            dve.drain().then_inc(work_free[slot], 1)

        def zero_pads():
            for q in (qp_h, qp_l):
                dve.memset(q[HI, 0, :].bitcast(F32), 0.0)
                i = dve.memset(q[LO, 1, :].bitcast(F32), 0.0)
            return i

        def q_pair(scale):
            w, slot = work()
            dve.wait_ge(high_ready, t.next(high_ready))
            for h, rows in ((0, LO), (1, HI)):
                i = dve.scalar_tensor_tensor(out=qp_l[rows, h, :], in0=ps[rows, slot, :], scalar=scale,
                                             in1=qp_h[rows, h, :].bitcast(F32), op0=ALU.mult, op1=ALU.subtract)
            i.then_inc(work_free[slot], 1)

        dve.wait_ge(init_in, 32)
        for dst, c in ((tri_r, C_TRI), (rest_r, C_REST), (id_r, C_ID)):
            dve.tensor_copy(dst[:, :], con[:, c:c + P])
        dve.tensor_copy(neg_flat, con[:, C_NEG:C_NEG + 512])
        dve.memset(zero_r[:, :].bitcast(F32), 0.0)
        dve.memset(vp_h[:, 0, :, 64:P].bitcast(F32), 0.0)
        dve.memset(vp_h[:, 1, :, 0:64].bitcast(F32), 0.0)
        dve.memset(vp_l[:, 0, :, 64:P].bitcast(F32), 0.0)
        dve.memset(vp_l[:, 1, :, 0:64].bitcast(F32), 0.0)
        zero_pads().then_inc(const_ready, 1)
        dve.wait_ge(x_in, 16 * KT)
        norm(x_t, KT, S, V_PRE, hh, hl)

        for pair in range(SB_PAIRS):
            q_pair(SCALE_64)
            w, slot = work()
            low_out(k_l[:, :], k_h[:, :], ps[:, slot, :], slot)
            skip()
            w, slot = work()
            dve.wait_ge(high_ready, t.next(high_ready))
            tiles = ps[:, slot, :].rearrange("p (k f) -> p k f", k=8)
            dve.tensor_tensor(vp_l[:, 0, :, 0:64], tiles[:, :, 0:64], vp_h[:, 0, :, 0:64].bitcast(F32), ALU.subtract)
            low(vp_l[:, 1, :, 64:P], tiles[:, :, 64:P], vp_h[:, 1, :, 64:P]).then_inc(work_free[slot], 1)
            pwl_base = t.take(pwl_ready, NU)
            for u in range(NU + 2):
                if 0 < u <= NU:
                    chunk, kb, first, nb = SB_UNITS[u - 1]
                    z = zb[(u - 1) % 2]
                    dve.wait_ge(tri_done, t.next(tri_done))
                    d = dve.tensor_tensor(z[:, :, 0:nb], z[:, :, 0:nb], aux[:, :, first:first + nb], ALU.subtract)
                    if kb >= 4 * chunk:
                        chain(d)
                        a, b = (0, 256) if kb == 4 * chunk + 3 else (0, P)
                        for h in range(2):
                            d = dve.tensor_tensor(z[:, h, a:b], z[:, h, a:b], con[:, C_CAP + 256 - b:C_CAP + 256], ALU.min)
                    d.then_inc(d_ready, 1)
                if u < NU:
                    chunk, kb, first, n = SB_UNITS[u]
                    w, slot = work()
                    z, e = zb[u % 2], eb
                    if pwl_base + u > 1:
                        dve.wait_ge(pwl_ready, pwl_base + u - 1)
                    zsrc = ps[:, slot, :].rearrange("p (h q) -> p h q", h=2)
                    dve.tensor_copy(z[:, :, 0:n], zsrc[:, :, 0:n]).then_inc(work_free[slot], 1)
                    evacuated(w)
                    dve.wait_ge(ln_ready, t.next(ln_ready))
                    i = dve.scalar_tensor_tensor(out=e[:, :, 0:n], in0=z[:, :, 0:n], scalar=0.0, in1=e[:, :, 0:n],
                                                 op0=ALU.max, op1=ALU.add)
                    if kb >= 4 * chunk:
                        chain(i)
                        b = 256 if kb == 4 * chunk + 3 else P
                        for h in range(2):
                            i = dve.tensor_tensor(e[:, h, 0:b], e[:, h, 0:b], con[:, C_MASK01 + 256 - b:C_MASK01 + 256], ALU.mult)
                    i.then_inc(sp_ready, 1)
                if 0 < u <= NU:
                    dve.wait_ge(pwh_ready, t.next(pwh_ready))
                    low(pw_l[:, :, 0:nb], zb[(u - 1) % 2][:, :, 0:nb], pw_h[:, :, 0:nb]).then_inc(pwl_ready, 1)
                if u < NU:
                    dve.wait_ge(sph_ready, t.next(sph_ready))
                    low(sp_l[u % 2][:, :, 0:n], e[:, :, 0:n], sp_h[u % 2][:, :, 0:n]).then_inc(spl_ready, 1)
                if u >= 2 and SB_UNITS[u - 2][1] == 0:
                    o = t.take("o_chunk")
                    c = SB_UNITS[u - 2][0]
                    dve.wait_ge(oh_ready, t.next(oh_ready))
                    cols = slice(c * HALF, (c + 1) * HALF)
                    low(o_l[:, pair, cols], ob[:, o % 2, :], o_h[:, pair, cols]).then_inc(o_ready, 1)

        chain(dve.memset(cu[:, 0:2], 0.0))
        for j in range(CONV_TILES):
            w = t.take("work")
            w2, slot = work()
            evacuated(w)
            dve.tensor_tensor(cu[:, 2:2 + S], ps[:, slot, :], cc[:, :], ALU.mult).then_inc(work_free[slot], 1)
            evacuated(w2)
            if j > 0:
                dve.wait_ge(tile_split, j)
            chain(dve.tensor_scalar(cv[:, :], cu[:, 2:2 + S], vcol(V_CONV + 8 + j), None, ALU.mult))
            for tap in (1, 0):
                chain(dve.scalar_tensor_tensor(out=cv[:, :], in0=cu[:, tap:tap + S], scalar=vcol(V_CONV + 4 * tap + j),
                                               in1=cv[:, :], op0=ALU.mult, op1=ALU.add))
            w, slot = work()
            dve.tensor_tensor(cv[:, :], cv[:, :], ps[:, slot, :], ALU.mult).then_inc(work_free[slot], 1)
            dve.wait_ge(high_ready, t.next(high_ready))
            low(c_l[:, j, :], cv[:, :], c_h[:, j, :]).then_inc(tile_split, 1)

        for m in range(KT):
            wa, wc = t.take("work"), t.take("work")
            w, slot = work()
            evacuated(wa)
            dve.tensor_tensor(ga[:, :], ps[:, slot, :], ga[:, :], ALU.mult).then_inc(work_free[slot], 1)
            w2, slot = work()
            evacuated(wc)
            dve.tensor_tensor(gc[:, :], ps[:, slot, :], gc[:, :], ALU.mult).then_inc(work_free[slot], 1)
            evacuated(w)
            evacuated(w2)
            dve.tensor_tensor(mix_t[:, m, :], ga[:, :], gc[:, :], ALU.add).then_inc(tile_ready, 1)
        for k in range(KT):
            dve.wait_ge(high_ready, t.next(high_ready))
            low(hl[:, k, :], mix_t[:, k, :], hh[:, k, :]).then_inc(tile_split, 1)
        skip(KT)
        barrier(dve, t, dve_end)
        dve.wait_ge(xold_in, 16)
        update(y_t, x_t, x_t, V_POST)
        norm(x_t, KT, S, V_MLP, hh, hl)

        nch = FF // FF_CHUNK
        t.take(tile_split, CONV_TILES + KT)
        for c in range(nch + 1):
            if c < nch:
                for j in range(2):
                    w = t.take("work")
                    evacuated(w)
                    if t.now(tile_split) > 0:
                        dve.wait_ge(tile_split, t.now(tile_split))
                    dve.tensor_tensor(ff[:, :], fr[:, :], fr[:, :], ALU.mult).then_inc(tile_ready, 1)
                    dve.wait_ge(high_ready, t.next(high_ready))
                    low(f_l[c % 2][:, j, :], ff[:, :], f_h[c % 2][:, j, :]).then_inc(tile_split, 1)
                    t.take(tile_split)
            if c == 1:
                skip(KT)
            elif c > 1:
                for m in range(KT):
                    w, slot = work()
                    dve.tensor_tensor(y_t[:, m, :], y_t[:, m, :], ps[:, slot, :], ALU.add).then_inc(work_free[slot], 1)
        barrier(dve, t, dve_end)
        update(y_t, x_t, x_t, V_POSTMLP)
        norm(x_t, KT, S, V_PLE, hh, hl)

        barrier(dve, t, dve_end)
        for k in range(2):
            dve.wait_ge(high_ready, t.next(high_ready))
            low(p_l[:, k, :], p_t[:, k, :], p_h[:, k, :]).then_inc(tile_split, 1)
        skip(KT)
        for m in range(KT):
            w = t.take("work")
            evacuated(w)
            chain(dve.tensor_tensor(pg[:, :], pg[:, :], y_t[:, m, :], ALU.mult))
            dve.tensor_tensor(x_t[:, m, :], x_t[:, m, :], pg[:, :], ALU.add).then_inc(tile_ready, 1)
        barrier(dve, t, dve_end)
        norm(m_t, KT, N_MEM, V_MEM, m_h, m_l)
        for layer in range(2):
            for j in range(2):
                w, slot = work()
                low_out(km_l[layer][:, j, :], km_h[layer][:, j, :], ps[:, slot, 0:N_MEM], slot)
            for j in range(2):
                skip()
                w, slot = work()
                low_out(vm_l[layer][:, :, j * P:(j + 1) * P], vm_h[layer][:, :, j * P:(j + 1) * P],
                        ps[:, slot, 0:N_MEM].rearrange("p (k f) -> p k f", k=2), slot)
        barrier(dve, t, dve_end)
        norm(x_t, KT, S, V_PRE2, hh, hl)

        def attend(heads, scale, keys_of, first_head=None):
            units = [(h, c) for h in range(heads) for c in range(4)]
            for n in range(len(units) + 1):
                if n < len(units):
                    h, c = units[n]
                    keys = keys_of(c)
                    if first_head is not None and c == 0:
                        dve.tensor_scalar(a_head[:, :], a_base[:, :], ccol(C_HEAD + first_head + h), None, ALU.mult).then_inc(ahead_ready, 1)
                    slots = []
                    for qi in range(2):
                        i = (2 * n + qi) % 4
                        w, slot = work()
                        slots.append((w, slot))
                        chain(dve.reduce_max(mx[:, i:i + 1], ps[:, slot, 0:keys], AX.X))
                        dve.tensor_scalar(nm[:, i:i + 1], mx[:, i:i + 1], -scale, None, ALU.mult).then_inc(nm_ready, 1)
                    for qi in range(2):
                        i = (2 * n + qi) % 4
                        w, slot = slots[qi]
                        dve.wait_ge(p_ready, t.next(p_ready))
                        dve.reciprocal(rinv[:, i:i + 1], rsum[:, i:i + 1]).then_inc(work_free[slot], 1)
                        evacuated(w)
                        p = prob[n % 2][qi][:, 0:keys]
                        dve.tensor_scalar(p, p, rinv[:, i:i + 1], None, ALU.mult).then_inc(pn_ready, 1)
                if n > 0:
                    for j in range(keys_of(units[n - 1][1]) // 256):
                        g = t.take("pt")
                        dve.wait_ge(pth_ready, t.next(pth_ready))
                        low(pt_l[g % 2][:, :], aux[:, g % 2, :], pt_h[g % 2][:, :]).then_inc(ptl_ready, 1)

        def memory_pair():
            q_pair(1.0)
            attend(2, SCALE_64, lambda c: N_MEM)

        def gates_and_output(gain, ready):
            barrier(dve, t, dve_end)
            n_out = t.take("out_use", KT) // 4
            for m in range(KT):
                w = t.take("work")
                evacuated(w)
                dve.wait_ge(out_in[m % 4], 16 * (n_out + m // 4 + 1))
                g = gt[m % 2][:, :]
                dve.tensor_tensor(g, g, go[m % 4][:, :], ALU.mult).then_inc(tile_ready, 1)
                dve.wait_ge(high_ready, t.next(high_ready))
                low(y_l[:, m, :], g, y_h[:, m, :]).then_inc(tile_split, 1)
            skip(KT)
            barrier(dve, t, dve_end)
            dve.wait_ge(xold_in, 32 if gain == V_POST2 else 48)
            update(z_t, xold_t, x_t, gain, ready)

        def rope(slot, dst):
            chain(dve.tensor_tensor(dst[64:96, :], ps[64:96, slot, :], trig[64:96, :], ALU.mult))
            chain(dve.tensor_tensor(ps[64:96, slot, :], ps[96:P, slot, :], trig[96:P, :], ALU.mult))
            return dve.tensor_tensor(dst[64:96, :], ps[64:96, slot, :], dst[64:96, :], ALU.add)

        barrier(dve, t, dve_end)
        zero_pads()
        for _ in range(2):
            memory_pair()
        barrier(dve, t, dve_end)
        dve.wait_ge(pos_in, 16)
        a0, a1, a2 = (a[HI, :] for a in ang)
        chain(dve.tensor_copy(a0, posi[HI, :]))
        chain(dve.tensor_scalar(a1, a0, ccol(C_INV, HI), None, ALU.mult))
        chain(dve.tensor_scalar(a2, a1, 1.0 / (2 * np.pi), None, ALU.mult))
        chain(dve.tensor_scalar(a2, a2, ccol(C_OFF, HI), None, ALU.add))
        chain(dve.tensor_scalar(a2, a2, 12582912.0, None, ALU.add))
        chain(dve.tensor_scalar(a2, a2, -12582912.0, None, ALU.add))
        turn = 2 * np.pi
        c1 = 6.28125
        c2 = float(np.float32(np.round((turn - c1) * 2 ** 21) / 2 ** 21))
        c3 = float(np.float32(turn - c1 - c2))
        for c in (c1, c2, c3):
            chain(dve.scalar_tensor_tensor(out=a1, in0=a2, scalar=-c, in1=a1, op0=ALU.mult, op1=ALU.add))
        chain(dve.tensor_scalar(a1, a1, ccol(C_SHIFT, HI), None, ALU.add))
        dve.tensor_scalar(a1, a1, 3.1415925, -3.1415925, ALU.min, ALU.max).then_inc(table_ready, 1)
        dve.wait_ge(sin_ready, t.next(sin_ready))
        chain(dve.tensor_scalar(trig[96:P, :], trig[96:P, :], ccol(C_SIGN, slice(96, P)), None, ALU.mult))
        skip(5)
        w, slot = work()
        rope(slot, qf).then_inc(work_free[slot], 1)
        barrier(dve, t, dve_end)
        norm(cq_t, 3, S, V_QN, cq_h, cq_l)
        norm(ckv_t, 2, S, V_KVN, ckv_h, ckv_l)
        barrier(dve, t, dve_end)
        dve.wait_ge(high_ready, t.next(high_ready))
        chain(dve.tensor_tensor(ka_l[64:96, :], qf[64:96, :], ka_h[64:96, :].bitcast(F32), ALU.subtract))
        for h in range(MLA_HEADS):
            w, slot = work()
            dve.wait_ge(qn_ready, t.next(qn_ready))
            rope(slot, qf).then_inc(rope_ready, 1)
            dve.wait_ge(high_ready, t.next(high_ready))
            low(qa_l[0:96, :], qf[0:96, :], qa_h[0:96, :]).then_inc(work_free[slot], 1)
            w, slot = work()
            low_out(ka_l[LO, :], ka_h[LO, :], kvf[LO, :], slot)
            w, slot = work()
            low_out(va_l[:, :, :], va_h[:, :, :], ps[:, slot, :].rearrange("p (k f) -> p k f", k=8)[:, :, 64:P], slot)
            attend(1, SCALE_MLA, lambda c: (c + 1) * 256)
        gates_and_output(V_POST2, upd_ready)
        norm(x_t, KT, S, V_PRE2 + 8, hh, hl)

        barrier(dve, t, dve_end)
        zero_pads()
        for _ in range(2):
            memory_pair()
        w = t.take("work")
        chain(dve.memset(fone[:, :], 1.0))
        dve.wait_ge(ln_ready, t.next(ln_ready))
        chain(dve.scalar_tensor_tensor(out=fe[:, :], in0=fx[:, :], scalar=0.0, in1=fe[:, :], op0=ALU.min, op1=ALU.subtract))
        chain(dve.tensor_tensor_scan(out=fx[:, :], data0=fone[:, :], data1=fe[:, :], initial=0.0, op0=ALU.mult, op1=ALU.add))
        chain(dve.tensor_scalar(fx[:, :], fx[:, :], 1.0 / SCALE_64, None, ALU.mult))
        chain(dve.tensor_copy(b_all[:, :], fx[:, :]))
        chain(dve.tensor_copy(a_base[0:32, :], b_all[0:32, :].bitcast(F32)))
        chain(dve.tensor_tensor(a_base[32:64, :], fx[32:64, :], b_all[32:64, :].bitcast(F32), ALU.subtract))
        chain(dve.memset(a_base[HI, :], -1.0))
        chain(dve.tensor_tensor(b_all[96:P, :], fx[96:P, :], b_all[96:P, :].bitcast(F32), ALU.subtract))
        chain(dve.memset(b_all[LO, :].bitcast(F32), 1.0))
        for pair in range(FOX_PAIRS):
            q_pair(1.0)
            w, slot = work()
            low_out(k_l[:, :], k_h[:, :], ps[:, slot, :], slot)
            skip()
            w, slot = work()
            low_out(vf_l[:, :, :], vf_h[:, :, :], ps[:, slot, :].rearrange("p (k f) -> p k f", k=8), slot)
            attend(2, SCALE_64, lambda c: (c + 1) * 256, 2 * pair)
        gates_and_output(V_POST2 + 8, final_ready)


    ctx.close()



def tiles_of(w):
    k, m = w.shape[0] // P, w.shape[1] // P
    return w.reshape(k, P, m, P).transpose(2, 1, 0, 3)


def padded(w, cols):
    full = np.zeros((w.shape[0], P), np.float32)
    for at, a, b in cols:
        full[:, at:at + b - a] = w[:, a:b]
    return full


def weight_stream(w_in, w_attn_out, w_conv_out, w_o, w_up, w_down, w_ple_gate, w_ple_proj, w_mem_kv,
                  w_out, w_in_a, w_q_up_a, w_kv_up_a, w_in_b):
    slabs = []
    win = tiles_of(w_in)
    for pair in range(SB_PAIRS):
        slabs += [win[4 * i + pair] for i in range(3)]
    for j in range(CONV_TILES):
        slabs += [win[12 + 4 * i + j] for i in (1, 2, 0)]
    ao, co = tiles_of(w_attn_out), tiles_of(w_conv_out)
    for m in range(KT):
        slabs += [win[24 + m], win[32 + m], np.concatenate([ao[m], co[m]], 1)]
    slabs += list(tiles_of(w_o))
    up = tiles_of(w_up)
    for c in range(FF // FF_CHUNK + 1):
        if c < FF // FF_CHUNK:
            slabs += [up[2 * c], up[2 * c + 1]]
        if c > 0:
            down = tiles_of(w_down[(c - 1) * FF_CHUNK:c * FF_CHUNK])
            slabs += [np.concatenate(down[4 * q:4 * q + 4], 1) for q in range(2)]
    pp = tiles_of(w_ple_proj)
    slabs += [np.concatenate(pp[4 * q:4 * q + 4], 1) for q in range(2)]
    slabs += list(tiles_of(w_ple_gate))
    for layer in range(2):
        slabs += list(tiles_of(w_mem_kv[layer]))
    slabs += list(tiles_of(w_in_a[:, 672:928])) + list(tiles_of(w_in_a[:, 0:640]))
    slabs += list(tiles_of(padded(w_in_a, [(64, 640, 672), (96, 656, 672), (112, 640, 656)])))
    for h in range(MLA_HEADS):
        q = tiles_of(padded(w_q_up_a, [(0, 96 * h, 96 * h + 96), (96, 96 * h + 80, 96 * h + 96), (112, 96 * h + 64, 96 * h + 80)]))[0]
        kv = tiles_of(w_kv_up_a[:, P * h:P * (h + 1)])[0]
        slabs.append(np.concatenate([q, kv, np.zeros((P, 3, P), np.float32)], 1))
    slabs += list(tiles_of(w_in_a[:, 928:1952])) + list(tiles_of(w_out[0]))
    slabs += list(tiles_of(w_in_b[:, 2316:2572]))
    slabs += list(tiles_of(padded(w_in_b, [(32 * q, 2304, 2316) for q in range(4)])))
    qkv = tiles_of(w_in_b[:, 0:2304])
    for pair in range(FOX_PAIRS):
        slabs += [qkv[6 * i + pair] for i in range(3)]
    slabs += list(tiles_of(w_in_b[:, 2572:3596])) + list(tiles_of(w_out[1]))
    assert len(slabs) == TOTAL_SLABS
    return np.ascontiguousarray(np.stack(slabs))


def vectors(gains, b_gate, w_conv, b_f):
    v = np.zeros((P, N_VEC), np.float32)
    for at, g in gains:
        v[:, at:at + g.size // P] = g.reshape(-1, P).T
    v[:, V_BGA:V_BGA + 16] = b_gate.reshape(16, P).T
    v[:, V_CONV:V_CONV + 12] = w_conv.reshape(12, P).T
    for q in range(4):
        v[32 * q:32 * q + MLA_HEADS, V_BF] = b_f
    return v


def constants():
    c = np.zeros((P, N_CONST), np.float32)
    i = np.arange(P)
    before = i[:, None] < i[None, :]
    c[:, C_ID:C_ID + P] = np.eye(P)
    c[:, C_ONE:C_ONE + P] = 1.0
    c[:, C_TRI:C_TRI + P] = ~before
    c[:, C_REST:C_REST + P] = before
    c[:, C_MASK01 + P:C_MASK01 + 256] = before
    c[:, C_CAP:C_CAP + P] = NEG
    c[:, C_CAP + P:C_CAP + 256] = np.where(before, -NEG, NEG)
    key = np.arange(256)
    for qi in range(2):
        c[:, C_NEG + 256 * qi:C_NEG + 256 * (qi + 1)] = np.where(key[None, :] <= i[:, None] + P * qi, 0.0, NEG)
    for h in range(12):
        c[h::32, C_HEAD + h] = 1.0
    half = 16
    inv = (np.float32(10000.0) ** (-np.arange(half, dtype=np.float32) / half)).astype(np.float32)
    c[64:, C_INV] = np.tile(inv, 4)
    c[64:96, C_OFF], c[64:96, C_SHIFT] = 0.25, np.pi / 2
    c[96:112, C_SIGN], c[112:, C_SIGN] = -1.0, 1.0
    c[:, C_EPS] = EPS
    return c


def kernel(**inputs):
    from concourse import bacc
    from concourse.bass_utils import run_bass_kernel_spmd

    a = {name: np.asarray(value) for name, value in inputs.items()}
    arrays = {
        "wall": weight_stream(a["w_in"][0], a["w_attn_out"][0], a["w_conv_out"][0], a["w_o"][0], a["w_up"][0],
                              a["w_down"][0], a["w_ple_gate"][0], a["w_ple_proj"][0], a["w_mem_kv_2"], a["w_out_2"],
                              a["w_in_a_2"][0], a["w_q_up_a_2"][0], a["w_kv_up_a_2"][0], a["w_in_b_2"][0]),
        "vecs": vectors([(V_PRE, a["g_pre_mix"]), (V_POST, a["g_post_mix"]), (V_MLP, a["g_pre_mlp"]),
                         (V_POSTMLP, a["g_post_mlp"]), (V_PLE, a["g_ple"]), (V_PRE2, a["norm_pre_2"]),
                         (V_POST2, a["norm_post_2"]), (V_MEM, a["mem_norm_2"]), (V_QN, a["q_norm_a_2"]),
                         (V_KVN, a["kv_norm_a_2"])], a["b_gate"], a["w_conv"], a["b_f_2"][0]),
        "consts": constants(),
        "xt": np.ascontiguousarray(a["x"][0].T),
        "pt": np.ascontiguousarray(a["p"][0, 0].T),
        "memt": np.ascontiguousarray(a["mem_2"][0].T),
        "pos": np.ascontiguousarray(a["positions_2"][0]),
    }
    nc = bacc.Bacc("TRN2", target_bir_lowering=False, num_devices=1)
    args = [nc.dram_tensor(n, v.shape, mybir.dt.from_np(v.dtype), kind="ExternalInput").ap() for n, v in arrays.items()]
    args.append(nc.dram_tensor("spill_x", [P, KT, S], F32).ap())
    args.append(nc.dram_tensor("spill_out", [KT, P, S], F32).ap())
    args.append(nc.dram_tensor("out_t", [D, S], F32, kind="ExternalOutput").ap())
    program(nc, *args)
    r = run_bass_kernel_spmd(nc, [arrays], core_ids=[0])
    return np.ascontiguousarray(r.results[0]["out_t"].T)[None]
```

```python
from contextlib import ExitStack

import numpy as np

import concourse.bass as bass
from concourse import mybir

F32 = mybir.dt.float32
F32R = mybir.dt.float32r
I32 = mybir.dt.int32
ALU = mybir.AluOpType
ACT = mybir.ActivationFunctionType
AX = mybir.AxisListType

P = 128
S = 1024
D = 1024
KT = D // P
HALF = 512
N_MEM = 256
EPS = 1e-6
SB_PAIRS = 4
CONV_TILES = 4
FF = 4 * D
FF_CHUNK = 256
MLA_HEADS = 12
FOX_PAIRS = 6
MAIN_TILES = 6
SCALE_64 = 64.0 ** -0.5
SCALE_MLA = 96.0 ** -0.5
NEG = -float(2.0 ** 100)
UNIT = 4096
UNITS = 27

C_ID, C_ONE, C_TRI, C_REST = 0, 128, 256, 384
C_MASK01, C_CAP, C_NEG = 512, 768, 1024
C_HEAD = 1536
C_INV, C_OFF, C_SIGN, C_SHIFT = 1548, 1549, 1550, 1551
C_EPS = 1552
N_CONST = 1554

V_PRE, V_POST, V_MLP, V_POSTMLP, V_PLE = 0, 8, 16, 24, 32
V_PRE2, V_POST2, V_MEM = 40, 56, 72
V_QN, V_KVN = 80, 83
V_BGA, V_BGC = 85, 93
V_CONV = 101
V_BF = 113
N_VEC = 114

N_SLABS = {"sb": 3 * SB_PAIRS, "conv": 3 * CONV_TILES, "mix": 3 * KT, "wo": KT,
           "mlp": 4 * (FF // FF_CHUNK), "ple": 2 + KT, "mem": 8,
           "a_in": 2 + 3 + 2 + 1, "mla": MLA_HEADS, "a_gate": KT, "a_out": KT,
           "b_in": 3, "fox": 3 * FOX_PAIRS, "b_gate": KT, "b_out": KT}
TOTAL_SLABS = sum(N_SLABS.values())


class Tally:

    def __init__(self):
        self.counts = {}

    def now(self, what):
        return self.counts.get(what if isinstance(what, str) else id(what), 0)

    def take(self, what, k=1):
        before = self.now(what)
        self.counts[what if isinstance(what, str) else id(what)] = before + k
        return before

    def next(self, what, k=1):
        return self.take(what, k) + k


def program(nc, wall, vecs, consts, xt, pt, memt, pos, spill_x, spill_out, spill_gate, out):
    ctx = ExitStack()

    def sb(name, shape, dt):
        return ctx.enter_context(nc.sbuf_tensor(name, shape, dt))

    def sem(name):
        return ctx.enter_context(nc.semaphore(name))

    con = sb("con", [P, N_CONST], F32)
    vec = sb("vec", [P, N_VEC], F32)
    tri_r = sb("tri_r", [P, P], F32R)
    rest_r = sb("rest_r", [P, P], F32R)
    id_r = sb("id_r", [P, P], F32R)
    neg_r = sb("neg_r", [P, 2, 256], F32R)
    zero_r = sb("zero_r", [P, P], F32R)
    neg_flat = neg_r[:, :, :].rearrange("p a b -> p (a b)")
    raw = sb("raw", [P, 2, KT, P], F32)
    wh = sb("wh", [P, 2, KT, P], F32R)
    wl = sb("wl", [P, 2, KT, P], F32R)
    with nc.sbuf_tensor("xold_t", [P, KT, S], F32) as xold_t, nc.sbuf_tensor("z_t", [P, KT, S], F32) as z_t:
        pass
    with ExitStack() as second:
        qa2_h, qa2_l, ka2_h, ka2_l = (second.enter_context(nc.sbuf_tensor(n, [P, S], F32R))
                                      for n in ("qa2_h", "qa2_l", "ka2_h", "ka2_l"))
        va2_h, va2_l = (second.enter_context(nc.sbuf_tensor(n, [P, 8, 64], F32R)) for n in ("va2_h", "va2_l"))
    hh = sb("hh", [P, KT, S], F32R)
    hl = sb("hl", [P, KT, S], F32R)
    small = sb("small", [P, 64], F32)
    rt, rs = small[:, 0:8], small[:, 8:16]
    mx, nm, rsum, rinv = (small[:, a:a + 4] for a in (16, 20, 24, 28))
    region = nc.sbuf_base

    def at(unit, name, shape, dt, extra=0):
        with ExitStack() as s:
            if unit or extra:
                s.enter_context(nc.sbuf_tensor(name + "_below", [P, unit * UNIT // 4 + extra // 4], F32))
            t = s.enter_context(nc.sbuf_tensor(name, shape, dt))
        return t

    assert region + UNITS * UNIT <= nc.sbuf_usable_end, (region, nc.sbuf_usable_end)
    gate_t = z_t
    ident, ones = con[:, C_ID:C_ID + P], con[:, C_ONE:C_ONE + P]

    x_t = at(0, "x_t", [P, KT, S], F32)
    y_t = at(8, "y_t", [P, KT, S], F32)
    sq = [at(22 + i, f"sq{i}", [P, S], F32) for i in range(2)]
    nt = [at(24 + i, f"nt{i}", [P, S], F32) for i in range(2)]
    acc = at(26, "acc", [P, S], F32)
    o_h, o_l = at(0, "o_h", [P, 4, S], F32R), at(4, "o_l", [P, 4, S], F32R)
    qp_h, qp_l = at(8, "qp_h", [P, 2, S], F32R), at(10, "qp_l", [P, 2, S], F32R)
    k_h, k_l = at(12, "k_h", [P, S], F32R), at(13, "k_l", [P, S], F32R)
    vp_h, vp_l = at(14, "vp_h", [P, 2, 8, P], F32R), at(16, "vp_l", [P, 2, 8, P], F32R)
    zb = [at(18 + i, f"zb{i}", [P, 2, HALF], F32) for i in range(2)]
    eb = at(20, "eb", [P, 2, HALF], F32)
    vt = at(20, "vt", [P, S], F32)
    sp_h = [at(21 + i, f"sp_h{i}", [P, 2, HALF], F32R) for i in range(2)]
    sp_l = [at(23 + i, f"sp_l{i}", [P, 2, HALF], F32R) for i in range(2)]
    pw_h, pw_l = at(25, "pw_h", [P, 2, HALF], F32R), at(26, "pw_l", [P, 2, HALF], F32R)
    c_h, c_l = at(8, "c_h", [P, 4, S], F32R), at(12, "c_l", [P, 4, S], F32R)
    cc = at(16, "cc", [P, S], F32)
    cu = at(17, "cu", [P, 2 + S], F32)
    cv = at(19, "cv", [P, S], F32)
    mix_t = at(16, "mix_t", [P, KT, S], F32)
    ga, gc = at(24, "ga", [P, S], F32), at(25, "gc", [P, S], F32)
    f_h = [at(16 + 2 * i, f"f_h{i}", [P, 2, S], F32R) for i in range(2)]
    f_l = [at(20 + 2 * i, f"f_l{i}", [P, 2, S], F32R) for i in range(2)]
    fr, ff = at(24, "fr", [P, S], F32), at(25, "ff", [P, S], F32)
    p_t = at(16, "p_t", [P, 2, S], F32)
    p_h, p_l = at(18, "p_h", [P, 2, S], F32R), at(20, "p_l", [P, 2, S], F32R)
    pg = at(22, "pg", [P, S], F32)
    m_t = at(8, "m_t", [P, KT, N_MEM], F32)
    m_h, m_l = at(10, "m_h", [P, KT, N_MEM], F32R), at(12, "m_l", [P, KT, N_MEM], F32R)
    mv = at(14, "mv", [P, N_MEM], F32)
    km_h = [at(18 + 2 * i, f"km_h{i}", [P, 2, N_MEM], F32R) for i in range(2)]
    km_l = [at(18 + 2 * i, f"km_l{i}", [P, 2, N_MEM], F32R, 2048) for i in range(2)]
    vm_h = [at(19 + 2 * i, f"vm_h{i}", [P, 2, 2 * P], F32R) for i in range(2)]
    vm_l = [at(19 + 2 * i, f"vm_l{i}", [P, 2, 2 * P], F32R, 2048) for i in range(2)]
    prob = [[at(16, "prob00", [P, S], F32), at(17, "prob01", [P, S], F32)],
            [at(22, "prob10", [P, S], F32), at(23, "prob11", [P, S], F32)]]
    pt_h = [at(24 + i, f"pt_h{i}", [P, HALF], F32R) for i in range(2)]
    pt_l = [at(24 + i, f"pt_l{i}", [P, HALF], F32R, 2048) for i in range(2)]
    ot = at(26, "ot", [P, S], F32)
    cq_h, cq_l = at(0, "cq_h", [P, 3, S], F32R), at(3, "cq_l", [P, 3, S], F32R)
    ckv_h, ckv_l = at(6, "ckv_h", [P, 2, S], F32R), at(13, "ckv_l", [P, 2, S], F32R)
    cq_t, ckv_t = at(8, "cq_t", [P, 3, S], F32), at(11, "ckv_t", [P, 2, S], F32)
    qa_h, qa_l = at(8, "qa_h", [P, S], F32R), at(9, "qa_l", [P, S], F32R)
    ka_h, ka_l = at(10, "ka_h", [P, S], F32R), at(11, "ka_l", [P, S], F32R)
    kvf = at(12, "kvf", [P, S], F32)
    va_h, va_l = at(15, "va_h", [P, 8, 64], F32R), at(15, "va_l", [P, 8, 64], F32R, 2048)
    qa, ka, va = ((qa_h, qa_l), (qa2_h, qa2_l)), ((ka_h, ka_l), (ka2_h, ka2_l)), ((va_h, va_l), (va2_h, va2_l))
    trig = at(18, "trig", [P, S], F32)
    qf = at(19, "qf", [P, S], F32)
    ang = [at(22 + i, f"ang{i}", [P, S], F32) for i in range(3)]
    posi = at(25, "posi", [P, S], I32)
    qf_pad = ((qp_h, qp_l), (at(12, "qp2_h", [P, 2, S], F32R), at(14, "qp2_l", [P, 2, S], F32R)))
    kf = [(at(4 + 2 * i, f"kf_h{i}", [P, S], F32R), at(5 + 2 * i, f"kf_l{i}", [P, S], F32R)) for i in range(2)]
    vf = [(at(18 + 2 * i, f"vf_h{i}", [P, 8, P], F32R), at(19 + 2 * i, f"vf_l{i}", [P, 8, P], F32R)) for i in range(2)]
    fvt = at(0, "fvt", [P, S], F32)
    a_base, a_head, b_all = at(1, "a_base", [P, S], F32), at(2, "a_head", [P, S], F32R), at(3, "b_all", [P, S], F32R)
    fx, fe, fone = at(12, "fx", [P, S], F32), at(13, "fe", [P, S], F32), at(14, "fone", [P, S], F32)
    y_h, y_l = at(0, "y_h", [P, KT, S], F32R), at(8, "y_l", [P, KT, S], F32R)
    gt = [at(16 + i, f"gt{i}", [P, S], F32) for i in range(2)]
    go = [at(22 + i, f"go{i}", [P, S], F32) for i in range(4)]
    ps = ctx.enter_context(nc.psum_tensor("ps", [P, 2, S], F32))
    aux = ctx.enter_context(nc.psum_tensor("aux", [P, 2, HALF], F32))
    ob = ctx.enter_context(nc.psum_tensor("ob", [P, 2, HALF], F32))

    init_in, x_in, p_in, m_in, pos_in, xold_in = map(sem, ("init_in", "x_in", "p_in", "m_in", "pos_in", "xold_in"))
    raw_in, out_in = [sem(f"raw_in{i}") for i in range(2)], [sem(f"out_in{i}") for i in range(4)]
    ot_out, spill_done, end_out = map(sem, ("ot_out", "spill_done", "end_out"))
    w_high, w_split, slab_begun, work_done = map(sem, ("w_high", "w_split", "slab_begun", "work_done"))
    work_free = [sem(f"work_free{i}") for i in range(2)]
    act_end, dve_end, act_chain, dve_chain = map(sem, ("act_end", "dve_end", "act_chain", "dve_chain"))
    const_ready = sem("const_ready")
    high_ready, tile_ready, tile_split = map(sem, ("high_ready", "tile_ready", "tile_split"))
    sq_ready, sq_used, rt_ready, diag_ready = map(sem, ("sq_ready", "sq_used", "rt_ready", "diag_ready"))
    nt_ready, nh_ready, norm_ready = map(sem, ("nt_ready", "nh_ready", "norm_ready"))
    upd_ready, final_ready = map(sem, ("upd_ready", "final_ready"))
    ln_ready, sp_ready, sph_ready, spl_ready = map(sem, ("ln_ready", "sp_ready", "sph_ready", "spl_ready"))
    tri_done, d_ready, pwh_ready, pwl_ready = map(sem, ("tri_done", "d_ready", "pwh_ready", "pwl_ready"))
    av_done, oh_ready, o_ready = map(sem, ("av_done", "oh_ready", "o_ready"))
    nm_ready, p_ready, pn_ready, pt_done = map(sem, ("nm_ready", "p_ready", "pn_ready", "pt_done"))
    pth_ready, ptl_ready, oa_done, oa_taken = map(sem, ("pth_ready", "ptl_ready", "oa_done", "oa_taken"))
    table_ready, sin_ready, qn_ready, rope_ready = map(sem, ("table_ready", "sin_ready", "qn_ready", "rope_ready"))
    ahead_ready, fox_ready = map(sem, ("ahead_ready", "fox_ready"))
    gate_out, gate_in = [sem(f"gate_out{i}") for i in range(2)], sem("gate_in")
    block = ctx.enter_context(nc.Block())

    def barrier(eng, t, me):
        eng.drain().then_inc(me, 1)
        n = t.next("end")
        eng.wait_ge(act_end, n)
        eng.wait_ge(dve_end, n)

    SB_UNITS = []
    for chunk in range(2):
        for kb in range(4 * chunk + 3, -1, -1):
            first = min(max(kb * P - chunk * HALF, 0), HALF - 256)
            SB_UNITS.append((chunk, kb, first, HALF - first))
    NU = len(SB_UNITS)
    def attention_steps(heads, pieces):
        table, group = pieces
        steps = []
        for n in range(4 * heads + 1):
            h, c = divmod(n, 4)
            following = h // group + 1
            piece = table.get((h % group, c)) if following * group < heads else None
            steps.append((n if n < 4 * heads else None, n - 1 if n > 0 else None, piece, following))
        return steps

    MEMORY = ({(1, 0): "q"}, 2)
    LATENT = ({(0, 0): "q", (0, 1): "kv", (0, 2): "vt"}, 1)
    FOX = ({(0, 0): "q", (0, 1): "k", (1, 0): "v", (1, 1): "vt"}, 2)

    def widths(keys):
        return [(0, min(keys, HALF))] + ([(HALF, keys)] if keys > HALF else [])

    @block.sync
    def _(sp):
        sp.dma_start(con[:], consts).then_inc(init_in, 16)
        sp.dma_start(vec[:], vecs).then_inc(init_in, 16)
        for k in range(KT):
            sp.dma_start(x_t[:, k, :], xt[k * P:(k + 1) * P, :]).then_inc(x_in, 16)
        for s in range(2):
            sp.dma_start(raw[:, s, :, :], wall[s]).then_inc(raw_in[s], 16)

        with sp.Fori(1, TOTAL_SLABS // 2) as i:
            for s in range(2):
                sp.wait_ge(w_split, 2 * i + s - 1)
                sp.dma_start(raw[:, s, :, :], wall[bass.ds(2 * i + s, 1)].rearrange("a p k m -> (a p) k m")).then_inc(raw_in[s], 16)

        if TOTAL_SLABS % 2:
            sp.wait_ge(w_split, TOTAL_SLABS - 2)
            sp.dma_start(raw[:, 0, :, :], wall[TOTAL_SLABS - 1]).then_inc(raw_in[0], 16)
        for k in range(KT):
            sp.wait_ge(final_ready, k + 1)
            sp.dma_start(out[k * P:(k + 1) * P, :], x_t[:, k, :]).then_inc(end_out, 16)
        sp.wait_ge(end_out, 16 * KT)

    @block.gpsimd
    def _(pool):
        def split(s, slab_words):
            loaded, begun, high = slab_words
            pool.wait_ge(raw_in[s], loaded)
            if begun is not None:
                pool.wait_ge(slab_begun, begun)
            pool.tensor_tensor(wh[:, s, :, :], raw[:, s, :, :], ones.unsqueeze(1).broadcast_to([P, KT, P]), ALU.mult).then_inc(w_high, 1)
            pool.wait_ge(w_high, high)
            pool.tensor_tensor(wl[:, s, :, :], raw[:, s, :, :], wh[:, s, :, :].bitcast(F32), ALU.subtract).then_inc(w_split, 1)

        for s in range(2):
            split(s, (16, None, s + 1))
        with pool.Fori(1, TOTAL_SLABS // 2) as i:
            for s in range(2):
                split(s, (16 * i + 16, 2 * i + s, 2 * i + s + 1))
        if TOTAL_SLABS % 2:
            last = TOTAL_SLABS - 1
            split(0, (8 * last + 16, last, last + 1))

    @block.tensor
    def _(pe):
        t = Tally()

        def work():
            w = t.take("work")
            if w >= 2:
                pe.wait_ge(work_free[w % 2], w // 2)
            return w, w % 2

        def evacuated(w):
            pe.wait_ge(work_free[w % 2], w // 2 + 1)

        def slab():
            s = t.take("slab")
            pe.wait_ge(w_split, s + 1)
            t.fresh = True
            return s % 2

        def proj(w, sl, ks, rh, rl, n=S, ready=None):
            halves = [(a, min(a + HALF, n)) for a in range(0, n, HALF)]
            for i, k in enumerate(ks):
                if ready:
                    ready(i)
                for j, (lw, r) in enumerate(((wh, rh), (wh, rl), (wl, rh))):
                    for a, b in halves:
                        m = pe.matmul(ps[:, w, a:b], lw[:, sl, k, :], r[:, i, a:b],
                                      start=(i == 0 and j == 0), stop=(i == len(ks) - 1 and j == 2))
                        if t.fresh:
                            m.then_inc(slab_begun, 1)
                            t.fresh = False
            m.then_inc(work_done, 1)

        def product(ks, rh, rl, n=S, ready=None, sl=None):
            sl = slab() if sl is None else sl
            w, slot = work()
            proj(slot, sl, ks, rh, rl, n, ready)
            return w

        def transposes(src, n):
            w, slot = work()
            for j in range(n):
                m = pe.transpose(ps[:, slot, j * P:(j + 1) * P], src[:, j * P:(j + 1) * P], ident)
            m.then_inc(work_done, 1)
            return w

        def norm_stats(ktiles, n):
            pe.wait_ge(sq_used, t.next(sq_used, ktiles))
            w, slot = work()
            for j in range(n // P):
                m = pe.matmul(ps[:, slot, j:j + 1], acc[:, j * P:(j + 1) * P], ones[:, 0:1], start=True, stop=True)
            m.then_inc(work_done, 1)
            pe.wait_ge(diag_ready, t.next(diag_ready))
            w, slot = work()
            for a in range(0, n, HALF):
                b = min(a + HALF, n)
                m = pe.matmul(ps[:, slot, a:b], ones, sq[0][:, a:b], start=True, stop=True)
            m.then_inc(work_done, 1)

        def norm_tiles(ktiles):
            base = t.take(norm_ready, ktiles)
            return lambda i: pe.wait_ge(norm_ready, base + i + 1)

        pe.wait_ge(init_in, 32)
        norm_stats(KT, S)
        ready = norm_tiles(KT)

        pe.wait_ge(const_ready, 1)
        for pair in range(SB_PAIRS):
            for _ in range(2):
                product(range(KT), hh, hl, ready=ready)
                ready = None
            w = product(range(KT), hh, hl)
            evacuated(w)
            w = transposes(vt, 8)
            evacuated(w)

            def z_unit(u):
                chunk, kb, first, n = SB_UNITS[u]
                w, slot = work()
                for h in range(2):
                    for j, (l, r) in enumerate(((k_h, qp_h), (k_l, qp_h), (k_h, qp_l))):
                        q0 = chunk * HALF + first
                        m = pe.matmul(ps[:, slot, h * HALF:h * HALF + n], l[:, kb * P:(kb + 1) * P],
                                      r[:, h, q0:q0 + n], start=(j == 0), stop=(j == 2))
                m.then_inc(work_done, 1)

            def suffix(u, tri):
                chunk, kb, first, n = SB_UNITS[u]
                for h in range(2):
                    for r in (sp_h[u % 2], sp_l[u % 2]):
                        m = pe.matmul(aux[:, h, first:first + n], tri[:, :], r[:, h, 0:n],
                                      start=False, stop=True, skip_group_check=True)
                return m

            def clear_sums():
                for h in range(2):
                    pe.matmul(aux[:, h, :], zero_r[:, :], neg_flat, start=True, stop=True, skip_group_check=True)

            def av(u):
                chunk, kb, first, n = SB_UNITS[u]
                pe.wait_ge(pwl_ready, t.next(pwl_ready))
                o = t.o_chunk % 2
                if kb == 4 * chunk + 3:
                    if t.o_chunk >= 2:
                        pe.wait_ge(o_ready, t.o_chunk - 1)
                    pe.matmul(ob[:, o, :], zero_r[:, :], neg_flat, start=True, stop=True, skip_group_check=True)
                for h in range(2):
                    for l, r in ((vp_h, pw_h), (vp_l, pw_h), (vp_h, pw_l)):
                        m = pe.matmul(ob[:, o, first:first + n], l[:, h, kb, :], r[:, h, 0:n],
                                      start=False, stop=True, skip_group_check=True)
                m.then_inc(av_done, 1)
                if kb == 0:
                    t.o_chunk += 1

            if pair == 0:
                t.o_chunk = 0
            z_unit(0)
            for u in range(NU + 1):
                if u + 1 < NU:
                    z_unit(u + 1)
                if u > 0:
                    pe.wait_ge(d_ready, t.next(d_ready))
                if u < NU:
                    if SB_UNITS[u][1] == 4 * SB_UNITS[u][0] + 3:
                        clear_sums()
                    else:
                        suffix(u - 1, rest_r)
                    pe.wait_ge(spl_ready, t.next(spl_ready))
                    suffix(u, tri_r).then_inc(tri_done, 1)
                if u > 0:
                    av(u - 1)

        for j in range(CONV_TILES):
            for _ in range(3):
                product(range(KT), hh, hl)

        for m in range(KT):
            product(range(KT), hh, hl)
            product(range(KT), hh, hl)
            sl = slab()
            product(range(4), o_h, o_l, sl=sl, ready=(lambda i: pe.wait_ge(o_ready, 2 * SB_PAIRS)) if m == 0 else None)
            product(range(4, 8), c_h, c_l, sl=sl,
                    ready=(lambda i: pe.wait_ge(tile_split, CONV_TILES)) if m == 0 else None)
        t.take(tile_split, CONV_TILES)

        def from_split(ktiles):
            base = t.take(tile_split, ktiles)
            return lambda i: pe.wait_ge(tile_split, base + i + 1)

        ready = from_split(KT)
        for m in range(KT):
            product(range(KT), hh, hl, ready=ready if m == 0 else None)

        norm_stats(KT, S)
        norm_stats(KT, S)
        ready = norm_tiles(KT)
        nch = FF // FF_CHUNK
        for c in range(nch + 1):
            if c < nch:
                for j in range(2):
                    product(range(KT), hh, hl, ready=ready)
                    ready = None
            if c > 0:
                b = t.take(tile_split, 2)
                for q in range(2):
                    sl = slab()
                    for m in range(4):
                        product([2 * m, 2 * m + 1], f_h[(c - 1) % 2], f_l[(c - 1) % 2], sl=sl,
                                ready=(lambda i: pe.wait_ge(tile_split, b + i + 1)) if q == m == 0 else None)

        norm_stats(KT, S)
        norm_stats(KT, S)
        nready = norm_tiles(KT)
        ready = from_split(2)
        for q in range(2):
            sl = slab()
            for m in range(4):
                product([2 * m, 2 * m + 1], p_h, p_l, sl=sl, ready=ready)
                ready = None
        for m in range(KT):
            product(range(KT), hh, hl, ready=nready)
            nready = None

        norm_stats(KT, N_MEM)
        ready = norm_tiles(KT)
        for layer in range(2):
            for j in range(2):
                product(range(KT), m_h, m_l, n=N_MEM, ready=ready)
                ready = None
            for j in range(2):
                w = product(range(KT), m_h, m_l, n=N_MEM)
                evacuated(w)
                transposes(mv, 2)

        norm_stats(KT, S)
        ready = norm_tiles(KT)

        def attend(heads, pieces, project, q_of, k_of, v_of, rows, keys_of, causal, bias=None):
            def scores(n, qi):
                h, c = divmod(n, 4)
                keys = keys_of(c)
                w, slot = work()
                q0 = c * 256 + qi * P
                q, k = q_of(h), k_of(h)
                parts = [(q[0], k[0], rows), (q[0], k[1], rows), (q[1], k[0], rows)]
                parts = [(l[0:rows, q0:q0 + P], r, n_rows) for l, r, n_rows in parts]
                if bias:
                    if qi == 0:
                        pe.wait_ge(ahead_ready, t.next(ahead_ready))
                    parts.append((bias[0][:, q0:q0 + P], bias[1], P))
                for a, b in widths(keys):
                    masked = causal and b == keys
                    for j, (l, r, n_rows) in enumerate(parts):
                        m = pe.matmul(ps[:, slot, a:b], l, r[0:n_rows, a:b], start=(j == 0),
                                      stop=(j == len(parts) - 1 and not masked), skip_group_check=True)
                    if masked:
                        m = pe.matmul(ps[:, slot, b - 256:b], id_r[:, :], neg_r[:, qi, :], start=False, stop=True,
                                      skip_group_check=True)
                m.then_inc(work_done, 1)

            def turn(n, j):
                if j == 0:
                    pe.wait_ge(pn_ready, t.next(pn_ready, 2))
                g = t.take("pt")
                if g >= 2:
                    pe.wait_ge(ptl_ready, g - 1)
                for kbl in range(2):
                    for qi in range(2):
                        kb = 2 * j + kbl
                        m = pe.transpose(aux[:, g % 2, kbl * 256 + qi * P:kbl * 256 + (qi + 1) * P],
                                         prob[n % 2][qi][:, kb * P:(kb + 1) * P], ident)
                m.then_inc(pt_done, 1)
                return g

            def values(n, g, j):
                h, c = divmod(n, 4)
                o = t.now("oa")
                if j == 0:
                    if o >= 2:
                        pe.wait_ge(oa_taken, o - 1)
                pe.wait_ge(ptl_ready, g + 1)
                last = j == keys_of(c) // 256 - 1
                for kbl in range(2):
                    kb = 2 * j + kbl
                    for i, (l, r) in enumerate(((0, pt_h), (1, pt_h), (0, pt_l))):
                        m = pe.matmul(ob[0:64, o % 2, 0:256], v_of(h, kb)[l], r[g % 2][:, kbl * 256:(kbl + 1) * 256],
                                      start=(kb == 0 and i == 0), stop=(last and kbl == 1 and i == 2), skip_group_check=True)
                if last:
                    t.take("oa")
                    m.then_inc(oa_done, 1)

            for now, before, piece, following in attention_steps(heads, pieces):
                groups = keys_of(before % 4) // 256 if before is not None else 0
                turned = []
                if now == 0:
                    for w in (t.now("work") - 1, t.now("work") - 2):
                        evacuated(w)
                for i in range(2):
                    if now is not None:
                        scores(now, i)
                    if i < groups:
                        turned.append(turn(before, i))
                for j in range(groups):
                    values(before, turned[j], j)
                    if j + 2 < groups:
                        turned.append(turn(before, j + 2))
                if piece:
                    project(piece, following)

        def memory_attention(layer, ready):
            product(range(KT), hh, hl, ready=ready)
            attend(4, MEMORY, lambda piece, pair: product(range(KT), hh, hl),
                   lambda h: [q[:, h % 2, :] for q in qf_pad[h // 2]], lambda h: (km_h[layer][:, h // 2, :], km_l[layer][:, h // 2, :]),
                   lambda h, kb: (vm_h[layer][:, kb, h * 64:h * 64 + 64], vm_l[layer][:, kb, h * 64:h * 64 + 64]),
                   P, lambda c: N_MEM, False)

        def gates():
            for m in range(KT):
                product(range(KT), hh, hl)

        def output():
            ready = from_split(KT)
            for m in range(KT):
                product(range(KT), y_h, y_l, ready=ready if m == 0 else None)
            norm_stats(KT, S)

        memory_attention(0, ready)
        for _ in range(5):
            product(range(KT), hh, hl)
        gates()
        product(range(KT), hh, hl)
        norm_stats(3, S)
        readyq = norm_tiles(3)
        norm_stats(2, S)
        readykv = norm_tiles(2)
        state = {}

        def latent_piece(piece, h):
            if piece == "q":
                state["slab"] = slab()
                product(range(3), cq_h, cq_l, sl=state["slab"], ready=readyq if h == 0 else None)
            elif piece == "kv":
                state["kv"] = product(range(3, 5), ckv_h, ckv_l, sl=state["slab"], ready=readykv if h == 0 else None)
            else:
                evacuated(state["kv"])
                transposes(kvf, 8)

        for piece in ("q", "kv", "vt"):
            latent_piece(piece, 0)
        evacuated(t.now("work") - 1)
        attend(MLA_HEADS, LATENT, latent_piece, lambda h: qa[h % 2], lambda h: ka[h % 2],
               lambda h, kb: [v[:, kb, :] for v in va[h % 2]], 96, lambda c: (c + 1) * 256, True)
        output()

        norm_stats(KT, S)
        ready = norm_tiles(KT)
        memory_attention(1, ready)
        product(range(KT), hh, hl)

        def fox_piece(piece, pair):
            if piece == "vt":
                evacuated(state["v"])
                transposes(fvt, 8)
            else:
                state[piece] = product(range(KT), hh, hl)

        for piece in ("q", "k", "v", "vt"):
            fox_piece(piece, 0)
        attend(2 * FOX_PAIRS, FOX, fox_piece, lambda h: [q[:, h % 2, :] for q in qf_pad[h // 2 % 2]], lambda h: kf[h // 2 % 2],
               lambda h, kb: [v[:, kb, h % 2 * 64:h % 2 * 64 + 64] for v in vf[h // 2 % 2]],
               P, lambda c: (c + 1) * 256, True, (a_head, b_all))
        gates()
        output()
        assert t.now("slab") == TOTAL_SLABS, (t.now("slab"), TOTAL_SLABS)

    vcol = lambda c, rows=slice(0, P): vec[rows, c:c + 1]
    ccol = lambda c, rows=slice(0, P): con[rows, c:c + 1]
    LO, HI = slice(0, 64), slice(64, P)

    @block.scalar
    def _(act):
        t = Tally()

        def work():
            w = t.take("work")
            act.wait_ge(work_done, w + 1)
            return w, w % 2

        def skip(n=1):
            t.take("work", n)

        def evacuated(w):
            act.wait_ge(work_free[w % 2], w // 2 + 1)

        def chain(ins):
            ins.then_inc(act_chain, 1)
            act.wait_ge(act_chain, t.next(act_chain))

        def copy(out_, in_, scale=1.0):
            return act.activation(out_, in_, ACT.Copy, scale=scale)

        def take_out(dst, func=ACT.Copy, n=S, **kw):
            w, slot = work()
            act.activation(dst, ps[:, slot, 0:n], func, **kw).then_inc(work_free[slot], 1)
            return w

        def norm_stats(src, ktiles, n, d, ready=None):
            base = t.take(sq_used, ktiles)
            for k in range(ktiles):
                if ready:
                    ready(k)
                if k >= 2:
                    act.wait_ge(sq_used, base + k - 1)
                act.activation(sq[k % 2][:, 0:n], src[:, k, :], ACT.Square).then_inc(sq_ready, 1)
            w, slot = work()
            act.activation(rt[:, 0:n // P], ps[:, slot, 0:n // P], ACT.Sqrt, bias=ccol(C_EPS), scale=1.0 / d).then_inc(rt_ready, 1)
            skip()

        def norm_tiles(ktiles, n, dst):
            for k in range(ktiles):
                act.wait_ge(nt_ready, t.next(nt_ready))
                copy(dst[:, k, :], nt[k % 2][:, 0:n]).then_inc(nh_ready, 1)

        def updated():
            base = t.take(upd_ready, KT)
            return lambda i: act.wait_ge(upd_ready, base + i + 1)

        def q_pair(q=qp_h):
            w, slot = work()
            copy(q[LO, 0, :], ps[LO, slot, :], SCALE_64)
            copy(q[HI, 1, :], ps[HI, slot, :], SCALE_64).then_inc(high_ready, 1)

        act.wait_ge(init_in, 32)
        act.wait_ge(x_in, 16 * KT)
        norm_stats(x_t, KT, S, D)
        norm_tiles(KT, S, hh)

        act.preload_act_table_set("natural_log_exp_and_others")
        for pair in range(SB_PAIRS):
            q_pair()
            w, slot = work()
            copy(k_h[:, :], ps[:, slot, :]).then_inc(high_ready, 1)
            take_out(vt[:, :])
            w, slot = work()
            tiles = ps[:, slot, :].rearrange("p (k f) -> p k f", k=8)
            copy(vp_h[:, 0, :, 0:64], tiles[:, :, 0:64])
            copy(vp_h[:, 1, :, 64:P], tiles[:, :, 64:P]).then_inc(high_ready, 1)
            d_base, spl_base, av_base = t.take(d_ready, NU), t.take(spl_ready, NU), t.take(av_done, NU)
            for u in range(NU + 2):
                if u < NU:
                    n = SB_UNITS[u][3]
                    w = t.take("work")
                    evacuated(w)
                    if spl_base + u > 0:
                        act.wait_ge(spl_ready, spl_base + u)
                    z, e = zb[u % 2][:, :, 0:n], eb[:, :, 0:n]
                    chain(act.activation(e, z, ACT.Abs))
                    chain(act.activation(e, e, ACT.Exp, scale=-1.0))
                if 0 < u <= NU:
                    nb = SB_UNITS[u - 1][3]
                    zp = zb[(u - 1) % 2][:, :, 0:nb]
                    act.wait_ge(d_ready, d_base + u)
                    act.activation(zp, zp, ACT.Exp).then_inc(act_chain, 1)
                    exp_done = t.next(act_chain)
                if u < NU:
                    act.activation(e, e, ACT.Ln, bias=ccol(C_ONE), scale=1.0).then_inc(ln_ready, 1)
                if 0 < u <= NU:
                    act.wait_ge(act_chain, exp_done)
                    if av_base + u > 1:
                        act.wait_ge(av_done, av_base + u - 1)
                    copy(pw_h[:, :, 0:nb], zp).then_inc(pwh_ready, 1)
                if u < NU:
                    act.wait_ge(sp_ready, t.next(sp_ready))
                    copy(sp_h[u % 2][:, :, 0:n], e).then_inc(sph_ready, 1)
                if u >= 2 and SB_UNITS[u - 2][1] == 0:
                    o = t.take("o_chunk")
                    if av_base + u > 1:
                        act.wait_ge(av_done, av_base + u - 1)
                    c = SB_UNITS[u - 2][0]
                    copy(o_h[:, pair, c * HALF:(c + 1) * HALF], ob[:, o % 2, :]).then_inc(oh_ready, 1)

        for j in range(CONV_TILES):
            take_out(cc[:, :])
            skip()
            w = t.take("work")
            evacuated(w)
            copy(c_h[:, j, :], cv[:, :]).then_inc(high_ready, 1)

        base = t.take(tile_ready, KT)
        for m in range(KT):
            if base + m > 0:
                act.wait_ge(tile_ready, base + m)
            take_out(ga[:, :], ACT.Sigmoid, bias=vcol(V_BGA + m))
            take_out(gc[:, :], ACT.Sigmoid, bias=vcol(V_BGC + m))
            skip(2)
        act.wait_ge(work_done, t.now("work"))
        act.wait_ge(tile_ready, base + KT)
        act.dma_start(x_t[:, :, :], xt.rearrange("(k p) s -> p k s", p=P)).then_inc(xold_in, 16)
        for k in range(KT):
            copy(hh[:, k, :], mix_t[:, k, :]).then_inc(high_ready, 1)

        for m in range(KT):
            take_out(y_t[:, m, :])
        barrier(act, t, act_end)
        norm_stats(y_t, KT, S, D)
        norm_stats(x_t, KT, S, D, updated())
        norm_tiles(KT, S, hh)

        nch = FF // FF_CHUNK
        for c in range(nch + 1):
            if c < nch:
                for j in range(2):
                    take_out(fr[:, :], ACT.Relu)
                    act.wait_ge(tile_ready, t.next(tile_ready))
                    copy(f_h[c % 2][:, j, :], ff[:, :]).then_inc(high_ready, 1)
            if c == 1:
                for m in range(KT):
                    take_out(y_t[:, m, :])
            elif c > 1:
                skip(KT)
        barrier(act, t, act_end)
        act.dma_start(p_t[:, :, :], pt.rearrange("(k p) s -> p k s", p=P)).then_inc(p_in, 16)
        norm_stats(y_t, KT, S, D)
        norm_stats(x_t, KT, S, D, updated())
        norm_tiles(KT, S, hh)

        barrier(act, t, act_end)
        act.wait_ge(p_in, 16)
        for k in range(2):
            copy(p_h[:, k, :], p_t[:, k, :]).then_inc(high_ready, 1)
        for m in range(KT):
            take_out(y_t[:, m, :])
        base = t.take(tile_ready, KT)
        for m in range(KT):
            if base + m > 0:
                act.wait_ge(tile_ready, base + m)
            take_out(pg[:, :], ACT.Sigmoid)
        act.wait_ge(tile_ready, base + KT)
        spilled = [0]

        def spill():
            act.dma_start(spill_x, x_t[:, :, :]).then_inc(spill_done, 16)
            spilled[0] += 16

        spill()
        act.dma_start(m_t[:, :, :], memt.rearrange("(k p) s -> p k s", p=P)).then_inc(m_in, 16)
        barrier(act, t, act_end)
        act.wait_ge(m_in, 16)
        norm_stats(m_t, KT, N_MEM, D)
        norm_tiles(KT, N_MEM, m_h)
        for layer in range(2):
            for j in range(2):
                w, slot = work()
                copy(km_h[layer][:, j, :], ps[:, slot, 0:N_MEM]).then_inc(high_ready, 1)
            for j in range(2):
                take_out(mv[:, :], n=N_MEM)
                w, slot = work()
                copy(vm_h[layer][:, :, j * P:(j + 1) * P], ps[:, slot, 0:N_MEM].rearrange("p (k f) -> p k f", k=2)).then_inc(high_ready, 1)
        barrier(act, t, act_end)
        norm_stats(x_t, KT, S, D)
        norm_tiles(KT, S, hh)

        def attend(heads, pieces, project, keys_of, tile_of):
            def turned():
                g = t.take("pt")
                act.wait_ge(pt_done, g + 1)
                copy(pt_h[g % 2][:, :], aux[:, g % 2, :]).then_inc(pth_ready, 1)

            for now, before, piece, following in attention_steps(heads, pieces):
                groups = keys_of(before % 4) // 256 if before is not None else 0
                for i in range(2):
                    if i < groups:
                        turned()
                    if now is not None:
                        keys = keys_of(now % 4)
                        w = t.take("work")
                        j = (2 * now + i) % 4
                        act.wait_ge(nm_ready, t.next(nm_ready))
                        act.activation(prob[now % 2][i][:, 0:keys], ps[:, w % 2, 0:keys], ACT.Exp, bias=nm[:, j:j + 1],
                                       scale=1.0, accum_out=rsum[:, j:j + 1]).then_inc(work_free[w % 2], 1)
                for _ in range(2, groups):
                    turned()
                if before is not None:
                    h, c = divmod(before, 4)
                    rows = (LO, HI)[h % 2]
                    o = t.take("oa")
                    act.wait_ge(oa_done, o + 1)
                    if c == 0 and h % 2 == 0:
                        if t.now(ot_out) > 0:
                            act.wait_ge(ot_out, t.now(ot_out))
                    copy(ot[rows, c * 256:(c + 1) * 256], ob[0:64, o % 2, 0:256]).then_inc(oa_taken, 1)
                    if c == 3 and h % 2 == 1:
                        act.wait_ge(oa_taken, t.now("oa"))
                        act.dma_start(spill_out[tile_of(h // 2)], ot[:, :]).then_inc(ot_out, 16)
                        t.take(ot_out, 16)
                if piece:
                    project(piece, following)

        def memory_attention():
            q_pair(qf_pad[0][0])
            attend(4, MEMORY, lambda piece, pair: q_pair(qf_pad[pair][0]), lambda c: N_MEM, lambda pair: MAIN_TILES + pair)

        def gates_to_dram():
            for m in range(KT):
                if m >= 2:
                    act.wait_ge(gate_out[m % 2], 16 * (m // 2))
                w = take_out(gt[m % 2][:, :], ACT.Silu)
                evacuated(w)
                act.dma_start(spill_gate[m], gt[m % 2][:, :]).then_inc(gate_out[m % 2], 16)

        def gates_and_output(gates_here):
            barrier(act, t, act_end)
            if t.now(ot_out) > 0:
                act.wait_ge(ot_out, t.now(ot_out))
            base, n_out = t.take(tile_ready, KT), t.take(out_in, KT) // 4

            def fetch(m):
                act.dma_start(go[m % 4][:, :], spill_out[m]).then_inc(out_in[m % 4], 16)

            for m in range(4):
                fetch(m)
            if gates_here:
                for m in range(KT):
                    if m > 0:
                        act.wait_ge(tile_ready, base + m)
                    last = take_out(gt[m % 2][:, :], ACT.Silu)
                    if m > 0:
                        copy(y_h[:, m - 1, :], gt[(m - 1) % 2][:, :]).then_inc(high_ready, 1)
                        if m + 3 < KT:
                            fetch(m + 3)
                act.wait_ge(tile_ready, base + KT)
                copy(y_h[:, KT - 1, :], gt[(KT - 1) % 2][:, :]).then_inc(high_ready, 1)
                act.wait_ge(work_done, last + 1)
            else:
                for m in range(KT):
                    act.wait_ge(tile_ready, base + m + 1)
                    if m + 4 < KT:
                        fetch(m + 4)
                    copy(y_h[:, m, :], gate_t[:, m, :]).then_inc(high_ready, 1)
            act.wait_ge(spill_done, spilled[0])
            act.dma_start(xold_t[:, :, :], spill_x).then_inc(xold_in, 16)
            for m in range(KT):
                take_out(z_t[:, m, :])
            barrier(act, t, act_end)
            norm_stats(z_t, KT, S, D)

        barrier(act, t, act_end)
        memory_attention()
        barrier(act, t, act_end)
        act.dma_start(posi[HI, :], pos.partition_broadcast(64)).then_inc(pos_in, 16)
        for j in range(3):
            take_out(cq_t[:, j, :])
        for j in range(2):
            take_out(ckv_t[:, j, :])
        gates_to_dram()
        skip()
        act.wait_ge(table_ready, 1)
        act.activation(trig[HI, :], ang[1][HI, :], ACT.Sin).then_inc(sin_ready, 1)
        if t.now(ot_out) > 0:
            act.wait_ge(ot_out, t.now(ot_out))
        act.wait_ge(spill_done, spilled[0])
        barrier(act, t, act_end)
        norm_stats(cq_t, 3, S, 384)
        norm_tiles(3, S, cq_h)
        norm_stats(ckv_t, 2, S, 256)
        norm_tiles(2, S, ckv_h)
        barrier(act, t, act_end)
        copy(ka_h[64:96, :], qf[64:96, :])
        copy(ka2_h[64:96, :], qf[64:96, :]).then_inc(high_ready, 1)
        for i in range(2):
            act.wait_ge(gate_out[i], 16 * KT // 2)
        act.dma_start(gate_t[:, :, :], spill_gate.rearrange("k p s -> p k s")).then_inc(gate_in, 16)

        def latent_piece(piece, h):
            if piece == "q":
                w, slot = work()
                copy(qf[LO, :], ps[LO, slot, :], SCALE_MLA).then_inc(qn_ready, 1)
                act.wait_ge(rope_ready, t.next(rope_ready))
                copy(qa[h % 2][0][0:96, :], qf[0:96, :]).then_inc(high_ready, 1)
            elif piece == "kv":
                w, slot = work()
                chain(copy(kvf[:, :], ps[:, slot, :]))
                copy(ka[h % 2][0][LO, :], kvf[LO, :]).then_inc(high_ready, 1)
            else:
                w, slot = work()
                copy(va[h % 2][0][:, :, :], ps[:, slot, :].rearrange("p (k f) -> p k f", k=8)[:, :, 64:P]).then_inc(high_ready, 1)

        for piece in ("q", "kv", "vt"):
            latent_piece(piece, 0)
        attend(MLA_HEADS, LATENT, latent_piece, lambda c: (c + 1) * 256, lambda pair: pair)
        gates_and_output(False)
        ready = updated()
        norm_stats(x_t, KT, S, D, ready)
        spill()
        norm_tiles(KT, S, hh)

        barrier(act, t, act_end)
        act.wait_ge(spill_done, spilled[0])
        memory_attention()
        w, slot = work()
        act.preload_act_table_set("natural_log_exp_and_others")
        act.activation(fx[:, :], ps[:, slot, :], ACT.Identity, bias=vcol(V_BF)).then_inc(work_free[slot], 1)
        evacuated(w)
        chain(act.activation(fe[:, :], fx[:, :], ACT.Abs))
        chain(act.activation(fe[:, :], fe[:, :], ACT.Exp, scale=-1.0))
        act.activation(fe[:, :], fe[:, :], ACT.Ln, bias=ccol(C_ONE), scale=1.0).then_inc(ln_ready, 1)

        def fox_piece(piece, pair):
            if piece == "q":
                q_pair(qf_pad[pair % 2][0])
            elif piece == "k":
                w, slot = work()
                copy(kf[pair % 2][0][:, :], ps[:, slot, :]).then_inc(high_ready, 1)
            elif piece == "v":
                take_out(fvt[:, :])
            else:
                w, slot = work()
                copy(vf[pair % 2][0][:, :, :], ps[:, slot, :].rearrange("p (k f) -> p k f", k=8)).then_inc(high_ready, 1)

        act.wait_ge(fox_ready, 1)
        for piece in ("q", "k", "v", "vt"):
            fox_piece(piece, 0)
        attend(2 * FOX_PAIRS, FOX, fox_piece, lambda c: (c + 1) * 256, lambda pair: pair)
        gates_and_output(True)

    @block.vector
    def _(dve):
        t = Tally()

        def work():
            w = t.take("work")
            dve.wait_ge(work_done, w + 1)
            return w, w % 2

        def skip(n=1):
            t.take("work", n)

        def evacuated(w):
            dve.wait_ge(work_free[w % 2], w // 2 + 1)

        def link(ins):
            ins.then_inc(dve_chain, 1)
            return t.next(dve_chain)

        def chain(ins):
            dve.wait_ge(dve_chain, link(ins))

        def low(dst, src, hi):
            return dve.tensor_tensor(dst, src, hi.bitcast(F32), ALU.subtract)

        def low_out(dst, hi, slot_src, slot):
            dve.wait_ge(high_ready, t.next(high_ready))
            low(dst, slot_src, hi).then_inc(work_free[slot], 1)

        def norm_stats(ktiles, n):
            base, used = t.take(sq_ready, ktiles), t.take(sq_used, ktiles)
            for k in range(ktiles):
                dve.wait_ge(sq_ready, base + k + 1)
                if k == 0:
                    dve.tensor_copy(acc[:, 0:n], sq[0][:, 0:n]).then_inc(sq_used, 1)
                else:
                    dve.wait_ge(sq_used, used + k)
                    dve.tensor_tensor(acc[:, 0:n], acc[:, 0:n], sq[k % 2][:, 0:n], ALU.add).then_inc(sq_used, 1)
            w = t.take("work")
            dve.wait_ge(rt_ready, t.next(rt_ready))
            dve.reciprocal(rs[:, 0:n // P], rt[:, 0:n // P]).then_inc(work_free[w % 2], 1)
            evacuated(w)
            for j in range(n // P):
                i = dve.tensor_scalar(sq[0][:, j * P:(j + 1) * P], ident, rs[:, j:j + 1], None, ALU.mult)
            i.then_inc(diag_ready, 1)
            return work()

        def norm_tiles(src, ktiles, n, gain, hi, lo, slot):
            base = t.take(norm_ready, ktiles)
            for k in range(ktiles + 1):
                if k < ktiles:
                    if k >= 2:
                        dve.wait_ge(norm_ready, base + k - 1)
                    dve.scalar_tensor_tensor(out=nt[k % 2][:, 0:n], in0=src[:, k, :], scalar=vcol(gain + k),
                                                 in1=ps[:, slot, 0:n], op0=ALU.mult, op1=ALU.mult).then_inc(nt_ready, 1)
                if k > 0:
                    dve.wait_ge(nh_ready, t.next(nh_ready))
                    low(lo[:, k - 1, :], nt[(k - 1) % 2][:, 0:n], hi[:, k - 1, :]).then_inc(norm_ready, 1)
            dve.drain().then_inc(work_free[slot], 1)

        def norm(src, ktiles, n, gain, hi, lo):
            w, slot = norm_stats(ktiles, n)
            norm_tiles(src, ktiles, n, gain, hi, lo, slot)

        def update(ysrc, xsrc, dst, gain, ready=upd_ready):
            w, slot = norm_stats(KT, S)
            before = None
            for k in range(KT + 1):
                if k < KT:
                    now = link(dve.scalar_tensor_tensor(out=ysrc[:, k, :], in0=ysrc[:, k, :], scalar=vcol(gain + k),
                                                        in1=ps[:, slot, :], op0=ALU.mult, op1=ALU.mult))
                if k > 0:
                    dve.wait_ge(dve_chain, before)
                    dve.tensor_tensor(dst[:, k - 1, :], xsrc[:, k - 1, :], ysrc[:, k - 1, :], ALU.add).then_inc(ready, 1)
                before = now
            dve.drain().then_inc(work_free[slot], 1)

        def zero_pads(pads):
            for q in pads:
                dve.memset(q[HI, 0, :].bitcast(F32), 0.0)
                i = dve.memset(q[LO, 1, :].bitcast(F32), 0.0)
            return i

        def q_pair(q_high=qp_h, q_low=qp_l):
            w, slot = work()
            dve.wait_ge(high_ready, t.next(high_ready))
            for h, rows in ((0, LO), (1, HI)):
                i = dve.scalar_tensor_tensor(out=q_low[rows, h, :], in0=ps[rows, slot, :], scalar=SCALE_64,
                                             in1=q_high[rows, h, :].bitcast(F32), op0=ALU.mult, op1=ALU.subtract)
            i.then_inc(work_free[slot], 1)

        dve.wait_ge(init_in, 32)
        for dst, c in ((tri_r, C_TRI), (rest_r, C_REST), (id_r, C_ID)):
            dve.tensor_copy(dst[:, :], con[:, c:c + P])
        dve.tensor_copy(neg_flat, con[:, C_NEG:C_NEG + 512])
        dve.memset(zero_r[:, :].bitcast(F32), 0.0)
        dve.memset(vp_h[:, 0, :, 64:P].bitcast(F32), 0.0)
        dve.memset(vp_h[:, 1, :, 0:64].bitcast(F32), 0.0)
        dve.memset(vp_l[:, 0, :, 64:P].bitcast(F32), 0.0)
        dve.memset(vp_l[:, 1, :, 0:64].bitcast(F32), 0.0)
        zero_pads((qp_h, qp_l)).then_inc(const_ready, 1)
        dve.wait_ge(x_in, 16 * KT)
        norm(x_t, KT, S, V_PRE, hh, hl)

        for pair in range(SB_PAIRS):
            q_pair()
            w, slot = work()
            low_out(k_l[:, :], k_h[:, :], ps[:, slot, :], slot)
            skip()
            w, slot = work()
            dve.wait_ge(high_ready, t.next(high_ready))
            tiles = ps[:, slot, :].rearrange("p (k f) -> p k f", k=8)
            dve.tensor_tensor(vp_l[:, 0, :, 0:64], tiles[:, :, 0:64], vp_h[:, 0, :, 0:64].bitcast(F32), ALU.subtract)
            low(vp_l[:, 1, :, 64:P], tiles[:, :, 64:P], vp_h[:, 1, :, 64:P]).then_inc(work_free[slot], 1)
            pwl_base = t.take(pwl_ready, NU)
            for u in range(NU + 2):
                if 0 < u <= NU:
                    chunk, kb, first, nb = SB_UNITS[u - 1]
                    z = zb[(u - 1) % 2]
                    dve.wait_ge(tri_done, t.next(tri_done))
                    d = dve.tensor_tensor(z[:, :, 0:nb], z[:, :, 0:nb], aux[:, :, first:first + nb], ALU.subtract)
                    if kb >= 4 * chunk:
                        chain(d)
                        a, b = (0, 256) if kb == 4 * chunk + 3 else (0, P)
                        for h in range(2):
                            d = dve.tensor_tensor(z[:, h, a:b], z[:, h, a:b], con[:, C_CAP + 256 - b:C_CAP + 256], ALU.min)
                    d.then_inc(d_ready, 1)
                if u < NU:
                    chunk, kb, first, n = SB_UNITS[u]
                    w, slot = work()
                    z, e = zb[u % 2], eb
                    if pwl_base + u > 1:
                        dve.wait_ge(pwl_ready, pwl_base + u - 1)
                    zsrc = ps[:, slot, :].rearrange("p (h q) -> p h q", h=2)
                    dve.tensor_copy(z[:, :, 0:n], zsrc[:, :, 0:n]).then_inc(work_free[slot], 1)
                    evacuated(w)
                    dve.wait_ge(ln_ready, t.next(ln_ready))
                    i = dve.scalar_tensor_tensor(out=e[:, :, 0:n], in0=z[:, :, 0:n], scalar=0.0, in1=e[:, :, 0:n],
                                                 op0=ALU.max, op1=ALU.add)
                    if kb >= 4 * chunk:
                        chain(i)
                        b = 256 if kb == 4 * chunk + 3 else P
                        for h in range(2):
                            i = dve.tensor_tensor(e[:, h, 0:b], e[:, h, 0:b], con[:, C_MASK01 + 256 - b:C_MASK01 + 256], ALU.mult)
                    i.then_inc(sp_ready, 1)
                if 0 < u <= NU:
                    dve.wait_ge(pwh_ready, t.next(pwh_ready))
                    low(pw_l[:, :, 0:nb], zb[(u - 1) % 2][:, :, 0:nb], pw_h[:, :, 0:nb]).then_inc(pwl_ready, 1)
                if u < NU:
                    dve.wait_ge(sph_ready, t.next(sph_ready))
                    low(sp_l[u % 2][:, :, 0:n], e[:, :, 0:n], sp_h[u % 2][:, :, 0:n]).then_inc(spl_ready, 1)
                if u >= 2 and SB_UNITS[u - 2][1] == 0:
                    o = t.take("o_chunk")
                    c = SB_UNITS[u - 2][0]
                    dve.wait_ge(oh_ready, t.next(oh_ready))
                    cols = slice(c * HALF, (c + 1) * HALF)
                    low(o_l[:, pair, cols], ob[:, o % 2, :], o_h[:, pair, cols]).then_inc(o_ready, 1)

        chain(dve.memset(cu[:, 0:2], 0.0))
        for j in range(CONV_TILES):
            w = t.take("work")
            w2, slot = work()
            evacuated(w)
            dve.tensor_tensor(cu[:, 2:2 + S], ps[:, slot, :], cc[:, :], ALU.mult).then_inc(work_free[slot], 1)
            evacuated(w2)
            if j > 0:
                dve.wait_ge(tile_split, j)
            chain(dve.tensor_scalar(cv[:, :], cu[:, 2:2 + S], vcol(V_CONV + 8 + j), None, ALU.mult))
            for tap in (1, 0):
                chain(dve.scalar_tensor_tensor(out=cv[:, :], in0=cu[:, tap:tap + S], scalar=vcol(V_CONV + 4 * tap + j),
                                               in1=cv[:, :], op0=ALU.mult, op1=ALU.add))
            w, slot = work()
            dve.tensor_tensor(cv[:, :], cv[:, :], ps[:, slot, :], ALU.mult).then_inc(work_free[slot], 1)
            dve.wait_ge(high_ready, t.next(high_ready))
            low(c_l[:, j, :], cv[:, :], c_h[:, j, :]).then_inc(tile_split, 1)

        for m in range(KT):
            wa, wc = t.take("work"), t.take("work")
            w, slot = work()
            evacuated(wa)
            dve.tensor_tensor(ga[:, :], ps[:, slot, :], ga[:, :], ALU.mult).then_inc(work_free[slot], 1)
            w2, slot = work()
            evacuated(wc)
            dve.tensor_tensor(gc[:, :], ps[:, slot, :], gc[:, :], ALU.mult).then_inc(work_free[slot], 1)
            evacuated(w)
            evacuated(w2)
            dve.tensor_tensor(mix_t[:, m, :], ga[:, :], gc[:, :], ALU.add).then_inc(tile_ready, 1)
        for k in range(KT):
            dve.wait_ge(high_ready, t.next(high_ready))
            low(hl[:, k, :], mix_t[:, k, :], hh[:, k, :]).then_inc(tile_split, 1)
        skip(KT)
        barrier(dve, t, dve_end)
        dve.wait_ge(xold_in, 16)
        update(y_t, x_t, x_t, V_POST)
        norm(x_t, KT, S, V_MLP, hh, hl)

        nch = FF // FF_CHUNK
        t.take(tile_split, CONV_TILES + KT)
        for c in range(nch + 1):
            if c < nch:
                for j in range(2):
                    w = t.take("work")
                    evacuated(w)
                    if t.now(tile_split) > 0:
                        dve.wait_ge(tile_split, t.now(tile_split))
                    dve.tensor_tensor(ff[:, :], fr[:, :], fr[:, :], ALU.mult).then_inc(tile_ready, 1)
                    dve.wait_ge(high_ready, t.next(high_ready))
                    low(f_l[c % 2][:, j, :], ff[:, :], f_h[c % 2][:, j, :]).then_inc(tile_split, 1)
                    t.take(tile_split)
            if c == 1:
                skip(KT)
            elif c > 1:
                for m in range(KT):
                    w, slot = work()
                    dve.tensor_tensor(y_t[:, m, :], y_t[:, m, :], ps[:, slot, :], ALU.add).then_inc(work_free[slot], 1)
        barrier(dve, t, dve_end)
        update(y_t, x_t, x_t, V_POSTMLP)
        norm(x_t, KT, S, V_PLE, hh, hl)

        barrier(dve, t, dve_end)
        for k in range(2):
            dve.wait_ge(high_ready, t.next(high_ready))
            low(p_l[:, k, :], p_t[:, k, :], p_h[:, k, :]).then_inc(tile_split, 1)
        skip(KT)
        for m in range(KT):
            w = t.take("work")
            evacuated(w)
            chain(dve.tensor_tensor(pg[:, :], pg[:, :], y_t[:, m, :], ALU.mult))
            dve.tensor_tensor(x_t[:, m, :], x_t[:, m, :], pg[:, :], ALU.add).then_inc(tile_ready, 1)
        barrier(dve, t, dve_end)
        norm(m_t, KT, N_MEM, V_MEM, m_h, m_l)
        for layer in range(2):
            for j in range(2):
                w, slot = work()
                low_out(km_l[layer][:, j, :], km_h[layer][:, j, :], ps[:, slot, 0:N_MEM], slot)
            for j in range(2):
                skip()
                w, slot = work()
                low_out(vm_l[layer][:, :, j * P:(j + 1) * P], vm_h[layer][:, :, j * P:(j + 1) * P],
                        ps[:, slot, 0:N_MEM].rearrange("p (k f) -> p k f", k=2), slot)
        barrier(dve, t, dve_end)
        norm(x_t, KT, S, V_PRE2, hh, hl)

        def attend(heads, pieces, project, keys_of, forget=False):
            def maximum(n, qi):
                w, slot = work()
                i = (2 * n + qi) % 4
                dve.tensor_reduce(nm[:, i:i + 1], ps[:, slot, 0:keys_of(n % 4)], AX.X, ALU.max, negate=True).then_inc(nm_ready, 1)
                return w

            def normed(n, qi, w):
                i = (2 * n + qi) % 4
                evacuated(w)
                chain(dve.reciprocal(rinv[:, i:i + 1], rsum[:, i:i + 1]))
                p = prob[n % 2][qi][:, 0:keys_of(n % 4)]
                dve.tensor_scalar(p, p, rinv[:, i:i + 1], None, ALU.mult).then_inc(pn_ready, 1)

            def turned():
                g = t.take("pt")
                dve.wait_ge(pth_ready, t.next(pth_ready))
                low(pt_l[g % 2][:, :], aux[:, g % 2, :], pt_h[g % 2][:, :]).then_inc(ptl_ready, 1)

            def forget_terms(n):
                h, c = divmod(n, 4)
                dve.tensor_scalar(a_head[:, c * 256:(c + 1) * 256], a_base[:, c * 256:(c + 1) * 256], ccol(C_HEAD + h),
                                  None, ALU.mult).then_inc(ahead_ready, 1)

            if forget:
                forget_terms(0)
            for now, before, piece, following in attention_steps(heads, pieces):
                groups = keys_of(before % 4) // 256 if before is not None else 0
                ws = []
                for i in range(2):
                    if now is not None:
                        ws.append(maximum(now, i))
                    if i < groups:
                        turned()
                if forget and now is not None and now + 1 < 4 * heads:
                    forget_terms(now + 1)
                for i in range(2):
                    if now is not None:
                        normed(now, i, ws[i])
                    if i + 2 < groups:
                        turned()
                if piece:
                    project(piece, following)

        def memory_attention():
            q_pair(*qf_pad[0])
            attend(4, MEMORY, lambda piece, pair: q_pair(*qf_pad[pair]), lambda c: N_MEM)

        def gates_and_output(gain, ready, gates_here):
            barrier(dve, t, dve_end)
            n_out = t.take("out_use", KT) // 4
            if not gates_here:
                dve.wait_ge(gate_in, 16)
            for m in range(KT):
                g = gate_t[:, m, :]
                if gates_here:
                    w = t.take("work")
                    evacuated(w)
                    g = gt[m % 2][:, :]
                dve.wait_ge(out_in[m % 4], 16 * (n_out + m // 4 + 1))
                dve.tensor_tensor(g, g, go[m % 4][:, :], ALU.mult).then_inc(tile_ready, 1)
                dve.wait_ge(high_ready, t.next(high_ready))
                low(y_l[:, m, :], g, y_h[:, m, :]).then_inc(tile_split, 1)
            skip(KT)
            barrier(dve, t, dve_end)
            dve.wait_ge(xold_in, 32 if gain == V_POST2 else 48)
            update(z_t, xold_t, x_t, gain, ready)

        def rope(slot, dst):
            chain(dve.tensor_tensor(dst[64:96, :], ps[64:96, slot, :], trig[64:96, :], ALU.mult))
            chain(dve.tensor_tensor(ps[64:96, slot, :], ps[96:P, slot, :], trig[96:P, :], ALU.mult))
            return dve.tensor_tensor(dst[64:96, :], ps[64:96, slot, :], dst[64:96, :], ALU.add)

        barrier(dve, t, dve_end)
        zero_pads(qf_pad[0] + qf_pad[1])
        memory_attention()
        barrier(dve, t, dve_end)
        dve.wait_ge(pos_in, 16)
        a0, a1, a2 = (a[HI, :] for a in ang)
        chain(dve.tensor_copy(a0, posi[HI, :]))
        chain(dve.tensor_scalar(a1, a0, ccol(C_INV, HI), None, ALU.mult))
        chain(dve.tensor_scalar(a2, a1, 1.0 / (2 * np.pi), None, ALU.mult))
        chain(dve.tensor_scalar(a2, a2, ccol(C_OFF, HI), None, ALU.add))
        chain(dve.tensor_scalar(a2, a2, 12582912.0, None, ALU.add))
        chain(dve.tensor_scalar(a2, a2, -12582912.0, None, ALU.add))
        turn = 2 * np.pi
        c1 = 6.28125
        c2 = float(np.float32(np.round((turn - c1) * 2 ** 21) / 2 ** 21))
        c3 = float(np.float32(turn - c1 - c2))
        for c in (c1, c2, c3):
            chain(dve.scalar_tensor_tensor(out=a1, in0=a2, scalar=-c, in1=a1, op0=ALU.mult, op1=ALU.add))
        chain(dve.tensor_scalar(a1, a1, ccol(C_SHIFT, HI), None, ALU.add))
        dve.tensor_scalar(a1, a1, 3.1415925, -3.1415925, ALU.min, ALU.max).then_inc(table_ready, 1)
        dve.wait_ge(sin_ready, t.next(sin_ready))
        chain(dve.tensor_scalar(trig[96:P, :], trig[96:P, :], ccol(C_SIGN, slice(96, P)), None, ALU.mult))
        skip(5 + KT)
        w, slot = work()
        rope(slot, qf).then_inc(work_free[slot], 1)
        evacuated(w)
        dve.tensor_scalar(trig[HI, :], trig[HI, :], SCALE_MLA, None, ALU.mult)
        barrier(dve, t, dve_end)
        norm(cq_t, 3, S, V_QN, cq_h, cq_l)
        norm(ckv_t, 2, S, V_KVN, ckv_h, ckv_l)
        barrier(dve, t, dve_end)
        dve.wait_ge(high_ready, t.next(high_ready))
        low(ka_l[64:96, :], qf[64:96, :], ka_h[64:96, :])
        chain(low(ka2_l[64:96, :], qf[64:96, :], ka2_h[64:96, :]))

        def latent_piece(piece, h):
            if piece == "q":
                w, slot = work()
                dve.wait_ge(qn_ready, t.next(qn_ready))
                rope(slot, qf).then_inc(rope_ready, 1)
                dve.wait_ge(high_ready, t.next(high_ready))
                low(qa[h % 2][1][0:96, :], qf[0:96, :], qa[h % 2][0][0:96, :]).then_inc(work_free[slot], 1)
            elif piece == "kv":
                w, slot = work()
                low_out(ka[h % 2][1][LO, :], ka[h % 2][0][LO, :], kvf[LO, :], slot)
            else:
                w, slot = work()
                low_out(va[h % 2][1][:, :, :], va[h % 2][0][:, :, :],
                        ps[:, slot, :].rearrange("p (k f) -> p k f", k=8)[:, :, 64:P], slot)

        for piece in ("q", "kv", "vt"):
            latent_piece(piece, 0)
        attend(MLA_HEADS, LATENT, latent_piece, lambda c: (c + 1) * 256)
        gates_and_output(V_POST2, upd_ready, False)
        norm(x_t, KT, S, V_PRE2 + 8, hh, hl)

        barrier(dve, t, dve_end)
        zero_pads(qf_pad[0] + qf_pad[1])
        memory_attention()
        w = t.take("work")
        chain(dve.memset(fone[:, :], 1.0))
        dve.wait_ge(ln_ready, t.next(ln_ready))
        chain(dve.scalar_tensor_tensor(out=fe[:, :], in0=fx[:, :], scalar=0.0, in1=fe[:, :], op0=ALU.min, op1=ALU.subtract))
        chain(dve.tensor_tensor_scan(out=fx[:, :], data0=fone[:, :], data1=fe[:, :], initial=0.0, op0=ALU.mult, op1=ALU.add))
        chain(dve.tensor_copy(b_all[:, :], fx[:, :]))
        chain(dve.tensor_copy(a_base[0:32, :], b_all[0:32, :].bitcast(F32)))
        chain(dve.tensor_tensor(a_base[32:64, :], fx[32:64, :], b_all[32:64, :].bitcast(F32), ALU.subtract))
        chain(dve.memset(a_base[HI, :], -1.0))
        chain(dve.tensor_tensor(b_all[96:P, :], fx[96:P, :], b_all[96:P, :].bitcast(F32), ALU.subtract))
        dve.memset(b_all[LO, :].bitcast(F32), 1.0)
        chain(dve.memset(qf_pad[1][0][HI, 0, :].bitcast(F32), 0.0))
        chain(dve.memset(qf_pad[1][0][LO, 1, :].bitcast(F32), 0.0))
        dve.memset(qf_pad[1][1][HI, 0, :].bitcast(F32), 0.0).then_inc(fox_ready, 1)

        def fox_piece(piece, pair):
            if piece == "q":
                q_pair(*qf_pad[pair % 2])
            elif piece == "k":
                w, slot = work()
                low_out(kf[pair % 2][1][:, :], kf[pair % 2][0][:, :], ps[:, slot, :], slot)
            elif piece == "v":
                skip()
            else:
                w, slot = work()
                low_out(vf[pair % 2][1][:, :, :], vf[pair % 2][0][:, :, :],
                        ps[:, slot, :].rearrange("p (k f) -> p k f", k=8), slot)

        for piece in ("q", "k", "v", "vt"):
            fox_piece(piece, 0)
        attend(2 * FOX_PAIRS, FOX, fox_piece, lambda c: (c + 1) * 256, forget=True)
        gates_and_output(V_POST2 + 8, final_ready, True)


    ctx.close()



def tiles_of(w):
    k, m = w.shape[0] // P, w.shape[1] // P
    return w.reshape(k, P, m, P).transpose(2, 1, 0, 3)


def padded(w, cols):
    full = np.zeros((w.shape[0], P), np.float32)
    for at, a, b in cols:
        full[:, at:at + b - a] = w[:, a:b]
    return full


def weight_stream(w_in, w_attn_out, w_conv_out, w_o, w_up, w_down, w_ple_gate, w_ple_proj, w_mem_kv,
                  w_out, w_in_a, w_q_up_a, w_kv_up_a, w_in_b):
    slabs = []
    win = tiles_of(w_in)
    for pair in range(SB_PAIRS):
        slabs += [win[4 * i + pair] for i in range(3)]
    for j in range(CONV_TILES):
        slabs += [win[12 + 4 * i + j] for i in (1, 2, 0)]
    ao, co = tiles_of(w_attn_out), tiles_of(w_conv_out)
    for m in range(KT):
        slabs += [win[24 + m], win[32 + m], np.concatenate([ao[m], co[m]], 1)]
    slabs += list(tiles_of(w_o))
    up = tiles_of(w_up)
    for c in range(FF // FF_CHUNK + 1):
        if c < FF // FF_CHUNK:
            slabs += [up[2 * c], up[2 * c + 1]]
        if c > 0:
            down = tiles_of(w_down[(c - 1) * FF_CHUNK:c * FF_CHUNK])
            slabs += [np.concatenate(down[4 * q:4 * q + 4], 1) for q in range(2)]
    pp = tiles_of(w_ple_proj)
    slabs += [np.concatenate(pp[4 * q:4 * q + 4], 1) for q in range(2)]
    slabs += list(tiles_of(w_ple_gate))
    for layer in range(2):
        slabs += list(tiles_of(w_mem_kv[layer]))
    slabs += list(tiles_of(w_in_a[:, 672:928])) + list(tiles_of(w_in_a[:, 0:640]))
    slabs += list(tiles_of(w_in_a[:, 928:1952]))
    slabs += list(tiles_of(padded(w_in_a, [(64, 640, 672), (96, 656, 672), (112, 640, 656)])))
    for h in range(MLA_HEADS):
        q = tiles_of(padded(w_q_up_a, [(0, 96 * h, 96 * h + 96), (96, 96 * h + 80, 96 * h + 96), (112, 96 * h + 64, 96 * h + 80)]))[0]
        kv = tiles_of(w_kv_up_a[:, P * h:P * (h + 1)])[0]
        slabs.append(np.concatenate([q, kv, np.zeros((P, 3, P), np.float32)], 1))
    slabs += list(tiles_of(w_out[0]))
    slabs += list(tiles_of(w_in_b[:, 2316:2572]))
    slabs += list(tiles_of(padded(w_in_b, [(32 * q, 2304, 2316) for q in range(4)])))
    qkv = tiles_of(w_in_b[:, 0:2304])
    for pair in range(FOX_PAIRS):
        slabs += [qkv[6 * i + pair] for i in range(3)]
    slabs += list(tiles_of(w_in_b[:, 2572:3596])) + list(tiles_of(w_out[1]))
    assert len(slabs) == TOTAL_SLABS
    return np.ascontiguousarray(np.stack(slabs))


def vectors(gains, b_gate, w_conv, b_f):
    v = np.zeros((P, N_VEC), np.float32)
    for at, g in gains:
        v[:, at:at + g.size // P] = g.reshape(-1, P).T
    v[:, V_BGA:V_BGA + 16] = b_gate.reshape(16, P).T
    v[:, V_CONV:V_CONV + 12] = w_conv.reshape(12, P).T
    for q in range(4):
        v[32 * q:32 * q + MLA_HEADS, V_BF] = b_f
    return v


def constants():
    c = np.zeros((P, N_CONST), np.float32)
    i = np.arange(P)
    before = i[:, None] < i[None, :]
    c[:, C_ID:C_ID + P] = np.eye(P)
    c[:, C_ONE:C_ONE + P] = 1.0
    c[:, C_TRI:C_TRI + P] = ~before
    c[:, C_REST:C_REST + P] = before
    c[:, C_MASK01 + P:C_MASK01 + 256] = before
    c[:, C_CAP:C_CAP + P] = NEG
    c[:, C_CAP + P:C_CAP + 256] = np.where(before, -NEG, NEG)
    key = np.arange(256)
    for qi in range(2):
        c[:, C_NEG + 256 * qi:C_NEG + 256 * (qi + 1)] = np.where(key[None, :] <= i[:, None] + P * qi, 0.0, NEG)
    for h in range(12):
        c[h::32, C_HEAD + h] = 1.0
    half = 16
    inv = (np.float32(10000.0) ** (-np.arange(half, dtype=np.float32) / half)).astype(np.float32)
    c[64:, C_INV] = np.tile(inv, 4)
    c[64:96, C_OFF], c[64:96, C_SHIFT] = 0.25, np.pi / 2
    c[96:112, C_SIGN], c[112:, C_SIGN] = -1.0, 1.0
    c[:, C_EPS] = EPS
    return c


def kernel(**inputs):
    from concourse import bacc
    from concourse.bass_utils import run_bass_kernel_spmd

    a = {name: np.asarray(value) for name, value in inputs.items()}
    arrays = {
        "wall": weight_stream(a["w_in"][0], a["w_attn_out"][0], a["w_conv_out"][0], a["w_o"][0], a["w_up"][0],
                              a["w_down"][0], a["w_ple_gate"][0], a["w_ple_proj"][0], a["w_mem_kv_2"], a["w_out_2"],
                              a["w_in_a_2"][0], a["w_q_up_a_2"][0], a["w_kv_up_a_2"][0], a["w_in_b_2"][0]),
        "vecs": vectors([(V_PRE, a["g_pre_mix"]), (V_POST, a["g_post_mix"]), (V_MLP, a["g_pre_mlp"]),
                         (V_POSTMLP, a["g_post_mlp"]), (V_PLE, a["g_ple"]), (V_PRE2, a["norm_pre_2"]),
                         (V_POST2, a["norm_post_2"]), (V_MEM, a["mem_norm_2"]), (V_QN, a["q_norm_a_2"]),
                         (V_KVN, a["kv_norm_a_2"])], a["b_gate"], a["w_conv"], a["b_f_2"][0]),
        "consts": constants(),
        "xt": np.ascontiguousarray(a["x"][0].T),
        "pt": np.ascontiguousarray(a["p"][0, 0].T),
        "memt": np.ascontiguousarray(a["mem_2"][0].T),
        "pos": np.ascontiguousarray(a["positions_2"][0]),
    }
    nc = bacc.Bacc("TRN2", target_bir_lowering=False, num_devices=1)
    args = [nc.dram_tensor(n, v.shape, mybir.dt.from_np(v.dtype), kind="ExternalInput").ap() for n, v in arrays.items()]
    args.append(nc.dram_tensor("spill_x", [P, KT, S], F32).ap())
    args.append(nc.dram_tensor("spill_out", [KT, P, S], F32).ap())
    args.append(nc.dram_tensor("spill_gate", [KT, P, S], F32).ap())
    args.append(nc.dram_tensor("out_t", [D, S], F32, kind="ExternalOutput").ap())
    program(nc, *args)
    r = run_bass_kernel_spmd(nc, [arrays], core_ids=[0])
    return np.ascontiguousarray(r.results[0]["out_t"].T)[None]
```

```python
from contextlib import ExitStack

import numpy as np

import concourse.bass as bass
from concourse import mybir

F32 = mybir.dt.float32
F32R = mybir.dt.float32r
I32 = mybir.dt.int32
ALU = mybir.AluOpType
ACT = mybir.ActivationFunctionType
AX = mybir.AxisListType

P = 128
S = 1024
D = 1024
KT = D // P
HALF = 512
N_MEM = 256
EPS = 1e-6
SB_PAIRS = 4
CONV_TILES = 4
FF = 4 * D
FF_CHUNK = 256
MLA_HEADS = 12
FOX_PAIRS = 6
MAIN_TILES = 6
SCALE_64 = 64.0 ** -0.5
SCALE_MLA = 96.0 ** -0.5
NEG = -float(2.0 ** 100)
UNIT = 4096
UNITS = 27

C_ID, C_ONE, C_TRI, C_REST = 0, 128, 256, 384
C_MASK01, C_CAP, C_NEG = 512, 768, 1024
C_HEAD = 1536
C_INV, C_OFF, C_SIGN, C_SHIFT = 1548, 1549, 1550, 1551
C_EPS = 1552
N_CONST = 1554

V_PRE, V_POST, V_MLP, V_POSTMLP, V_PLE = 0, 8, 16, 24, 32
V_PRE2, V_POST2, V_MEM = 40, 56, 72
V_QN, V_KVN = 80, 83
V_BGA, V_BGC = 85, 93
V_CONV = 101
V_BF = 113
N_VEC = 114

N_SLABS = {"sb": 3 * SB_PAIRS, "conv": 3 * CONV_TILES, "mix": 3 * KT, "wo": KT,
           "mlp": 4 * (FF // FF_CHUNK), "ple": 2 + KT, "mem": 8,
           "a_in": 2 + 3 + 2 + 1, "mla": MLA_HEADS, "a_gate": KT, "a_out": KT,
           "b_in": 3, "fox": 3 * FOX_PAIRS, "b_gate": KT, "b_out": KT}
TOTAL_SLABS = sum(N_SLABS.values())


class Tally:

    def __init__(self):
        self.counts = {}

    def now(self, what):
        return self.counts.get(what if isinstance(what, str) else id(what), 0)

    def take(self, what, k=1):
        before = self.now(what)
        self.counts[what if isinstance(what, str) else id(what)] = before + k
        return before

    def next(self, what, k=1):
        return self.take(what, k) + k


def program(nc, wall, vecs, consts, xt, pt, memt, pos, spill_x, spill_o, spill_out, spill_gate, out):
    ctx = ExitStack()

    def sb(name, shape, dt):
        return ctx.enter_context(nc.sbuf_tensor(name, shape, dt))

    def sem(name):
        return ctx.enter_context(nc.semaphore(name))

    con = sb("con", [P, N_CONST], F32)
    vec = sb("vec", [P, N_VEC], F32)
    tri_r = sb("tri_r", [P, P], F32R)
    rest_r = sb("rest_r", [P, P], F32R)
    id_r = sb("id_r", [P, P], F32R)
    neg_r = sb("neg_r", [P, 2, 256], F32R)
    zero_r = sb("zero_r", [P, P], F32R)
    neg_flat = neg_r[:, :, :].rearrange("p a b -> p (a b)")
    raw = sb("raw", [P, 2, KT, P], F32)
    wh = sb("wh", [P, 2, KT, P], F32R)
    wl = sb("wl", [P, 2, KT, P], F32R)
    with nc.sbuf_tensor("xold_t", [P, KT, S], F32) as xold_t, nc.sbuf_tensor("z_t", [P, KT, S], F32) as z_t:
        pass
    with ExitStack() as second:
        qa2_h, qa2_l, ka2_h, ka2_l = (second.enter_context(nc.sbuf_tensor(n, [P, S], F32R))
                                      for n in ("qa2_h", "qa2_l", "ka2_h", "ka2_l"))
        va2_h, va2_l = (second.enter_context(nc.sbuf_tensor(n, [P, 8, 64], F32R)) for n in ("va2_h", "va2_l"))
    hh = sb("hh", [P, KT, S], F32R)
    hl = sb("hl", [P, KT, S], F32R)
    small = sb("small", [P, 64], F32)
    rt, rs = (small[:, 0:8], small[:, 32:40]), small[:, 8:16]
    nm, rsum, rinv = (small[:, a:a + 4] for a in (20, 24, 28))
    region = nc.sbuf_base

    def at(unit, name, shape, dt, extra=0):
        with ExitStack() as s:
            if unit or extra:
                s.enter_context(nc.sbuf_tensor(name + "_below", [P, unit * UNIT // 4 + extra // 4], F32))
            t = s.enter_context(nc.sbuf_tensor(name, shape, dt))
        return t

    assert region + UNITS * UNIT <= nc.sbuf_usable_end, (region, nc.sbuf_usable_end)
    gate_t = z_t
    ident, ones = con[:, C_ID:C_ID + P], con[:, C_ONE:C_ONE + P]

    x_t = at(0, "x_t", [P, KT, S], F32)
    y_t = at(8, "y_t", [P, KT, S], F32)
    sq = [at(24 + i, f"sq{i}", [P, S], F32) for i in range(2)]
    diag = at(26, "diag", [P, S], F32)
    nt = [at(22 + i, f"nt{i}", [P, S], F32) for i in range(2)]
    pads = [(at(8 + 4 * i, f"qp_h{i}", [P, 2, S], F32R), at(10 + 4 * i, f"qp_l{i}", [P, 2, S], F32R)) for i in range(2)]
    ks = [(at(2 + 2 * i, f"k_h{i}", [P, S], F32R), at(3 + 2 * i, f"k_l{i}", [P, S], F32R)) for i in range(2)]
    vs = [(at(u, f"v_h{u}", [P, 8, P], F32R), at(u + 1, f"v_l{u}", [P, 8, P], F32R)) for u in (6, 16)]
    vts = [at(u, f"vt{u}", [P, S], F32) for u in (6, 16)]
    op = at(0, "op", [P, 2, S], F32R)
    op_h, op_l = op[:, 0, :], op[:, 1, :]
    zb = [at(18 + i, f"zb{i}", [P, 2, HALF], F32) for i in range(3)]
    pw_l = [at(18 + i, f"pw_l{i}", [P, 2, HALF], F32R) for i in range(3)]
    eb = [at(21 + i, f"eb{i}", [P, 2, HALF], F32) for i in range(3)]
    sp_l = [at(21 + i, f"sp_l{i}", [P, 2, HALF], F32R) for i in range(3)]
    sp_h = [at(24 + i, f"sp_h{i}", [P, 2, HALF], F32R) for i in range(2)]
    pw_h = at(26, "pw_h", [P, 2, HALF], F32R)
    o_all = at(0, "o_all", [P, 2, 4, S], F32R)
    o_h, o_l = o_all[:, 0, :, :], o_all[:, 1, :, :]
    c_h, c_l = at(8, "c_h", [P, 4, S], F32R), at(12, "c_l", [P, 4, S], F32R)
    cc = at(16, "cc", [P, S], F32)
    cu = at(17, "cu", [P, 2 + S], F32)
    cv = at(19, "cv", [P, S], F32)
    mix_t = at(16, "mix_t", [P, KT, S], F32)
    ga, gc = at(24, "ga", [P, S], F32), at(25, "gc", [P, S], F32)
    f_h = [at(16 + 2 * i, f"f_h{i}", [P, 2, S], F32R) for i in range(2)]
    f_l = [at(20 + 2 * i, f"f_l{i}", [P, 2, S], F32R) for i in range(2)]
    row_sb = at(26, "row_sb", [P, S], F32)
    fr, ff = at(24, "fr", [P, S], F32), at(25, "ff", [P, S], F32)
    p_t = at(16, "p_t", [P, 2, S], F32)
    p_h, p_l = at(18, "p_h", [P, 2, S], F32R), at(20, "p_l", [P, 2, S], F32R)
    pg = at(22, "pg", [P, S], F32)
    m_t = at(16, "m_t", [P, KT, N_MEM], F32)
    m_h, m_l = at(10, "m_h", [P, KT, N_MEM], F32R), at(12, "m_l", [P, KT, N_MEM], F32R)
    mv = at(14, "mv", [P, N_MEM], F32)
    km_h = [at(18 + 2 * i, f"km_h{i}", [P, 2, N_MEM], F32R) for i in range(2)]
    km_l = [at(18 + 2 * i, f"km_l{i}", [P, 2, N_MEM], F32R, 2048) for i in range(2)]
    vm_h = [at(19 + 2 * i, f"vm_h{i}", [P, 2, 2 * P], F32R) for i in range(2)]
    vm_l = [at(19 + 2 * i, f"vm_l{i}", [P, 2, 2 * P], F32R, 2048) for i in range(2)]
    prob = [[at(16, "prob00", [P, S], F32), at(17, "prob01", [P, S], F32)],
            [at(22, "prob10", [P, S], F32), at(23, "prob11", [P, S], F32)]]
    pt_h = [at(24 + i, f"pt_h{i}", [P, HALF], F32R) for i in range(2)]
    pt_l = [at(24 + i, f"pt_l{i}", [P, HALF], F32R, 2048) for i in range(2)]
    ot = at(26, "ot", [P, S], F32)
    cq_t, ckv_t = at(3, "cq_t", [P, 3, S], F32), at(6, "ckv_t", [P, 2, S], F32)
    cq_h, cq_l = at(0, "cq_h", [P, 3, S], F32R), at(8, "cq_l", [P, 3, S], F32R)
    ckv_h, ckv_l = at(11, "ckv_h", [P, 2, S], F32R), at(13, "ckv_l", [P, 2, S], F32R)
    qa_h, qa_l = at(3, "qa_h", [P, S], F32R), at(4, "qa_l", [P, S], F32R)
    ka_h, ka_l = at(5, "ka_h", [P, S], F32R), at(6, "ka_l", [P, S], F32R)
    kvf = at(7, "kvf", [P, S], F32)
    va_h, va_l = at(15, "va_h", [P, 8, 64], F32R), at(15, "va_l", [P, 8, 64], F32R, 2048)
    qa, ka, va = ((qa_h, qa_l), (qa2_h, qa2_l)), ((ka_h, ka_l), (ka2_h, ka2_l)), ((va_h, va_l), (va2_h, va2_l))
    trig = at(18, "trig", [P, S], F32)
    qf = at(19, "qf", [P, S], F32)
    ang = [at(26, "ang0", [P, S], F32), at(19, "ang1", [P, S], F32), at(18, "ang2", [P, S], F32)]
    posi = at(15, "posi", [P, S], I32)
    kf = [(at(4 + 2 * i, f"kf_h{i}", [P, S], F32R), at(5 + 2 * i, f"kf_l{i}", [P, S], F32R)) for i in range(2)]
    vf = [(at(18 + 2 * i, f"vf_h{i}", [P, 8, P], F32R), at(19 + 2 * i, f"vf_l{i}", [P, 8, P], F32R)) for i in range(2)]
    fvt = at(0, "fvt", [P, S], F32)
    a_base, a_head, b_all = at(1, "a_base", [P, S], F32), at(2, "a_head", [P, S], F32R), at(3, "b_all", [P, S], F32R)
    fx, fe, fone = at(4, "fx", [P, S], F32), at(5, "fe", [P, S], F32), at(6, "fone", [P, S], F32)
    y_h, y_l = at(0, "y_h", [P, KT, S], F32R), at(8, "y_l", [P, KT, S], F32R)
    gt, gt_late = ([at(u + i, f"gt{u + i}", [P, S], F32) for i in range(2)] for u in (1, 16))
    go = [at(22 + i, f"go{i}", [P, S], F32) for i in range(4)]
    ps = ctx.enter_context(nc.psum_tensor("ps", [P, 2, S], F32))
    aux = ctx.enter_context(nc.psum_tensor("aux", [P, 2, HALF], F32))
    row = aux[:, :, :].rearrange("p a b -> p (a b)")
    ob = ctx.enter_context(nc.psum_tensor("ob", [P, 2, HALF], F32))

    init_in, p_in, m_in, pos_in, xold_in = map(sem, ("init_in", "p_in", "m_in", "pos_in", "xold_in"))
    x_in = [sem(f"x_in{k}") for k in range(KT)]
    raw_in, out_in = [sem(f"raw_in{i}") for i in range(2)], [sem(f"out_in{i}") for i in range(4)]
    ot_out, spill_done, end_out = map(sem, ("ot_out", "spill_done", "end_out"))
    w_high, w_split, slab_begun, work_done = map(sem, ("w_high", "w_split", "slab_begun", "work_done"))
    work_free = [sem(f"work_free{i}") for i in range(2)]
    act_end, dve_end, act_chain, dve_chain = map(sem, ("act_end", "dve_end", "act_chain", "dve_chain"))
    const_ready = sem("const_ready")
    high_ready, tile_ready, tile_split = map(sem, ("high_ready", "tile_ready", "tile_split"))
    sq_ready, sq_used, rt_ready, diag_ready = map(sem, ("sq_ready", "sq_used", "rt_ready", "diag_ready"))
    nt_ready, nh_ready, norm_ready = map(sem, ("nt_ready", "nh_ready", "norm_ready"))
    upd_ready, final_ready = map(sem, ("upd_ready", "final_ready"))
    ln_ready, sp_ready, sph_ready, spl_ready = map(sem, ("ln_ready", "sp_ready", "sph_ready", "spl_ready"))
    tri_done, d_ready, pwh_ready, pwl_ready = map(sem, ("tri_done", "d_ready", "pwh_ready", "pwl_ready"))
    av_done, oh_ready, o_ready = map(sem, ("av_done", "oh_ready", "o_ready"))
    abs_ready, ea_ready, pw_ready, rest_done = map(sem, ("abs_ready", "ea_ready", "pw_ready", "rest_done"))
    z_done, z_free, piece_done, piece_free = map(sem, ("z_done", "z_free", "piece_done", "piece_free"))
    op_left, o_in = map(sem, ("op_left", "o_in"))
    nm_ready, pn_ready, pt_done = map(sem, ("nm_ready", "pn_ready", "pt_done"))
    pth_ready, ptl_ready, oa_done, oa_taken = map(sem, ("pth_ready", "ptl_ready", "oa_done", "oa_taken"))
    table_ready, sin_ready, qn_ready, rope_ready = map(sem, ("table_ready", "sin_ready", "qn_ready", "rope_ready"))
    row_done = sem("row_done")
    ahead_ready, fox_ready = map(sem, ("ahead_ready", "fox_ready"))
    gate_out, gate_in = [sem(f"gate_out{i}") for i in range(2)], sem("gate_in")
    silu_ready = sem("silu_ready")
    block = ctx.enter_context(nc.Block())

    def barrier(eng, t, me):
        eng.drain().then_inc(me, 1)
        n = t.next("end")
        eng.wait_ge(act_end, n)
        eng.wait_ge(dve_end, n)

    SB_UNITS = []
    for pair in range(SB_PAIRS):
        for chunk in range(2):
            for kb in range(4 * chunk + 3, -1, -1):
                first = min(max(kb * P - chunk * HALF, 0), HALF - 256)
                SB_UNITS.append((pair, chunk, kb, first, HALF - first))
    NU = len(SB_UNITS)
    SB_PIECES = {0: ("vt", 0, 8), 1: ("q", 0, 2), 2: ("q", 2, 4), 3: ("q", 4, 6), 4: ("q", 6, 8), 5: ("k", 0, 2),
                 6: ("k", 2, 4), 7: ("k", 4, 6), 8: ("k", 6, 8), 9: ("v", 0, 3), 10: ("v", 3, 6), 11: ("v", 6, 8)}
    Z_SLOT, PIECE_SLOT = 0, 1

    def sb_piece(step):
        pair, u = divmod(step, NU // SB_PAIRS)
        if pair < SB_PAIRS and u in SB_PIECES:
            piece, a, b = SB_PIECES[u]
            pair += piece != "vt"
            if 0 < pair < SB_PAIRS:
                return piece, a, b, pair, 4 * (pair - 1) + ("q", "k", "v", "vt").index(piece)
        return None, 0, 0, 0, 0

    def first_of_chunk(u):
        return SB_UNITS[u][2] == 4 * SB_UNITS[u][1] + 3
    def attention_steps(heads, pieces):
        table, group = pieces
        steps = []
        for n in range(4 * heads + 1):
            h, c = divmod(n, 4)
            following = h // group + 1
            if group == heads:
                piece = table.get(n)
            else:
                piece = table.get((h % group, c)) if following * group < heads else None
            steps.append((n if n < 4 * heads else None, n - 1 if n > 0 else None, piece, following))
        return steps

    MEMORY = ({i + 2: piece for i, piece in enumerate(["cq0", "cq1", "cq2", "ckv0", "ckv1"] + [f"gate{m}" for m in range(5)])}, 4), \
             ({}, 4)
    LATENT = ({(0, 0): "q", (0, 1): "kv", (0, 2): "vt"}, 1)
    FOX = ({(0, 0): "q", (0, 1): "k", (1, 0): "v", (1, 1): "vt"}, 2)

    def widths(keys):
        return [(0, min(keys, HALF))] + ([(HALF, keys)] if keys > HALF else [])

    @block.sync
    def _(sp):
        sp.dma_start(con[:], consts).then_inc(init_in, 16)
        sp.dma_start(vec[:], vecs).then_inc(init_in, 16)
        for k in range(KT):
            sp.dma_start(x_t[:, k, :], xt[k * P:(k + 1) * P, :]).then_inc(x_in[k], 16)
        for s in range(2):
            sp.dma_start(raw[:, s, :, :], wall[s]).then_inc(raw_in[s], 16)

        with sp.Fori(1, TOTAL_SLABS // 2) as i:
            for s in range(2):
                sp.wait_ge(w_split, 2 * i + s - 1)
                sp.dma_start(raw[:, s, :, :], wall[bass.ds(2 * i + s, 1)].rearrange("a p k m -> (a p) k m")).then_inc(raw_in[s], 16)

        if TOTAL_SLABS % 2:
            sp.wait_ge(w_split, TOTAL_SLABS - 2)
            sp.dma_start(raw[:, 0, :, :], wall[TOTAL_SLABS - 1]).then_inc(raw_in[0], 16)
        for k in range(KT):
            sp.wait_ge(final_ready, k + 1)
            sp.dma_start(out[k * P:(k + 1) * P, :], x_t[:, k, :]).then_inc(end_out, 16)
        sp.wait_ge(end_out, 16 * KT)

    @block.gpsimd
    def _(pool):
        def split(s, slab_words):
            loaded, begun, high = slab_words
            pool.wait_ge(raw_in[s], loaded)
            if begun is not None:
                pool.wait_ge(slab_begun, begun)
            pool.tensor_tensor(wh[:, s, :, :], raw[:, s, :, :], ones.unsqueeze(1).broadcast_to([P, KT, P]), ALU.mult).then_inc(w_high, 1)
            pool.wait_ge(w_high, high)
            pool.tensor_tensor(wl[:, s, :, :], raw[:, s, :, :], wh[:, s, :, :].bitcast(F32), ALU.subtract).then_inc(w_split, 1)

        for s in range(2):
            split(s, (16, None, s + 1))
        with pool.Fori(1, TOTAL_SLABS // 2) as i:
            for s in range(2):
                split(s, (16 * i + 16, 2 * i + s, 2 * i + s + 1))
        if TOTAL_SLABS % 2:
            last = TOTAL_SLABS - 1
            split(0, (8 * last + 16, last, last + 1))

    @block.tensor
    def _(pe):
        t = Tally()

        def work():
            w = t.take("work")
            if w >= 2:
                pe.wait_ge(work_free[w % 2], w // 2)
            return w, w % 2

        def evacuated(w):
            pe.wait_ge(work_free[w % 2], w // 2 + 1)

        def slab():
            s = t.take("slab")
            pe.wait_ge(w_split, s + 1)
            t.fresh = True
            return s % 2

        def proj(w, sl, ks, rh, rl, n=S, ready=None):
            halves = [(a, min(a + HALF, n)) for a in range(0, n, HALF)]
            for i, k in enumerate(ks):
                if ready:
                    ready(i)
                for j, (lw, r) in enumerate(((wh, rh), (wh, rl), (wl, rh))):
                    for a, b in halves:
                        m = pe.matmul(ps[:, w, a:b], lw[:, sl, k, :], r[:, i, a:b],
                                      start=(i == 0 and j == 0), stop=(i == len(ks) - 1 and j == 2))
                        if t.fresh:
                            m.then_inc(slab_begun, 1)
                            t.fresh = False
            m.then_inc(work_done, 1)

        def product(ks, rh, rl, n=S, ready=None, sl=None):
            sl = slab() if sl is None else sl
            w, slot = work()
            proj(slot, sl, ks, rh, rl, n, ready)
            return w

        def transposes(src, n):
            w, slot = work()
            for j in range(n):
                m = pe.transpose(ps[:, slot, j * P:(j + 1) * P], src[:, j * P:(j + 1) * P], ident)
            m.then_inc(work_done, 1)
            return w

        def square_sums(k, ktiles, n, bank=0):
            pe.wait_ge(sq_ready, t.next(sq_ready))
            if k == 0:
                pe.matmul(ob[:, bank, 0:8], zero_r[:, :].bitcast(F32), ones[:, 0:8], start=True, stop=True, skip_group_check=True)
            at_slot = t.take("sq") % 2
            for j in range(n // P):
                m = pe.matmul(ob[:, bank, j:j + 1], sq[at_slot][:, j * P:(j + 1) * P], ones[:, 0:1],
                              start=False, stop=True, skip_group_check=True)
            m.then_inc(sq_used, 1)

        def norm_row(n):
            pe.wait_ge(diag_ready, t.next(diag_ready))
            for a in range(0, n, HALF):
                b = min(a + HALF, n)
                m = pe.matmul(row[:, a:b], ones, diag[:, a:b], start=True, stop=True)
            m.then_inc(row_done, 1)

        def norm_stats(ktiles, n):
            for k in range(ktiles):
                square_sums(k, ktiles, n)
            norm_row(n)

        def with_sums(make):
            for m in range(KT):
                make(m)
                if m > 0:
                    square_sums(m - 1, KT, S)
            square_sums(KT - 1, KT, S)

        def norm_tiles(ktiles):
            base = t.take(norm_ready, ktiles)
            return lambda i: pe.wait_ge(norm_ready, base + i + 1)

        pe.wait_ge(init_in, 32)
        pe.wait_ge(const_ready, 1)
        norm_stats(KT, S)
        ready = norm_tiles(KT)

        def sb_project(piece, pair):
            if piece == "vt":
                evacuated(t.now("work") - 1)
                transposes(vts[pair % 2], 8)
            else:
                product(range(KT), hh, hl, ready=ready if piece == "q" else None)

        def sb_part(step):
            piece, a, b, pair, number = sb_piece(step)
            if not piece:
                return
            if a == 0:
                if number > 0:
                    pe.wait_ge(piece_free, number)
                if piece != "vt":
                    t.sb_slab = slab()
            for k in range(a, b):
                if piece == "vt":
                    m = pe.transpose(ps[:, PIECE_SLOT, k * P:(k + 1) * P], vts[pair % 2][:, k * P:(k + 1) * P], ident)
                    continue
                for j, (lw, r) in enumerate(((wh, hh), (wh, hl), (wl, hh))):
                    for c in range(0, S, HALF):
                        m = pe.matmul(ps[:, PIECE_SLOT, c:c + HALF], lw[:, t.sb_slab, k, :], r[:, k, c:c + HALF],
                                      start=(k == 0 and j == 0), stop=(k == KT - 1 and j == 2))
                        if t.fresh:
                            m.then_inc(slab_begun, 1)
                            t.fresh = False
            if b == KT:
                m.then_inc(piece_done, 1)

        def logits(u):
            pair, chunk, kb, first, n = SB_UNITS[u]
            if u > 0:
                pe.wait_ge(z_free, u)
                if u % (NU // SB_PAIRS) == 0:
                    pe.wait_ge(piece_free, 4 * (pair - 1) + 2)
            k, q = ks[pair % 2], pads[pair % 2]
            for h in range(2):
                for j, (a, b) in enumerate(((0, 0), (1, 0), (0, 1))):
                    q0 = chunk * HALF + first
                    m = pe.matmul(ps[:, Z_SLOT, h * HALF:h * HALF + n], k[a][:, kb * P:(kb + 1) * P],
                                  q[b][:, h, q0:q0 + n], start=(j == 0), stop=(j == 2))
            m.then_inc(z_done, 1)

        def suffix(u, tri):
            first, n = SB_UNITS[u][3:]
            for h in range(2):
                for r in (sp_h[u % 2], sp_l[u % 3]):
                    m = pe.matmul(aux[:, h, first:first + n], tri[:, :], r[:, h, 0:n],
                                  start=False, stop=True, skip_group_check=True)
            return m

        def clear(banks):
            for h in range(2):
                m = pe.matmul(banks[:, h, :], zero_r[:, :], neg_flat, start=True, stop=True, skip_group_check=True)
            return m

        def av(u):
            pair, chunk, kb, first, n = SB_UNITS[u]
            pe.wait_ge(pwl_ready, u + 1)
            if first_of_chunk(u):
                if t.now("chunks") > 0:
                    pe.wait_ge(o_ready, t.now("chunks"))
                t.take("chunks")
                if chunk == 0 and pair > 0:
                    pe.wait_ge(piece_free, 4 * pair)
                clear(ob)
            v = vs[pair % 2]
            for h in range(2):
                for a, r in ((0, pw_h), (1, pw_h), (0, pw_l[u % 3])):
                    m = pe.matmul(ob[0:64, h, first:first + n], v[a][:, kb, h * 64:(h + 1) * 64], r[:, h, 0:n],
                                  start=False, stop=True, skip_group_check=True)
            m.then_inc(av_done, 1)

        for piece in ("q", "k", "v", "vt"):
            sb_project(piece, 0)
        for w in (t.now("work") - 2, t.now("work") - 1):
            evacuated(w)
        logits(0)
        clear(aux)
        for step in range(NU + 3):
            if step >= 3:
                av(step - 3)
            if 2 <= step < NU + 1:
                u = step - 2
                pe.wait_ge(d_ready, u + 1)
                if first_of_chunk(u + 1):
                    clear(aux).then_inc(rest_done, 1)
                else:
                    suffix(u, rest_r).then_inc(rest_done, 1)
            sb_part(step)
            if step + 1 < NU:
                logits(step + 1)
            if 1 <= step <= NU:
                pe.wait_ge(spl_ready, step)
                suffix(step - 1, tri_r).then_inc(tri_done, 1)
        pe.wait_ge(z_free, NU)
        pe.wait_ge(piece_free, 4 * (SB_PAIRS - 1))

        for j in range(CONV_TILES):
            for _ in range(3):
                product(range(KT), hh, hl)

        for m in range(KT):
            product(range(KT), hh, hl)
            product(range(KT), hh, hl)
            sl = slab()
            product(range(4), o_h, o_l, sl=sl, ready=(lambda i: pe.wait_ge(o_in, 32)) if m == 0 else None)
            product(range(4, 8), c_h, c_l, sl=sl,
                    ready=(lambda i: pe.wait_ge(tile_split, CONV_TILES)) if m == 0 else None)
        t.take(tile_split, CONV_TILES)

        def from_split(ktiles):
            base = t.take(tile_split, ktiles)
            return lambda i: pe.wait_ge(tile_split, base + i + 1)

        ready = from_split(KT)
        with_sums(lambda m: product(range(KT), hh, hl, ready=ready if m == 0 else None))
        norm_row(S)
        split_ready = norm_tiles(KT)

        def ready(k):
            square_sums(k, KT, S)
            split_ready(k)

        nch = FF // FF_CHUNK
        for c in range(nch + 1):
            if c < nch:
                for j in range(2):
                    product(range(KT), hh, hl, ready=ready)
                    ready = None
                if c == 0:
                    norm_row(S)
            if c > 0:
                b = t.take(tile_split, 2)
                for q in range(2):
                    sl = slab()
                    for m in range(4):
                        product([2 * m, 2 * m + 1], f_h[(c - 1) % 2], f_l[(c - 1) % 2], sl=sl,
                                ready=(lambda i: pe.wait_ge(tile_split, b + i + 1)) if q == m == 0 else None)
                        if c == nch and 4 * q + m >= 2:
                            square_sums(4 * q + m - 2, KT, S)
        for m in range(KT - 2, KT):
            square_sums(m, KT, S)
        norm_row(S)
        norm_stats(KT, S)
        nready = norm_tiles(KT)
        ready = from_split(2)
        for q in range(2):
            sl = slab()
            for m in range(4):
                product([2 * m, 2 * m + 1], p_h, p_l, sl=sl, ready=ready)
                ready = None
        for m in range(KT):
            product(range(KT), hh, hl, ready=nready)
            nready = None
            if m > 0:
                square_sums(m - 1, KT, N_MEM, 0)
                square_sums(m - 1, KT, S, 1)
        square_sums(KT - 1, KT, N_MEM, 0)
        square_sums(KT - 1, KT, S, 1)

        norm_row(N_MEM)
        ready = norm_tiles(KT)
        row_made = False
        for layer in range(2):
            for j in range(2):
                product(range(KT), m_h, m_l, n=N_MEM, ready=ready)
                ready = None
                if not row_made:
                    norm_row(S)
                    row_made = True
            for j in range(2):
                w = product(range(KT), m_h, m_l, n=N_MEM)
                evacuated(w)
                transposes(mv, 2)

        ready = norm_tiles(KT)

        def attend(heads, pieces, project, q_of, k_of, v_of, rows, keys_of, causal, bias=None):
            def scores(n, qi):
                h, c = divmod(n, 4)
                keys = keys_of(c)
                w, slot = work()
                q0 = c * 256 + qi * P
                q, k = q_of(h), k_of(h)
                parts = [(q[0], k[0], rows), (q[0], k[1], rows), (q[1], k[0], rows)]
                parts = [(l[0:rows, q0:q0 + P], r, n_rows) for l, r, n_rows in parts]
                if bias:
                    if qi == 0:
                        pe.wait_ge(ahead_ready, t.next(ahead_ready))
                    parts.append((bias[0][:, q0:q0 + P], bias[1], P))
                for a, b in widths(keys):
                    masked = causal and b == keys
                    for j, (l, r, n_rows) in enumerate(parts):
                        m = pe.matmul(ps[:, slot, a:b], l, r[0:n_rows, a:b], start=(j == 0),
                                      stop=(j == len(parts) - 1 and not masked), skip_group_check=True)
                    if masked:
                        m = pe.matmul(ps[:, slot, b - 256:b], id_r[:, :], neg_r[:, qi, :], start=False, stop=True,
                                      skip_group_check=True)
                m.then_inc(work_done, 1)

            def turn(n, j):
                if j == 0:
                    pe.wait_ge(pn_ready, t.next(pn_ready, 2))
                g = t.take("pt")
                if g >= 2:
                    pe.wait_ge(ptl_ready, g - 1)
                for kbl in range(2):
                    for qi in range(2):
                        kb = 2 * j + kbl
                        m = pe.transpose(aux[:, g % 2, kbl * 256 + qi * P:kbl * 256 + (qi + 1) * P],
                                         prob[n % 2][qi][:, kb * P:(kb + 1) * P], ident)
                m.then_inc(pt_done, 1)
                return g

            def values(n, g, j):
                h, c = divmod(n, 4)
                o = t.now("oa")
                if j == 0:
                    if o >= 2:
                        pe.wait_ge(oa_taken, o - 1)
                pe.wait_ge(ptl_ready, g + 1)
                last = j == keys_of(c) // 256 - 1
                for kbl in range(2):
                    kb = 2 * j + kbl
                    for i, (l, r) in enumerate(((0, pt_h), (1, pt_h), (0, pt_l))):
                        m = pe.matmul(ob[0:64, o % 2, 0:256], v_of(h, kb)[l], r[g % 2][:, kbl * 256:(kbl + 1) * 256],
                                      start=(kb == 0 and i == 0), stop=(last and kbl == 1 and i == 2), skip_group_check=True)
                if last:
                    t.take("oa")
                    m.then_inc(oa_done, 1)

            for now, before, piece, following in attention_steps(heads, pieces):
                groups = keys_of(before % 4) // 256 if before is not None else 0
                turned = []
                if now == 0:
                    for w in (t.now("work") - 1, t.now("work") - 2):
                        evacuated(w)
                for i in range(2):
                    if now is not None:
                        scores(now, i)
                    if i < groups:
                        turned.append(turn(before, i))
                if piece:
                    project(piece, following)
                for j in range(groups):
                    values(before, turned[j], j)
                    if j + 2 < groups:
                        turned.append(turn(before, j + 2))

        def memory_attention(layer, ready):
            product(range(KT), hh, hl, ready=ready)
            product(range(KT), hh, hl)
            attend(4, MEMORY[layer], lambda piece, group: product(range(KT), hh, hl),
                   lambda h: [q[:, h % 2, :] for q in pads[h // 2]], lambda h: (km_h[layer][:, h // 2, :], km_l[layer][:, h // 2, :]),
                   lambda h, kb: (vm_h[layer][:, kb, h * 64:h * 64 + 64], vm_l[layer][:, kb, h * 64:h * 64 + 64]),
                   P, lambda c: N_MEM, False)

        def gates():
            for m in range(KT):
                product(range(KT), hh, hl)

        def output():
            ready = from_split(KT)
            with_sums(lambda m: product(range(KT), y_h, y_l, ready=ready if m == 0 else None))
            norm_row(S)

        memory_attention(0, ready)
        product(range(KT), hh, hl)
        for k in range(3):
            square_sums(k, 3, S, 0)
        for k in range(2):
            square_sums(k, 2, S, 1)
        product(range(KT), hh, hl)
        norm_row(S)
        readyq = norm_tiles(3)
        product(range(KT), hh, hl)
        norm_row(S)
        readykv = norm_tiles(2)
        product(range(KT), hh, hl)
        state = {}

        def latent_piece(piece, h):
            if piece == "q":
                state["slab"] = slab()
                product(range(3), cq_h, cq_l, sl=state["slab"], ready=readyq if h == 0 else None)
            elif piece == "kv":
                state["kv"] = product(range(3, 5), ckv_h, ckv_l, sl=state["slab"], ready=readykv if h == 0 else None)
            else:
                evacuated(state["kv"])
                transposes(kvf, 8)

        for piece in ("q", "kv", "vt"):
            latent_piece(piece, 0)
        evacuated(t.now("work") - 1)
        attend(MLA_HEADS, LATENT, latent_piece, lambda h: qa[h % 2], lambda h: ka[h % 2],
               lambda h, kb: [v[:, kb, :] for v in va[h % 2]], P, lambda c: (c + 1) * 256, True)
        output()

        norm_stats(KT, S)
        ready = norm_tiles(KT)
        memory_attention(1, ready)
        product(range(KT), hh, hl)

        def fox_piece(piece, pair):
            if piece == "vt":
                evacuated(state["v"])
                transposes(fvt, 8)
            else:
                state[piece] = product(range(KT), hh, hl)

        for piece in ("q", "k", "v", "vt"):
            fox_piece(piece, 0)
        attend(2 * FOX_PAIRS, FOX, fox_piece, lambda h: [q[:, h % 2, :] for q in pads[h // 2 % 2]], lambda h: kf[h // 2 % 2],
               lambda h, kb: [v[:, kb, h % 2 * 64:h % 2 * 64 + 64] for v in vf[h // 2 % 2]],
               P, lambda c: (c + 1) * 256, True, (a_head, b_all))
        gates()
        output()
        assert t.now("slab") == TOTAL_SLABS, (t.now("slab"), TOTAL_SLABS)

    vcol = lambda c, rows=slice(0, P): vec[rows, c:c + 1]
    ccol = lambda c, rows=slice(0, P): con[rows, c:c + 1]
    LO, HI = slice(0, 64), slice(64, P)

    @block.scalar
    def _(act):
        t = Tally()

        def work():
            w = t.take("work")
            act.wait_ge(work_done, w + 1)
            return w, w % 2

        def skip(n=1):
            t.take("work", n)

        def evacuated(w):
            act.wait_ge(work_free[w % 2], w // 2 + 1)

        def chain(ins):
            ins.then_inc(act_chain, 1)
            act.wait_ge(act_chain, t.next(act_chain))

        def copy(out_, in_, scale=1.0):
            return act.activation(out_, in_, ACT.Copy, scale=scale)

        def take_out(dst, func=ACT.Copy, n=S, **kw):
            w, slot = work()
            act.activation(dst, ps[:, slot, 0:n], func, **kw).then_inc(work_free[slot], 1)
            return w

        def square(src, n=S):
            i = t.take(sq_used)
            if i >= 2:
                act.wait_ge(sq_used, i - 1)
            act.activation(sq[i % 2][:, 0:n], src, ACT.Square).then_inc(sq_ready, 1)

        def roots(n, d, bank=0, after=0):
            act.wait_ge(sq_used, t.now(sq_used) - after)
            act.activation(rt[bank][:, 0:n // P], ob[:, bank, 0:n // P], ACT.Sqrt, bias=ccol(C_EPS), scale=1.0 / d).then_inc(rt_ready, 1)

        def norm_stats(src, ktiles, n, d, ready=None):
            for k in range(ktiles):
                if ready:
                    ready(k)
                square(src[:, k, :], n)
            roots(n, d)

        def take_out_with_square(dst):
            w, slot = work()
            square(ps[:, slot, :])
            copy(dst, ps[:, slot, :]).then_inc(work_free[slot], 1)

        def norm_tiles(ktiles, n, dst, between=None):
            for k in range(ktiles):
                act.wait_ge(nt_ready, t.next(nt_ready))
                copy(dst[:, k, :], nt[k % 2][:, 0:n]).then_inc(nh_ready, 1)
                if between:
                    between(k)

        def updated():
            base = t.take(upd_ready, KT)
            return lambda i: act.wait_ge(upd_ready, base + i + 1)

        def q_pair(q):
            w, slot = work()
            copy(q[LO, 0, :], ps[LO, slot, :], SCALE_64)
            copy(q[HI, 1, :], ps[HI, slot, :], SCALE_64).then_inc(high_ready, 1)

        act.wait_ge(init_in, 32)
        norm_stats(x_t, KT, S, D, lambda k: act.wait_ge(x_in[k], 16))
        norm_tiles(KT, S, hh)

        act.preload_act_table_set("natural_log_exp_and_others")
        def sb_take(piece, pair, slot, free):
            if piece == "q":
                q = pads[pair % 2][0]
                copy(q[LO, 0, :], ps[LO, slot, :], SCALE_64)
                copy(q[HI, 1, :], ps[HI, slot, :], SCALE_64).then_inc(high_ready, 1)
            elif piece == "k":
                copy(ks[pair % 2][0][:, :], ps[:, slot, :]).then_inc(high_ready, 1)
            elif piece == "v":
                copy(vts[pair % 2][:, :], ps[:, slot, :]).then_inc(free, 1)
            else:
                copy(vs[pair % 2][0][:, :, :], ps[:, slot, :].rearrange("p (k f) -> p k f", k=8)).then_inc(high_ready, 1)

        for piece in ("q", "k", "v", "vt"):
            w, slot = work()
            sb_take(piece, 0, slot, work_free[slot])
        for step in range(NU + 4):
            a, m, b = step, step - 1, step - 2
            if a < NU:
                n = SB_UNITS[a][4]
                act.wait_ge(z_done, a + 1)
                if a >= 3:
                    act.wait_ge(rest_done, a - 2)
                e = eb[a % 3][:, :, 0:n]
                zsrc = ps[:, Z_SLOT, :].rearrange("p (h q) -> p h q", h=2)
                act.activation(e, zsrc[:, :, 0:n], ACT.Abs).then_inc(abs_ready, 1)
            if 0 <= b < NU:
                zb_n = zb[b % 3][:, :, 0:SB_UNITS[b][4]]
                act.wait_ge(d_ready, b + 1)
                act.activation(zb_n, zb_n, ACT.Exp).then_inc(pw_ready, 1)
            if a < NU:
                act.wait_ge(abs_ready, a + 1)
                act.activation(e, e, ACT.Exp, scale=-1.0).then_inc(ea_ready, 1)
            if 0 <= m < NU:
                nm_ = SB_UNITS[m][4]
                act.wait_ge(sp_ready, m + 1)
                if m >= 2:
                    act.wait_ge(rest_done, m - 1)
                copy(sp_h[m % 2][:, :, 0:nm_], eb[m % 3][:, :, 0:nm_]).then_inc(sph_ready, 1)
            if 0 <= b < NU:
                act.wait_ge(pw_ready, b + 1)
                if b >= 1:
                    act.wait_ge(av_done, b)
                copy(pw_h[:, :, 0:SB_UNITS[b][4]], zb_n).then_inc(pwh_ready, 1)
            if a < NU:
                act.wait_ge(ea_ready, a + 1)
                act.activation(e, e, ACT.Ln, bias=ccol(C_ONE), scale=1.0).then_inc(ln_ready, 1)
            done = step - 3
            if 0 <= done < NU and SB_UNITS[done][2] == 0:
                pair, chunk = SB_UNITS[done][0:2]
                act.wait_ge(av_done, done + 1)
                if chunk == 0 and pair > 0:
                    act.wait_ge(op_left, 16 * pair)
                cols = slice(chunk * HALF, (chunk + 1) * HALF)
                copy(op_h[LO, cols], ob[0:64, 0, :])
                copy(op_h[HI, cols], ob[0:64, 1, :]).then_inc(oh_ready, 1)
            sent = step - 4
            if 0 <= sent < NU and SB_UNITS[sent][1:3] == (1, 0):
                pair = SB_UNITS[sent][0]
                act.wait_ge(o_ready, 2 * pair + 2)
                act.dma_start(spill_o[pair], op[:, :, :].bitcast(F32)).then_inc(op_left, 16)
            piece, _, tiles, pair, number = sb_piece(step)
            if piece and tiles == KT:
                act.wait_ge(piece_done, number + 1)
                sb_take(piece, pair, PIECE_SLOT, piece_free)
        act.wait_ge(op_left, 16 * SB_PAIRS)
        for part in range(2):
            act.dma_start(o_all[:, part, :, :].bitcast(F32), spill_o[:, :, part, :].rearrange("k p s -> p k s")).then_inc(o_in, 16)

        for j in range(CONV_TILES):
            take_out(cc[:, :])
            skip()
            w = t.take("work")
            evacuated(w)
            copy(c_h[:, j, :], cv[:, :]).then_inc(high_ready, 1)

        base = t.take(tile_ready, KT)
        for m in range(KT):
            if base + m > 0:
                act.wait_ge(tile_ready, base + m)
            take_out(ga[:, :], ACT.Sigmoid, bias=vcol(V_BGA + m))
            take_out(gc[:, :], ACT.Sigmoid, bias=vcol(V_BGC + m))
            skip(2)
        act.wait_ge(work_done, t.now("work"))
        act.wait_ge(tile_ready, base + KT)
        act.dma_start(x_t[:, :, :], xt.rearrange("(k p) s -> p k s", p=P)).then_inc(xold_in, 16)
        for k in range(KT):
            copy(hh[:, k, :], mix_t[:, k, :]).then_inc(high_ready, 1)

        for m in range(KT):
            take_out_with_square(y_t[:, m, :])
        roots(S, D)
        updated_tile = updated()
        for k in range(KT):
            updated_tile(k)
            square(x_t[:, k, :])
            act.activation(hh[:, k, :], x_t[:, k, :], ACT.Identity, scale=vcol(V_MLP + k)).then_inc(nh_ready, 1)
        roots(S, D)

        nch = FF // FF_CHUNK
        for c in range(nch + 1):
            if c < nch:
                for j in range(2):
                    w = t.take("work")
                    evacuated(w)
                    chain(act.activation(ff[:, :], fr[:, :], ACT.Square))
                    copy(f_h[c % 2][:, j, :], ff[:, :]).then_inc(high_ready, 1)
            if c == 1:
                for m in range(KT):
                    take_out(y_t[:, m, :])
            elif 1 < c < nch:
                skip(KT)
            elif c == nch:
                for m in range(KT):
                    w = t.take("work")
                    evacuated(w)
                    square(y_t[:, m, :])
        act.dma_start(p_t[:, :, :], pt.rearrange("(k p) s -> p k s", p=P)).then_inc(p_in, 16)
        roots(S, D)
        act.wait_ge(p_in, 16)
        for k in range(2):
            copy(p_h[:, k, :], p_t[:, k, :]).then_inc(high_ready, 1)
        norm_stats(x_t, KT, S, D, updated())
        norm_tiles(KT, S, hh, lambda k: take_out(y_t[:, k, :]))

        act.dma_start(m_t[:, :, :], memt.rearrange("(k p) s -> p k s", p=P)).then_inc(m_in, 16)
        act.wait_ge(m_in, 16)
        base = t.take(tile_ready, KT)
        for m in range(KT):
            if m > 0:
                square(m_t[:, m - 1, :], N_MEM)
                act.wait_ge(tile_ready, base + m)
                square(x_t[:, m - 1, :])
            take_out(pg[:, :], ACT.Sigmoid)
        act.wait_ge(tile_ready, base + KT)
        square(m_t[:, KT - 1, :], N_MEM)
        square(x_t[:, KT - 1, :])
        spilled = [0]

        def spill():
            act.dma_start(spill_x, x_t[:, :, :]).then_inc(spill_done, 16)
            spilled[0] += 16

        spill()
        roots(N_MEM, D)
        roots(S, D, 1)
        barrier(act, t, act_end)
        norm_tiles(KT, N_MEM, m_h)

        def memory_out(i):
            layer, j = i // 4, i % 2
            if i % 4 < 2:
                w, slot = work()
                copy(km_h[layer][:, j, :], ps[:, slot, 0:N_MEM]).then_inc(high_ready, 1)
            else:
                take_out(mv[:, :], n=N_MEM)
                w, slot = work()
                copy(vm_h[layer][:, :, j * P:(j + 1) * P], ps[:, slot, 0:N_MEM].rearrange("p (k f) -> p k f", k=2)).then_inc(high_ready, 1)

        norm_tiles(KT, S, hh, memory_out)

        def attend(heads, pieces, project, keys_of, tile_of):
            def turned():
                g = t.take("pt")
                act.wait_ge(pt_done, g + 1)
                copy(pt_h[g % 2][:, :], aux[:, g % 2, :]).then_inc(pth_ready, 1)

            for now, before, piece, following in attention_steps(heads, pieces):
                groups = keys_of(before % 4) // 256 if before is not None else 0
                for i in range(2):
                    if i < groups:
                        turned()
                    if now is not None:
                        keys = keys_of(now % 4)
                        w = t.take("work")
                        j = (2 * now + i) % 4
                        act.wait_ge(nm_ready, t.next(nm_ready))
                        act.activation(prob[now % 2][i][:, 0:keys], ps[:, w % 2, 0:keys], ACT.Exp, bias=nm[:, j:j + 1],
                                       scale=1.0, accum_out=rsum[:, j:j + 1]).then_inc(work_free[w % 2], 1)
                if piece:
                    project(piece, following)
                for _ in range(2, groups):
                    turned()
                if before is not None:
                    h, c = divmod(before, 4)
                    rows = (LO, HI)[h % 2]
                    o = t.take("oa")
                    act.wait_ge(oa_done, o + 1)
                    if c == 0 and h % 2 == 0:
                        if t.now(ot_out) > 0:
                            act.wait_ge(ot_out, t.now(ot_out))
                    copy(ot[rows, c * 256:(c + 1) * 256], ob[0:64, o % 2, 0:256]).then_inc(oa_taken, 1)
                    if c == 3 and h % 2 == 1:
                        act.wait_ge(oa_taken, t.now("oa"))
                        act.dma_start(spill_out[tile_of(h // 2)], ot[:, :]).then_inc(ot_out, 16)
                        t.take(ot_out, 16)

        def memory_attention(layer):
            def piece_out(piece, group):
                if piece.startswith("cq"):
                    take_out(cq_t[:, int(piece[2:]), :])
                elif piece.startswith("ckv"):
                    take_out(ckv_t[:, int(piece[3:]), :])
                else:
                    gate_to_dram(int(piece[4:]))

            q_pair(pads[0][0])
            q_pair(pads[1][0])
            attend(4, MEMORY[layer], piece_out, lambda c: N_MEM, lambda pair: MAIN_TILES + pair)

        def gate_to_dram(m, tiles=gt):
            i = t.take("gates")
            if i >= 2:
                act.wait_ge(gate_out[i % 2], 16 * (i // 2))
            w = take_out(tiles[i % 2][:, :])
            evacuated(w)
            act.dma_start(spill_gate[m], tiles[i % 2][:, :]).then_inc(gate_out[i % 2], 16)

        def gates_from_dram():
            for i in range(2):
                act.wait_ge(gate_out[i], 8 * t.now("gates"))
            act.dma_start(gate_t[:, :, :], spill_gate.rearrange("k p s -> p k s")).then_inc(gate_in, 16)

        def gates_and_output(gates_here):
            barrier(act, t, act_end)
            act.wait_ge(ot_out, t.now(ot_out))
            base, n_out = t.take(tile_ready, KT), t.take(out_in, KT) // 4

            def fetch(m):
                act.dma_start(go[m % 4][:, :], spill_out[m]).then_inc(out_in[m % 4], 16)

            for m in range(4):
                fetch(m)
            def residual():
                act.wait_ge(spill_done, spilled[0])
                act.dma_start(xold_t[:, :, :], spill_x).then_inc(xold_in, 16)

            if gates_here:
                for m in range(KT):
                    if m > 0:
                        act.wait_ge(tile_ready, base + m)
                    last = take_out(gt_late[m % 2][:, :], ACT.Silu)
                    if m > 0:
                        copy(y_h[:, m - 1, :], gt_late[(m - 1) % 2][:, :]).then_inc(high_ready, 1)
                        if m + 3 < KT:
                            fetch(m + 3)
                act.wait_ge(tile_ready, base + KT)
                copy(y_h[:, KT - 1, :], gt_late[(KT - 1) % 2][:, :]).then_inc(high_ready, 1)
                act.wait_ge(work_done, last + 1)
                residual()
            else:
                residual()
                act.wait_ge(gate_in, 16)
                for m in range(KT + 1):
                    if m < KT:
                        act.activation(gate_t[:, m, :], gate_t[:, m, :], ACT.Silu).then_inc(silu_ready, 1)
                    if m > 0:
                        act.wait_ge(tile_ready, base + m)
                        if m + 3 < KT:
                            fetch(m + 3)
                        copy(y_h[:, m - 1, :], gate_t[:, m - 1, :]).then_inc(high_ready, 1)
            for m in range(KT):
                take_out_with_square(z_t[:, m, :])
            roots(S, D)

        act.wait_ge(spill_done, spilled[0])
        barrier(act, t, act_end)
        memory_attention(0)
        barrier(act, t, act_end)
        act.dma_start(posi[HI, :], pos.partition_broadcast(64)).then_inc(pos_in, 16)
        for k in range(3):
            if k == 2:
                gate_to_dram(5, gt_late)
            square(cq_t[:, k, :])
        roots(S, 384, 0)
        for k in range(2):
            square(ckv_t[:, k, :])
        roots(S, 256, 1)
        act.wait_ge(table_ready, 1)
        act.activation(trig[HI, :], ang[1][HI, :], ACT.Sin).then_inc(sin_ready, 1)
        skip()
        act.wait_ge(gate_out[0], 16 * 3)
        norm_tiles(3, S, cq_h)
        gate_to_dram(6, gt_late)
        norm_tiles(2, S, ckv_h)
        gate_to_dram(7, gt_late)
        barrier(act, t, act_end)
        for high in (ka_h, ka2_h):
            copy(high[64:96, :], qf[64:96, :])
            last = copy(high[96:P, :], qf[64:96, :])
        last.then_inc(high_ready, 1)
        gates_from_dram()

        def latent_piece(piece, h):
            if piece == "q":
                w, slot = work()
                copy(qf[LO, :], ps[LO, slot, :], SCALE_MLA).then_inc(qn_ready, 1)
                act.wait_ge(rope_ready, t.next(rope_ready))
                copy(qa[h % 2][0][:, :], qf[:, :]).then_inc(high_ready, 1)
            elif piece == "kv":
                w, slot = work()
                chain(copy(kvf[:, :], ps[:, slot, :]))
                copy(ka[h % 2][0][LO, :], kvf[LO, :]).then_inc(high_ready, 1)
            else:
                w, slot = work()
                copy(va[h % 2][0][:, :, :], ps[:, slot, :].rearrange("p (k f) -> p k f", k=8)[:, :, 64:P]).then_inc(high_ready, 1)

        for piece in ("q", "kv", "vt"):
            latent_piece(piece, 0)
        attend(MLA_HEADS, LATENT, latent_piece, lambda c: (c + 1) * 256, lambda pair: pair)
        gates_and_output(False)
        ready = updated()
        norm_stats(x_t, KT, S, D, ready)
        spill()
        norm_tiles(KT, S, hh)

        barrier(act, t, act_end)
        act.wait_ge(spill_done, spilled[0])
        memory_attention(1)
        w, slot = work()
        act.preload_act_table_set("natural_log_exp_and_others")
        act.activation(fx[:, :], ps[:, slot, :], ACT.Identity, bias=vcol(V_BF)).then_inc(work_free[slot], 1)
        evacuated(w)
        chain(act.activation(fe[:, :], fx[:, :], ACT.Abs))
        chain(act.activation(fe[:, :], fe[:, :], ACT.Exp, scale=-1.0))
        act.activation(fe[:, :], fe[:, :], ACT.Ln, bias=ccol(C_ONE), scale=1.0).then_inc(ln_ready, 1)

        def fox_piece(piece, pair):
            if piece == "q":
                q_pair(pads[pair % 2][0])
            elif piece == "k":
                w, slot = work()
                copy(kf[pair % 2][0][:, :], ps[:, slot, :]).then_inc(high_ready, 1)
            elif piece == "v":
                take_out(fvt[:, :])
            else:
                w, slot = work()
                copy(vf[pair % 2][0][:, :, :], ps[:, slot, :].rearrange("p (k f) -> p k f", k=8)).then_inc(high_ready, 1)

        act.wait_ge(fox_ready, 1)
        for piece in ("q", "k", "v", "vt"):
            fox_piece(piece, 0)
        attend(2 * FOX_PAIRS, FOX, fox_piece, lambda c: (c + 1) * 256, lambda pair: pair)
        gates_and_output(True)

    @block.vector
    def _(dve):
        t = Tally()

        def work():
            w = t.take("work")
            dve.wait_ge(work_done, w + 1)
            return w, w % 2

        def skip(n=1):
            t.take("work", n)

        def evacuated(w):
            dve.wait_ge(work_free[w % 2], w // 2 + 1)

        def link(ins):
            ins.then_inc(dve_chain, 1)
            return t.next(dve_chain)

        def chain(ins):
            dve.wait_ge(dve_chain, link(ins))

        def low(dst, src, hi):
            return dve.tensor_tensor(dst, src, hi.bitcast(F32), ALU.subtract)

        def low_out(dst, hi, slot_src, slot):
            dve.wait_ge(high_ready, t.next(high_ready))
            low(dst, slot_src, hi).then_inc(work_free[slot], 1)

        def norm_row(n, bank=0):
            dve.wait_ge(rt_ready, t.next(rt_ready))
            chain(dve.reciprocal(rs[:, 0:n // P], rt[bank][:, 0:n // P]))
            for j in range(n // P):
                i = dve.tensor_scalar(diag[:, j * P:(j + 1) * P], ident, rs[:, j:j + 1], None, ALU.mult)
            i.then_inc(diag_ready, 1)
            dve.wait_ge(row_done, t.next(row_done))

        def norm_tiles(src, ktiles, n, gain, hi, lo, between=None):
            base = t.take(norm_ready, ktiles)
            for k in range(ktiles + 1):
                if k < ktiles:
                    if k >= 2:
                        dve.wait_ge(norm_ready, base + k - 1)
                    dve.scalar_tensor_tensor(out=nt[k % 2][:, 0:n], in0=src[:, k, :], scalar=vcol(gain + k),
                                                 in1=row[:, 0:n], op0=ALU.mult, op1=ALU.mult).then_inc(nt_ready, 1)
                if k > 0:
                    dve.wait_ge(nh_ready, t.next(nh_ready))
                    low(lo[:, k - 1, :], nt[(k - 1) % 2][:, 0:n], hi[:, k - 1, :]).then_inc(norm_ready, 1)
                    if between:
                        between(k - 1)

        def norm(src, ktiles, n, gain, hi, lo, bank=0):
            norm_row(n, bank)
            norm_tiles(src, ktiles, n, gain, hi, lo)

        def update(ysrc, xsrc, dst, gain, ready=upd_ready, low_part=None):
            norm_row(S)
            before = None
            for k in range(KT + 1):
                if k < KT:
                    now = link(dve.scalar_tensor_tensor(out=ysrc[:, k, :], in0=ysrc[:, k, :], scalar=vcol(gain + k),
                                                        in1=row[:, :], op0=ALU.mult, op1=ALU.mult))
                if k > 0:
                    dve.wait_ge(dve_chain, before)
                    dve.tensor_tensor(dst[:, k - 1, :], xsrc[:, k - 1, :], ysrc[:, k - 1, :], ALU.add).then_inc(ready, 1)
                    if low_part and k > 1:
                        low_part(k - 2)
                before = now

        def zero_pads(pads):
            for q in pads:
                dve.memset(q[HI, 0, :].bitcast(F32), 0.0)
                i = dve.memset(q[LO, 1, :].bitcast(F32), 0.0)
            return i

        def q_pair(q_high, q_low):
            w, slot = work()
            dve.wait_ge(high_ready, t.next(high_ready))
            for h, rows in ((0, LO), (1, HI)):
                i = dve.scalar_tensor_tensor(out=q_low[rows, h, :], in0=ps[rows, slot, :], scalar=SCALE_64,
                                             in1=q_high[rows, h, :].bitcast(F32), op0=ALU.mult, op1=ALU.subtract)
            i.then_inc(work_free[slot], 1)

        dve.wait_ge(init_in, 32)
        for dst, c in ((tri_r, C_TRI), (rest_r, C_REST), (id_r, C_ID)):
            dve.tensor_copy(dst[:, :], con[:, c:c + P])
        dve.tensor_copy(neg_flat, con[:, C_NEG:C_NEG + 512])
        dve.memset(zero_r[:, :].bitcast(F32), 0.0)
        zero_pads(pads[0] + pads[1]).then_inc(const_ready, 1)
        norm(x_t, KT, S, V_PRE, hh, hl)

        def sb_take(piece, pair, slot, free):
            if piece == "v":
                return
            dve.wait_ge(high_ready, t.next(high_ready))
            if piece == "q":
                q_high, q_low = pads[pair % 2]
                for h, rows in ((0, LO), (1, HI)):
                    i = dve.scalar_tensor_tensor(out=q_low[rows, h, :], in0=ps[rows, slot, :], scalar=SCALE_64,
                                                 in1=q_high[rows, h, :].bitcast(F32), op0=ALU.mult, op1=ALU.subtract)
                i.then_inc(free, 1)
            elif piece == "k":
                low(ks[pair % 2][1][:, :], ps[:, slot, :], ks[pair % 2][0][:, :]).then_inc(free, 1)
            else:
                low(vs[pair % 2][1][:, :, :], ps[:, slot, :].rearrange("p (k f) -> p k f", k=8),
                    vs[pair % 2][0][:, :, :]).then_inc(free, 1)

        for piece in ("q", "k", "v", "vt"):
            w, slot = work()
            sb_take(piece, 0, slot, work_free[slot])
        for step in range(NU + 4):
            a, m, b = step, step - 1, step - 2
            if 0 <= b < NU:
                pair, chunk, kb, first, n = SB_UNITS[b]
                z = zb[b % 3]
                dve.wait_ge(tri_done, b + 1)
                d = dve.tensor_tensor(z[:, :, 0:n], z[:, :, 0:n], aux[:, :, first:first + n], ALU.subtract)
                if kb >= 4 * chunk:
                    chain(d)
                    c0, c1 = (0, 256) if kb == 4 * chunk + 3 else (0, P)
                    cap = con[:, C_CAP + 256 - c1:C_CAP + 256].unsqueeze(1).broadcast_to([P, 2, c1])
                    d = dve.tensor_tensor(z[:, :, c0:c1], z[:, :, c0:c1], cap, ALU.min)
                d.then_inc(d_ready, 1)
            if 0 <= m < NU:
                pair, chunk, kb, first, n = SB_UNITS[m]
                z, e = zb[m % 3], eb[m % 3]
                dve.wait_ge(z_free, m + 1)
                dve.wait_ge(ln_ready, m + 1)
                i = dve.scalar_tensor_tensor(out=e[:, :, 0:n], in0=z[:, :, 0:n], scalar=0.0, in1=e[:, :, 0:n],
                                             op0=ALU.max, op1=ALU.add)
                if kb >= 4 * chunk:
                    chain(i)
                    c1 = 256 if kb == 4 * chunk + 3 else P
                    mask = con[:, C_MASK01 + 256 - c1:C_MASK01 + 256].unsqueeze(1).broadcast_to([P, 2, c1])
                    i = dve.tensor_tensor(e[:, :, 0:c1], e[:, :, 0:c1], mask, ALU.mult)
                i.then_inc(sp_ready, 1)
            if a < NU:
                n = SB_UNITS[a][4]
                dve.wait_ge(abs_ready, a + 1)
                if a >= 3:
                    dve.wait_ge(av_done, a - 2)
                zsrc = ps[:, Z_SLOT, :].rearrange("p (h q) -> p h q", h=2)
                dve.tensor_copy(zb[a % 3][:, :, 0:n], zsrc[:, :, 0:n]).then_inc(z_free, 1)
            if 0 <= m < NU:
                n = SB_UNITS[m][4]
                dve.wait_ge(sph_ready, m + 1)
                low(sp_l[m % 3][:, :, 0:n], eb[m % 3][:, :, 0:n], sp_h[m % 2][:, :, 0:n]).then_inc(spl_ready, 1)
            if 0 <= b < NU:
                n = SB_UNITS[b][4]
                dve.wait_ge(pwh_ready, b + 1)
                low(pw_l[b % 3][:, :, 0:n], zb[b % 3][:, :, 0:n], pw_h[:, :, 0:n]).then_inc(pwl_ready, 1)
            done = step - 3
            if 0 <= done < NU and SB_UNITS[done][2] == 0:
                chunk = SB_UNITS[done][1]
                dve.wait_ge(oh_ready, t.next(oh_ready))
                cols = slice(chunk * HALF, (chunk + 1) * HALF)
                low(op_l[LO, cols], ob[0:64, 0, :], op_h[LO, cols])
                low(op_l[HI, cols], ob[0:64, 1, :], op_h[HI, cols]).then_inc(o_ready, 1)
            piece, _, tiles, pair, number = sb_piece(step)
            if piece and tiles == KT:
                dve.wait_ge(piece_done, number + 1)
                sb_take(piece, pair, PIECE_SLOT, piece_free)

        chain(dve.memset(cu[:, 0:2], 0.0))
        for j in range(CONV_TILES):
            w = t.take("work")
            w2, slot = work()
            evacuated(w)
            dve.tensor_tensor(cu[:, 2:2 + S], ps[:, slot, :], cc[:, :], ALU.mult).then_inc(work_free[slot], 1)
            evacuated(w2)
            if j > 0:
                dve.wait_ge(tile_split, j)
            chain(dve.tensor_scalar(cv[:, :], cu[:, 2:2 + S], vcol(V_CONV + 8 + j), None, ALU.mult))
            for tap in (1, 0):
                chain(dve.scalar_tensor_tensor(out=cv[:, :], in0=cu[:, tap:tap + S], scalar=vcol(V_CONV + 4 * tap + j),
                                               in1=cv[:, :], op0=ALU.mult, op1=ALU.add))
            w, slot = work()
            dve.tensor_tensor(cv[:, :], cv[:, :], ps[:, slot, :], ALU.mult).then_inc(work_free[slot], 1)
            dve.wait_ge(high_ready, t.next(high_ready))
            low(c_l[:, j, :], cv[:, :], c_h[:, j, :]).then_inc(tile_split, 1)

        for m in range(KT):
            wa, wc = t.take("work"), t.take("work")
            w, slot = work()
            evacuated(wa)
            dve.tensor_tensor(ga[:, :], ps[:, slot, :], ga[:, :], ALU.mult).then_inc(work_free[slot], 1)
            w2, slot = work()
            evacuated(wc)
            dve.tensor_tensor(gc[:, :], ps[:, slot, :], gc[:, :], ALU.mult).then_inc(work_free[slot], 1)
            evacuated(w)
            evacuated(w2)
            dve.tensor_tensor(mix_t[:, m, :], ga[:, :], gc[:, :], ALU.add).then_inc(tile_ready, 1)
        for k in range(KT):
            dve.wait_ge(high_ready, t.next(high_ready))
            low(hl[:, k, :], mix_t[:, k, :], hh[:, k, :]).then_inc(tile_split, 1)
        skip(KT)
        dve.wait_ge(xold_in, 16)

        def low_part(k):
            dve.wait_ge(nh_ready, t.next(nh_ready))
            dve.scalar_tensor_tensor(out=hl[:, k, :], in0=x_t[:, k, :], scalar=vcol(V_MLP + k),
                                     in1=hh[:, k, :].bitcast(F32), op0=ALU.mult, op1=ALU.subtract).then_inc(norm_ready, 1)

        t.take(norm_ready, KT)
        update(y_t, x_t, x_t, V_POST, low_part=low_part)
        low_part(KT - 1)
        norm_row(S)
        chain(dve.tensor_copy(row_sb[:, :], row[:, :]))

        nch = FF // FF_CHUNK
        t.take(tile_split, CONV_TILES + KT)
        for c in range(nch + 1):
            if c < nch:
                for j in range(2):
                    w, slot = work()
                    dve.scalar_tensor_tensor(out=fr[:, :], in0=ps[:, slot, :], scalar=0.0, in1=row_sb[:, :],
                                             op0=ALU.max, op1=ALU.mult).then_inc(work_free[slot], 1)
                    dve.wait_ge(high_ready, t.next(high_ready))
                    low(f_l[c % 2][:, j, :], ff[:, :], f_h[c % 2][:, j, :]).then_inc(tile_split, 1)
                    t.take(tile_split)
            if c == 1:
                skip(KT)
            elif c > 1:
                for m in range(KT):
                    w, slot = work()
                    dve.tensor_tensor(y_t[:, m, :], y_t[:, m, :], ps[:, slot, :], ALU.add).then_inc(work_free[slot], 1)
        update(y_t, x_t, x_t, V_POSTMLP)
        for k in range(2):
            dve.wait_ge(high_ready, t.next(high_ready))
            low(p_l[:, k, :], p_t[:, k, :], p_h[:, k, :]).then_inc(tile_split, 1)
        norm(x_t, KT, S, V_PLE, hh, hl)

        skip(KT)
        for m in range(KT):
            w = t.take("work")
            evacuated(w)
            chain(dve.tensor_tensor(pg[:, :], pg[:, :], y_t[:, m, :], ALU.mult))
            dve.tensor_tensor(x_t[:, m, :], x_t[:, m, :], pg[:, :], ALU.add).then_inc(tile_ready, 1)
        barrier(dve, t, dve_end)
        norm(m_t, KT, N_MEM, V_MEM, m_h, m_l)

        def memory_out(i):
            layer, j = i // 4, i % 2
            if i % 4 < 2:
                w, slot = work()
                low_out(km_l[layer][:, j, :], km_h[layer][:, j, :], ps[:, slot, 0:N_MEM], slot)
            else:
                skip()
                w, slot = work()
                low_out(vm_l[layer][:, :, j * P:(j + 1) * P], vm_h[layer][:, :, j * P:(j + 1) * P],
                        ps[:, slot, 0:N_MEM].rearrange("p (k f) -> p k f", k=2), slot)

        norm_row(S, 1)
        norm_tiles(x_t, KT, S, V_PRE2, hh, hl, memory_out)

        def attend(heads, pieces, project, keys_of, forget=False):
            def maximum(n, qi):
                w, slot = work()
                i = (2 * n + qi) % 4
                dve.tensor_reduce(nm[:, i:i + 1], ps[:, slot, 0:keys_of(n % 4)], AX.X, ALU.max, negate=True).then_inc(nm_ready, 1)
                return w

            def normed(n, qi, w):
                i = (2 * n + qi) % 4
                evacuated(w)
                chain(dve.reciprocal(rinv[:, i:i + 1], rsum[:, i:i + 1]))
                p = prob[n % 2][qi][:, 0:keys_of(n % 4)]
                dve.tensor_scalar(p, p, rinv[:, i:i + 1], None, ALU.mult).then_inc(pn_ready, 1)

            def turned():
                g = t.take("pt")
                dve.wait_ge(pth_ready, t.next(pth_ready))
                low(pt_l[g % 2][:, :], aux[:, g % 2, :], pt_h[g % 2][:, :]).then_inc(ptl_ready, 1)

            def forget_terms(n):
                h, c = divmod(n, 4)
                dve.tensor_scalar(a_head[:, c * 256:(c + 1) * 256], a_base[:, c * 256:(c + 1) * 256], ccol(C_HEAD + h),
                                  None, ALU.mult).then_inc(ahead_ready, 1)

            if forget:
                forget_terms(0)
            for now, before, piece, following in attention_steps(heads, pieces):
                groups = keys_of(before % 4) // 256 if before is not None else 0
                ws = []
                for i in range(2):
                    if now is not None:
                        ws.append(maximum(now, i))
                    if i < groups:
                        turned()
                if forget and now is not None and now + 1 < 4 * heads:
                    forget_terms(now + 1)
                for i in range(2):
                    if now is not None:
                        normed(now, i, ws[i])
                    if i + 2 < groups and not piece:
                        turned()
                if piece:
                    project(piece, following)
                    for _ in range(2, groups):
                        turned()

        def memory_attention(layer):
            q_pair(*pads[0])
            q_pair(*pads[1])
            attend(4, MEMORY[layer], lambda piece, group: skip(), lambda c: N_MEM)

        def gates_and_output(gain, ready, gates_here):
            barrier(dve, t, dve_end)
            n_out = t.take("out_use", KT) // 4
            for m in range(KT):
                if gates_here:
                    w = t.take("work")
                    evacuated(w)
                    g = gt_late[m % 2][:, :]
                else:
                    g = gate_t[:, m, :]
                    dve.wait_ge(silu_ready, m + 1)
                dve.wait_ge(out_in[m % 4], 16 * (n_out + m // 4 + 1))
                dve.tensor_tensor(g, g, go[m % 4][:, :], ALU.mult).then_inc(tile_ready, 1)
                dve.wait_ge(high_ready, t.next(high_ready))
                low(y_l[:, m, :], g, y_h[:, m, :]).then_inc(tile_split, 1)
            skip(KT)
            dve.wait_ge(xold_in, 32 if gain == V_POST2 else 48)
            update(z_t, xold_t, x_t, gain, ready)

        def rope(slot, dst):
            chain(dve.tensor_tensor(dst[64:96, :], ps[64:96, slot, :], trig[64:96, :], ALU.mult))
            chain(dve.tensor_tensor(ps[64:96, slot, :], ps[96:P, slot, :], trig[96:P, :], ALU.mult))
            return dve.tensor_tensor(dst[64:96, :], ps[64:96, slot, :], dst[64:96, :], ALU.add)

        barrier(dve, t, dve_end)
        zero_pads(pads[0] + pads[1])
        memory_attention(0)
        barrier(dve, t, dve_end)
        dve.wait_ge(pos_in, 16)
        a0, a1, a2 = (a[HI, :] for a in ang)
        chain(dve.tensor_copy(a0, posi[HI, :]))
        chain(dve.tensor_scalar(a1, a0, ccol(C_INV, HI), None, ALU.mult))
        chain(dve.tensor_scalar(a2, a1, 1.0 / (2 * np.pi), None, ALU.mult))
        chain(dve.tensor_scalar(a2, a2, ccol(C_OFF, HI), None, ALU.add))
        chain(dve.tensor_scalar(a2, a2, 12582912.0, None, ALU.add))
        chain(dve.tensor_scalar(a2, a2, -12582912.0, None, ALU.add))
        turn = 2 * np.pi
        c1 = 6.28125
        c2 = float(np.float32(np.round((turn - c1) * 2 ** 21) / 2 ** 21))
        c3 = float(np.float32(turn - c1 - c2))
        for c in (c1, c2, c3):
            chain(dve.scalar_tensor_tensor(out=a1, in0=a2, scalar=-c, in1=a1, op0=ALU.mult, op1=ALU.add))
        chain(dve.tensor_scalar(a1, a1, ccol(C_SHIFT, HI), None, ALU.add))
        dve.tensor_scalar(a1, a1, 3.1415925, -3.1415925, ALU.min, ALU.max).then_inc(table_ready, 1)
        skip()
        w, slot = work()
        norm(cq_t, 3, S, V_QN, cq_h, cq_l)
        dve.wait_ge(sin_ready, t.next(sin_ready))
        chain(dve.tensor_scalar(trig[96:P, :], trig[96:P, :], ccol(C_SIGN, slice(96, P)), None, ALU.mult))
        rope(slot, qf).then_inc(work_free[slot], 1)
        skip()
        norm(ckv_t, 2, S, V_KVN, ckv_h, ckv_l, 1)
        skip()
        evacuated(w)
        dve.tensor_scalar(trig[HI, :], trig[HI, :], SCALE_MLA, None, ALU.mult)
        barrier(dve, t, dve_end)
        dve.wait_ge(high_ready, t.next(high_ready))
        for high, rest in ((ka_h, ka_l), (ka2_h, ka2_l)):
            low(rest[64:96, :], qf[64:96, :], high[64:96, :])
            last = low(rest[96:P, :], qf[64:96, :], high[64:96, :])
        chain(last)

        def latent_piece(piece, h):
            if piece == "q":
                w, slot = work()
                dve.wait_ge(qn_ready, t.next(qn_ready))
                dve.tensor_tensor(qf[HI, :], ps[HI, slot, :], trig[HI, :], ALU.mult).then_inc(rope_ready, 1)
                dve.wait_ge(high_ready, t.next(high_ready))
                low(qa[h % 2][1][:, :], qf[:, :], qa[h % 2][0][:, :]).then_inc(work_free[slot], 1)
            elif piece == "kv":
                w, slot = work()
                low_out(ka[h % 2][1][LO, :], ka[h % 2][0][LO, :], kvf[LO, :], slot)
            else:
                w, slot = work()
                low_out(va[h % 2][1][:, :, :], va[h % 2][0][:, :, :],
                        ps[:, slot, :].rearrange("p (k f) -> p k f", k=8)[:, :, 64:P], slot)

        for piece in ("q", "kv", "vt"):
            latent_piece(piece, 0)
        attend(MLA_HEADS, LATENT, latent_piece, lambda c: (c + 1) * 256)
        gates_and_output(V_POST2, upd_ready, False)
        norm(x_t, KT, S, V_PRE2 + 8, hh, hl)

        barrier(dve, t, dve_end)
        zero_pads(pads[0] + pads[1])
        memory_attention(1)
        w = t.take("work")
        for i in range(2):
            dve.wait_ge(gate_out[i], 16 * KT // 2)
        chain(dve.memset(fone[:, :], 1.0))
        dve.wait_ge(ln_ready, NU + 1)
        chain(dve.scalar_tensor_tensor(out=fe[:, :], in0=fx[:, :], scalar=0.0, in1=fe[:, :], op0=ALU.min, op1=ALU.subtract))
        chain(dve.tensor_tensor_scan(out=fx[:, :], data0=fone[:, :], data1=fe[:, :], initial=0.0, op0=ALU.mult, op1=ALU.add))
        chain(dve.tensor_copy(b_all[:, :], fx[:, :]))
        chain(dve.tensor_copy(a_base[0:32, :], b_all[0:32, :].bitcast(F32)))
        chain(dve.tensor_tensor(a_base[32:64, :], fx[32:64, :], b_all[32:64, :].bitcast(F32), ALU.subtract))
        chain(dve.memset(a_base[HI, :], -1.0))
        chain(dve.tensor_tensor(b_all[96:P, :], fx[96:P, :], b_all[96:P, :].bitcast(F32), ALU.subtract))
        dve.memset(b_all[LO, :].bitcast(F32), 1.0).then_inc(fox_ready, 1)

        def fox_piece(piece, pair):
            if piece == "q":
                q_pair(*pads[pair % 2])
            elif piece == "k":
                w, slot = work()
                low_out(kf[pair % 2][1][:, :], kf[pair % 2][0][:, :], ps[:, slot, :], slot)
            elif piece == "v":
                skip()
            else:
                w, slot = work()
                low_out(vf[pair % 2][1][:, :, :], vf[pair % 2][0][:, :, :],
                        ps[:, slot, :].rearrange("p (k f) -> p k f", k=8), slot)

        for piece in ("q", "k", "v", "vt"):
            fox_piece(piece, 0)
        attend(2 * FOX_PAIRS, FOX, fox_piece, lambda c: (c + 1) * 256, forget=True)
        gates_and_output(V_POST2 + 8, final_ready, True)


    ctx.close()



def tiles_of(w):
    k, m = w.shape[0] // P, w.shape[1] // P
    return w.reshape(k, P, m, P).transpose(2, 1, 0, 3)


def padded(w, cols):
    full = np.zeros((w.shape[0], P), np.float32)
    for at, a, b in cols:
        full[:, at:at + b - a] = w[:, a:b]
    return full


def weight_stream(w_in, w_attn_out, w_conv_out, w_o, w_up, w_down, w_ple_gate, w_ple_proj, w_mem_kv,
                  w_out, w_in_a, w_q_up_a, w_kv_up_a, w_in_b):
    slabs = []
    win = tiles_of(w_in)
    for pair in range(SB_PAIRS):
        slabs += [win[4 * i + pair] for i in range(3)]
    for j in range(CONV_TILES):
        slabs += [win[12 + 4 * i + j] for i in (1, 2, 0)]
    ao, co = tiles_of(w_attn_out), tiles_of(w_conv_out)
    for m in range(KT):
        slabs += [win[24 + m], win[32 + m], np.concatenate([ao[m], co[m]], 1)]
    slabs += list(tiles_of(w_o))
    up = tiles_of(w_up)
    for c in range(FF // FF_CHUNK + 1):
        if c < FF // FF_CHUNK:
            slabs += [up[2 * c], up[2 * c + 1]]
        if c > 0:
            down = tiles_of(w_down[(c - 1) * FF_CHUNK:c * FF_CHUNK])
            slabs += [np.concatenate(down[4 * q:4 * q + 4], 1) for q in range(2)]
    pp = tiles_of(w_ple_proj)
    slabs += [np.concatenate(pp[4 * q:4 * q + 4], 1) for q in range(2)]
    slabs += list(tiles_of(w_ple_gate))
    for layer in range(2):
        slabs += list(tiles_of(w_mem_kv[layer]))
    slabs += list(tiles_of(w_in_a[:, 672:928])) + list(tiles_of(w_in_a[:, 0:640]))
    slabs += list(tiles_of(w_in_a[:, 928:1696]))
    slabs += list(tiles_of(padded(w_in_a, [(64, 640, 672), (96, 656, 672), (112, 640, 656)])))
    slabs += list(tiles_of(w_in_a[:, 1696:1952]))
    for h in range(MLA_HEADS):
        q = tiles_of(padded(w_q_up_a, [(0, 96 * h, 96 * h + 96), (96, 96 * h + 80, 96 * h + 96), (112, 96 * h + 64, 96 * h + 80)]))[0]
        kv = tiles_of(w_kv_up_a[:, P * h:P * (h + 1)])[0]
        slabs.append(np.concatenate([q, kv, np.zeros((P, 3, P), np.float32)], 1))
    slabs += list(tiles_of(w_out[0]))
    slabs += list(tiles_of(w_in_b[:, 2316:2572]))
    slabs += list(tiles_of(padded(w_in_b, [(32 * q, 2304, 2316) for q in range(4)])))
    qkv = tiles_of(w_in_b[:, 0:2304])
    for pair in range(FOX_PAIRS):
        slabs += [qkv[6 * i + pair] for i in range(3)]
    slabs += list(tiles_of(w_in_b[:, 2572:3596])) + list(tiles_of(w_out[1]))
    assert len(slabs) == TOTAL_SLABS
    return np.ascontiguousarray(np.stack(slabs))


def vectors(gains, b_gate, w_conv, b_f):
    v = np.zeros((P, N_VEC), np.float32)
    for at, g in gains:
        v[:, at:at + g.size // P] = g.reshape(-1, P).T
    v[:, V_BGA:V_BGA + 16] = b_gate.reshape(16, P).T
    v[:, V_CONV:V_CONV + 12] = w_conv.reshape(12, P).T
    for q in range(4):
        v[32 * q:32 * q + MLA_HEADS, V_BF] = b_f
    return v


def constants():
    c = np.zeros((P, N_CONST), np.float32)
    i = np.arange(P)
    before = i[:, None] < i[None, :]
    c[:, C_ID:C_ID + P] = np.eye(P)
    c[:, C_ONE:C_ONE + P] = 1.0
    c[:, C_TRI:C_TRI + P] = ~before
    c[:, C_REST:C_REST + P] = before
    c[:, C_MASK01 + P:C_MASK01 + 256] = before
    c[:, C_CAP:C_CAP + P] = NEG
    c[:, C_CAP + P:C_CAP + 256] = np.where(before, -NEG, NEG)
    key = np.arange(256)
    for qi in range(2):
        c[:, C_NEG + 256 * qi:C_NEG + 256 * (qi + 1)] = np.where(key[None, :] <= i[:, None] + P * qi, 0.0, NEG)
    for h in range(12):
        c[h::32, C_HEAD + h] = 1.0
    half = 16
    inv = (np.float32(10000.0) ** (-np.arange(half, dtype=np.float32) / half)).astype(np.float32)
    c[64:, C_INV] = np.tile(inv, 4)
    c[64:96, C_OFF], c[64:96, C_SHIFT] = 0.25, np.pi / 2
    c[96:112, C_SIGN], c[112:, C_SIGN] = -1.0, 1.0
    c[:, C_EPS] = EPS
    return c


def kernel(**inputs):
    from concourse import bacc
    from concourse.bass_utils import run_bass_kernel_spmd

    a = {name: np.asarray(value) for name, value in inputs.items()}
    arrays = {
        "wall": weight_stream(a["w_in"][0], a["w_attn_out"][0], a["w_conv_out"][0], a["w_o"][0], a["w_up"][0],
                              a["w_down"][0], a["w_ple_gate"][0], a["w_ple_proj"][0], a["w_mem_kv_2"], a["w_out_2"],
                              a["w_in_a_2"][0], a["w_q_up_a_2"][0], a["w_kv_up_a_2"][0], a["w_in_b_2"][0]),
        "vecs": vectors([(V_PRE, a["g_pre_mix"]), (V_POST, a["g_post_mix"]), (V_MLP, a["g_pre_mlp"]),
                         (V_POSTMLP, a["g_post_mlp"]), (V_PLE, a["g_ple"]), (V_PRE2, a["norm_pre_2"]),
                         (V_POST2, a["norm_post_2"]), (V_MEM, a["mem_norm_2"]), (V_QN, a["q_norm_a_2"]),
                         (V_KVN, a["kv_norm_a_2"])], a["b_gate"], a["w_conv"], a["b_f_2"][0]),
        "consts": constants(),
        "xt": np.ascontiguousarray(a["x"][0].T),
        "pt": np.ascontiguousarray(a["p"][0, 0].T),
        "memt": np.ascontiguousarray(a["mem_2"][0].T),
        "pos": np.ascontiguousarray(a["positions_2"][0]),
    }
    nc = bacc.Bacc("TRN2", target_bir_lowering=False, num_devices=1)
    args = [nc.dram_tensor(n, v.shape, mybir.dt.from_np(v.dtype), kind="ExternalInput").ap() for n, v in arrays.items()]
    args.append(nc.dram_tensor("spill_x", [P, KT, S], F32).ap())
    args.append(nc.dram_tensor("spill_o", [SB_PAIRS, P, 2, S], F32).ap())
    args.append(nc.dram_tensor("spill_out", [KT, P, S], F32).ap())
    args.append(nc.dram_tensor("spill_gate", [KT, P, S], F32).ap())
    args.append(nc.dram_tensor("out_t", [D, S], F32, kind="ExternalOutput").ap())
    program(nc, *args)
    r = run_bass_kernel_spmd(nc, [arrays], core_ids=[0])
    return np.ascontiguousarray(r.results[0]["out_t"].T)[None]
```
